# Optimizing a Trainium2 kernel written in Bass

```python
import math
import jax, jax.numpy as jnp
from jax import lax
import numpy as np

D_MODEL = 1024
BATCH = 1
SEQ = 256
DEPTH = 2

MEM_LEN = 256
D_MIX = D_MODEL
HEAD_DIM = 64
SSM_WIDTH = D_MIX // 4
SSM_GROUP = 16
SSM_GROUPS = SSM_WIDTH // SSM_GROUP
SSM_STATE = 64
CONV_WIDTH = D_MIX // 4
CONV_K = 31
NSA_WIDTH = D_MIX // 2
NSA_HEADS = NSA_WIDTH // HEAD_DIM
NSA_KV_HEADS = 2
NSA_GROUP = NSA_HEADS // NSA_KV_HEADS
N_BRANCH = 3
L_CMP = 32
CMP_STRIDE = 16
L_SEL = 64
N_SELECT = 16
N_LOCAL = 2
WINDOW = 512
NSA_Q_BLOCK = 64
SEL_FORCE = 1e6
T5_BUCKETS = 32
T5_MAX_DIST = 128
X_HEADS = 4
X_WIDTH = X_HEADS * HEAD_DIM
D_FF = 2816
N_EXPERTS = 8
TOP_K = 2
MOE_BLOCK = 256
N_DENSE = (DEPTH + 1) // 2
N_MOE = DEPTH // 2
PROJ_WIDTH = SSM_WIDTH + 2 * CONV_WIDTH + NSA_WIDTH + 6 * NSA_KV_HEADS * HEAD_DIM + N_BRANCH * NSA_HEADS
EPS = 1e-6

kernel_name = "hybrid_s5_conformer_nsa_moe_trunk"

def _rms(x):
    xf = x.astype(jnp.float32)
    return (xf * lax.rsqrt(jnp.mean(xf * xf, axis=-1, keepdims=True) + EPS)).astype(x.dtype)

def rms_norm(x, g):
    return _rms(x) * g

def layer_norm(x, g, b):
    xf = x.astype(jnp.float32)
    mu = jnp.mean(xf, axis=-1, keepdims=True)
    var = jnp.mean(jnp.square(xf - mu), axis=-1, keepdims=True)
    return ((xf - mu) * lax.rsqrt(var + EPS)).astype(x.dtype) * g + b

def masked_softmax(s, mask):
    s = jnp.where(mask, s.astype(jnp.float32), -jnp.inf)
    m = jnp.max(s, axis=-1, keepdims=True)
    m = jnp.where(jnp.isfinite(m), m, 0.0)
    p = jnp.exp(s - m)
    return p / jnp.maximum(jnp.sum(p, axis=-1, keepdims=True), 1e-30)

def t5_bucket(dist):
    n = jnp.maximum(dist, 0)
    max_exact = T5_BUCKETS // 2
    nf = jnp.maximum(n, 1).astype(jnp.float32)
    large = max_exact + (jnp.log(nf / max_exact) / math.log(T5_MAX_DIST / max_exact)
                         * (T5_BUCKETS - max_exact)).astype(jnp.int32)
    large = jnp.minimum(large, T5_BUCKETS - 1)
    return jnp.where(n < max_exact, n, large)

def _complex_linear_combine(e1, e2):
    a1r, a1i, b1r, b1i = e1
    a2r, a2i, b2r, b2i = e2
    return (a1r * a2r - a1i * a2i,
            a1r * a2i + a1i * a2r,
            a2r * b1r - a2i * b1i + b2r,
            a2r * b1i + a2i * b1r + b2i)

def s5_mixer(u, lam_re, lam_im, log_dt, b_re, b_im, c_re, c_im, d_skip, w_glu):
    bsz, seq, _ = u.shape
    dt = jnp.exp(log_dt.astype(jnp.float32))[:, None]
    lr, li = lam_re.astype(jnp.float32), lam_im.astype(jnp.float32)
    mag = jnp.exp(lr * dt)
    ar, ai = mag * jnp.cos(li * dt), mag * jnp.sin(li * dt)
    den = lr * lr + li * li
    fr = ((ar - 1.0) * lr + ai * li) / den
    fi = (ai * lr - (ar - 1.0) * li) / den
    bbr = fr[..., None] * b_re - fi[..., None] * b_im
    bbi = fr[..., None] * b_im + fi[..., None] * b_re
    ug = u.reshape(bsz, seq, SSM_GROUPS, SSM_GROUP).astype(jnp.float32)
    bur = jnp.einsum('bsgh,gph->bsgp', ug, bbr)
    bui = jnp.einsum('bsgh,gph->bsgp', ug, bbi)
    a_r = jnp.broadcast_to(ar, (1, seq, SSM_GROUPS, SSM_STATE))
    a_i = jnp.broadcast_to(ai, (1, seq, SSM_GROUPS, SSM_STATE))
    _, _, xr, xi = lax.associative_scan(_complex_linear_combine, (a_r, a_i, bur, bui), axis=1)
    y = (jnp.einsum('bsgp,ghp->bsgh', xr, c_re) - jnp.einsum('bsgp,ghp->bsgh', xi, c_im)
         + d_skip * ug)
    y = y.reshape(bsz, seq, SSM_WIDTH).astype(u.dtype)
    a, g = jnp.split(jax.nn.gelu(y) @ w_glu, 2, axis=-1)
    return a * jax.nn.sigmoid(g)

def conv_mixer(z, w_dw, b_dw, ln_g, ln_b, w_pw):
    a, g = jnp.split(z, 2, axis=-1)
    v = a * jax.nn.sigmoid(g)
    y = lax.conv_general_dilated(v, w_dw[:, None, :], window_strides=(1,),
                                 padding=[(CONV_K - 1, 0)],
                                 dimension_numbers=('NWC', 'WIO', 'NWC'),
                                 feature_group_count=CONV_WIDTH) + b_dw
    y = jax.nn.silu(layer_norm(y, ln_g, ln_b))
    return y @ w_pw

def nsa_compress(kv, pe, w1, w2):
    seq = kv.shape[2]
    n_cmp = (seq - L_CMP) // CMP_STRIDE + 1
    idx = jnp.arange(n_cmp)[:, None] * CMP_STRIDE + jnp.arange(L_CMP)[None, :]
    blocks = kv[:, :, idx] + pe
    flat = blocks.reshape(blocks.shape[0], blocks.shape[1], n_cmp, L_CMP * HEAD_DIM)
    return jax.nn.gelu(flat @ w1) @ w2

def cmp_to_sel_overlap(n_cmp, n_sel):
    cs = jnp.arange(n_cmp) * CMP_STRIDE
    ss = jnp.arange(n_sel) * L_SEL
    ov = jnp.minimum(cs[:, None] + L_CMP, ss[None, :] + L_SEL) - jnp.maximum(cs[:, None], ss[None, :])
    return jnp.maximum(ov, 0).astype(jnp.float32) / L_CMP

def nsa_mixer(q, k_c, v_c, k_s, v_s, k_w, v_w, gate_logits, q_gain, k_gain, cmp_pe, cmp_w1, cmp_w2, t5_table):
    bsz, seq, _ = q.shape
    qb = NSA_Q_BLOCK
    q = rms_norm(q.reshape(bsz, seq, NSA_HEADS, HEAD_DIM), q_gain)
    q = q.reshape(bsz, seq, NSA_KV_HEADS, NSA_GROUP, HEAD_DIM).transpose(0, 2, 3, 1, 4)

    def kv_heads(t):
        return t.reshape(bsz, seq, NSA_KV_HEADS, HEAD_DIM).transpose(0, 2, 1, 3)

    k_cmp = rms_norm(nsa_compress(kv_heads(k_c), cmp_pe[0], cmp_w1[0], cmp_w2[0]), k_gain[0])
    v_cmp = nsa_compress(kv_heads(v_c), cmp_pe[1], cmp_w1[1], cmp_w2[1])
    n_cmp = k_cmp.shape[2]
    n_sel = seq // L_SEL
    k_sel = min(N_SELECT, n_sel)
    k_slc = rms_norm(kv_heads(k_s), k_gain[1]).reshape(bsz, NSA_KV_HEADS, n_sel, L_SEL, HEAD_DIM)
    v_slc = kv_heads(v_s).reshape(bsz, NSA_KV_HEADS, n_sel, L_SEL, HEAD_DIM)
    pad = ((0, 0), (0, 0), (WINDOW, 0), (0, 0))
    k_win = jnp.pad(rms_norm(kv_heads(k_w), k_gain[2]), pad)
    v_win = jnp.pad(kv_heads(v_w), pad)
    gates = jax.nn.sigmoid(gate_logits.reshape(bsz, seq, NSA_KV_HEADS, NSA_GROUP, N_BRANCH)
                           .astype(jnp.float32)).astype(q.dtype).transpose(0, 2, 3, 1, 4)
    overlap = cmp_to_sel_overlap(n_cmp, n_sel)
    table_kg = t5_table.T.reshape(NSA_KV_HEADS, NSA_GROUP, T5_BUCKETS)
    cmp_end = jnp.arange(n_cmp) * CMP_STRIDE + (L_CMP - 1)
    sel_blk = jnp.arange(n_sel)
    b_ix = jnp.arange(bsz)[:, None, None, None]
    h_ix = jnp.arange(NSA_KV_HEADS)[None, :, None, None]
    kv_ix = jnp.arange(NSA_KV_HEADS)[None, :, None, None, None]
    g_ix = jnp.arange(NSA_GROUP)[None, None, :, None, None]
    scale = HEAD_DIM ** -0.5

    def shared_bias(dist):
        return jnp.moveaxis(t5_table[t5_bucket(dist)], -1, 0).reshape(NSA_KV_HEADS, NSA_GROUP, *dist.shape)

    def block(c):
        start = c * qb
        t = start + jnp.arange(qb)
        qc = lax.dynamic_slice_in_dim(q, start, qb, axis=3)
        gc = lax.dynamic_slice_in_dim(gates, start, qb, axis=3)
        dist_c = t[:, None] - cmp_end[None, :]
        s_c = jnp.einsum('bkgqd,bknd->bkgqn', qc, k_cmp).astype(jnp.float32) * scale + shared_bias(dist_c)
        p_c = masked_softmax(s_c, dist_c >= 0)
        o_c = jnp.einsum('bkgqn,bknd->bkgqd', p_c.astype(v_cmp.dtype), v_cmp)
        imp = jnp.einsum('bkgqn,nj->bkqj', p_c, overlap)
        blk_t = (t // L_SEL)[:, None]
        forced = (sel_blk[None, :] == 0) | (sel_blk[None, :] > blk_t - N_LOCAL)
        imp = jnp.where(sel_blk[None, :] > blk_t, -jnp.inf, jnp.where(forced, SEL_FORCE, imp))
        top_val, top_idx = lax.top_k(imp, k_sel)
        k_g = k_slc[b_ix, h_ix, top_idx].reshape(bsz, NSA_KV_HEADS, qb, k_sel * L_SEL, HEAD_DIM)
        v_g = v_slc[b_ix, h_ix, top_idx].reshape(bsz, NSA_KV_HEADS, qb, k_sel * L_SEL, HEAD_DIM)
        pos = (top_idx[..., None] * L_SEL + jnp.arange(L_SEL)).reshape(bsz, NSA_KV_HEADS, qb, k_sel * L_SEL)
        dist_s = t[:, None] - pos
        mask_s = (dist_s >= 0) & jnp.repeat(jnp.isfinite(top_val), L_SEL, axis=-1)
        bias_s = table_kg[kv_ix, g_ix, t5_bucket(dist_s)[:, :, None]]
        s_s = jnp.einsum('bkgqd,bkqsd->bkgqs', qc, k_g).astype(jnp.float32) * scale + bias_s
        p_s = masked_softmax(s_s, mask_s[:, :, None])
        o_s = jnp.einsum('bkgqs,bkqsd->bkgqd', p_s.astype(v_g.dtype), v_g)
        kw = lax.dynamic_slice_in_dim(k_win, start, WINDOW + qb, axis=2)
        vw = lax.dynamic_slice_in_dim(v_win, start, WINDOW + qb, axis=2)
        s_pos = start - WINDOW + jnp.arange(WINDOW + qb)
        dist_w = t[:, None] - s_pos[None, :]
        mask_w = (dist_w >= 0) & (dist_w < WINDOW) & (s_pos[None, :] >= 0)
        s_w = jnp.einsum('bkgqd,bknd->bkgqn', qc, kw).astype(jnp.float32) * scale + shared_bias(dist_w)
        p_w = masked_softmax(s_w, mask_w)
        o_w = jnp.einsum('bkgqn,bknd->bkgqd', p_w.astype(vw.dtype), vw)
        return gc[..., 0:1] * o_c + gc[..., 1:2] * o_s + gc[..., 2:3] * o_w

    out = lax.map(block, jnp.arange(seq // qb))
    return out.transpose(1, 0, 4, 2, 3, 5).reshape(bsz, seq, NSA_WIDTH)

def cross_attention(hn, memn, w_q, w_kv, q_gain, k_gain, w_o):
    bsz, seq, _ = hn.shape
    q = rms_norm((hn @ w_q).reshape(bsz, seq, X_HEADS, HEAD_DIM), q_gain)
    k, v = jnp.split(memn @ w_kv, 2, axis=-1)
    k = rms_norm(k.reshape(bsz, -1, X_HEADS, HEAD_DIM), k_gain)
    v = v.reshape(bsz, -1, X_HEADS, HEAD_DIM)
    s = jnp.einsum('bshd,bmhd->bhsm', q, k).astype(jnp.float32) * HEAD_DIM ** -0.5
    p = jax.nn.softmax(s, axis=-1).astype(v.dtype)
    o = jnp.einsum('bhsm,bmhd->bshd', p, v).reshape(bsz, seq, X_WIDTH)
    return o @ w_o

def swiglu(x, w_up, w_down):
    g, v = jnp.split(x @ w_up, 2, axis=-1)
    return (jax.nn.silu(g) * v) @ w_down

def moe_swiglu(x2, w_router, w_up, w_down):
    n_tok, d = x2.shape
    logits = (x2 @ w_router).astype(jnp.float32)
    top_val, top_idx = lax.top_k(logits, TOP_K)
    gate = jax.nn.softmax(top_val, axis=-1)
    e_flat = top_idx.reshape(-1)
    tok_flat = jnp.repeat(jnp.arange(n_tok), TOP_K)
    g_flat = gate.reshape(-1)
    n_asg = e_flat.shape[0]
    order = jnp.argsort(e_flat)
    e_s, tok_s, g_s = e_flat[order], tok_flat[order], g_flat[order]
    counts = jnp.bincount(e_flat, length=N_EXPERTS)
    padded = (counts + MOE_BLOCK - 1) // MOE_BLOCK * MOE_BLOCK
    start_s = jnp.cumsum(counts) - counts
    pad_end = jnp.cumsum(padded)
    start_p = pad_end - padded
    dest = start_p[e_s] + (jnp.arange(n_asg) - start_s[e_s])
    n_rows = (n_asg + MOE_BLOCK - 1) // MOE_BLOCK * MOE_BLOCK + N_EXPERTS * MOE_BLOCK
    row_tok = jnp.full((n_rows,), n_tok, jnp.int32).at[dest].set(tok_s)
    row_gate = jnp.zeros((n_rows,), jnp.float32).at[dest].set(g_s)
    n_blk = n_rows // MOE_BLOCK
    blk_exp = jnp.minimum(jnp.searchsorted(pad_end, jnp.arange(n_blk) * MOE_BLOCK, side='right'), N_EXPERTS - 1)
    x_pad = jnp.concatenate([x2, jnp.zeros((1, d), x2.dtype)], axis=0)
    xb = x_pad[row_tok].reshape(n_blk, MOE_BLOCK, d)

    def expert_block(args):
        xblk, e = args
        return swiglu(xblk, w_up[e], w_down[e])

    yb = lax.map(expert_block, (xb, blk_exp)).reshape(n_rows, d)
    y = yb * row_gate[:, None].astype(yb.dtype)
    return jax.ops.segment_sum(y, row_tok, num_segments=n_tok + 1)[:n_tok].astype(x2.dtype)

def setup_inputs(seed: int = 0) -> dict:
    key = jax.random.key(seed)
    ks = iter(jax.random.split(key, 40))
    f32 = jnp.float32
    L = DEPTH

    def nrm(shape, scale):
        return jax.random.normal(next(ks), shape, f32) * scale

    def gain(shape):
        return 1.0 + nrm(shape, 0.02)

    inp = {}
    inp['x'] = nrm((BATCH, SEQ, D_MODEL), 1.0)
    inp['mem'] = nrm((BATCH, MEM_LEN, D_MODEL), 1.0)
    inp['norm_mix'] = gain((L, D_MODEL))
    inp['w_in'] = nrm((L, D_MODEL, PROJ_WIDTH), D_MODEL ** -0.5)
    inp['ssm_lambda_re'] = -0.5 + nrm((L, SSM_GROUPS, SSM_STATE), 0.01)
    inp['ssm_lambda_im'] = math.pi * jnp.arange(SSM_STATE, dtype=f32) + nrm((L, SSM_GROUPS, SSM_STATE), 0.01)
    inp['ssm_log_dt'] = jax.random.uniform(next(ks), (L, SSM_GROUPS), f32, math.log(1e-3), math.log(1e-1))
    inp['ssm_b_re'] = nrm((L, SSM_GROUPS, SSM_STATE, SSM_GROUP), (2 * SSM_GROUP) ** -0.5)
    inp['ssm_b_im'] = nrm((L, SSM_GROUPS, SSM_STATE, SSM_GROUP), (2 * SSM_GROUP) ** -0.5)
    inp['ssm_c_re'] = nrm((L, SSM_GROUPS, SSM_GROUP, SSM_STATE), SSM_STATE ** -0.5)
    inp['ssm_c_im'] = nrm((L, SSM_GROUPS, SSM_GROUP, SSM_STATE), SSM_STATE ** -0.5)
    inp['ssm_d'] = nrm((L, SSM_GROUPS, SSM_GROUP), 1.0)
    inp['ssm_w_glu'] = nrm((L, SSM_WIDTH, 2 * SSM_WIDTH), SSM_WIDTH ** -0.5)
    inp['conv_w_dw'] = nrm((L, CONV_K, CONV_WIDTH), CONV_K ** -0.5)
    inp['conv_b_dw'] = nrm((L, CONV_WIDTH), 0.02)
    inp['conv_ln_g'] = gain((L, CONV_WIDTH))
    inp['conv_ln_b'] = nrm((L, CONV_WIDTH), 0.02)
    inp['conv_w_pw'] = nrm((L, CONV_WIDTH, CONV_WIDTH), CONV_WIDTH ** -0.5)
    inp['nsa_q_norm'] = gain((L, HEAD_DIM))
    inp['nsa_k_norm'] = gain((L, N_BRANCH, HEAD_DIM))
    inp['nsa_cmp_pe'] = nrm((L, 2, L_CMP, HEAD_DIM), 0.1)
    inp['nsa_cmp_w1'] = nrm((L, 2, L_CMP * HEAD_DIM, HEAD_DIM), (L_CMP * HEAD_DIM) ** -0.5)
    inp['nsa_cmp_w2'] = nrm((L, 2, HEAD_DIM, HEAD_DIM), HEAD_DIM ** -0.5)
    inp['mix_out_norm'] = gain((L, D_MIX))
    inp['w_out'] = nrm((L, D_MIX, D_MODEL), D_MIX ** -0.5)
    inp['t5_table'] = nrm((T5_BUCKETS, NSA_HEADS), 0.5)
    inp['norm_cross'] = gain((L, D_MODEL))
    inp['norm_mem'] = gain((L, D_MODEL))
    inp['x_w_q'] = nrm((L, D_MODEL, X_WIDTH), D_MODEL ** -0.5)
    inp['x_w_kv'] = nrm((L, D_MODEL, 2 * X_WIDTH), D_MODEL ** -0.5)
    inp['x_q_norm'] = gain((L, HEAD_DIM))
    inp['x_k_norm'] = gain((L, HEAD_DIM))
    inp['x_w_o'] = nrm((L, X_WIDTH, D_MODEL), X_WIDTH ** -0.5)
    inp['norm_ffn'] = gain((L, D_MODEL))
    inp['ffn_w_up'] = nrm((N_DENSE, D_MODEL, 2 * D_FF), D_MODEL ** -0.5)
    inp['ffn_w_down'] = nrm((N_DENSE, D_FF, D_MODEL), D_FF ** -0.5)
    inp['moe_router'] = nrm((N_MOE, D_MODEL, N_EXPERTS), D_MODEL ** -0.5)
    inp['moe_w_up'] = nrm((N_MOE, N_EXPERTS, D_MODEL, 2 * D_FF), D_MODEL ** -0.5)
    inp['moe_w_down'] = nrm((N_MOE, N_EXPERTS, D_FF, D_MODEL), D_FF ** -0.5)
    return inp

def reference(x, mem, norm_mix, w_in, ssm_lambda_re, ssm_lambda_im, ssm_log_dt, ssm_b_re, ssm_b_im,
              ssm_c_re, ssm_c_im, ssm_d, ssm_w_glu, conv_w_dw, conv_b_dw, conv_ln_g, conv_ln_b, conv_w_pw,
              nsa_q_norm, nsa_k_norm, nsa_cmp_pe, nsa_cmp_w1, nsa_cmp_w2, mix_out_norm, w_out, t5_table,
              norm_cross, norm_mem, x_w_q, x_w_kv, x_q_norm, x_k_norm, x_w_o, norm_ffn, ffn_w_up, ffn_w_down,
              moe_router, moe_w_up, moe_w_down):
    bsz, seq, d = x.shape
    kv_w = NSA_KV_HEADS * HEAD_DIM
    cuts = [int(c) for c in np.cumsum([SSM_WIDTH, 2 * CONV_WIDTH, NSA_WIDTH] + [kv_w] * 6)]
    h = x
    for layer in range(DEPTH):
        z = rms_norm(h, norm_mix[layer]) @ w_in[layer]
        u_ssm, z_conv, q, k_c, v_c, k_s, v_s, k_w, v_w, g_nsa = jnp.split(z, cuts, axis=-1)
        y_ssm = s5_mixer(u_ssm, ssm_lambda_re[layer], ssm_lambda_im[layer], ssm_log_dt[layer],
                         ssm_b_re[layer], ssm_b_im[layer], ssm_c_re[layer], ssm_c_im[layer],
                         ssm_d[layer], ssm_w_glu[layer])
        y_conv = conv_mixer(z_conv, conv_w_dw[layer], conv_b_dw[layer], conv_ln_g[layer],
                            conv_ln_b[layer], conv_w_pw[layer])
        y_nsa = nsa_mixer(q, k_c, v_c, k_s, v_s, k_w, v_w, g_nsa, nsa_q_norm[layer], nsa_k_norm[layer],
                          nsa_cmp_pe[layer], nsa_cmp_w1[layer], nsa_cmp_w2[layer], t5_table)
        y = jnp.concatenate([_rms(y_ssm), _rms(y_conv), _rms(y_nsa)], axis=-1) * mix_out_norm[layer]
        h = h + y @ w_out[layer]
        h = h + cross_attention(rms_norm(h, norm_cross[layer]), rms_norm(mem, norm_mem[layer]),
                                x_w_q[layer], x_w_kv[layer], x_q_norm[layer], x_k_norm[layer], x_w_o[layer])
        hn = rms_norm(h, norm_ffn[layer])
        if layer % 2 == 0:
            h = h + swiglu(hn, ffn_w_up[layer // 2], ffn_w_down[layer // 2])
        else:
            h = h + moe_swiglu(hn.reshape(bsz * seq, d), moe_router[layer // 2], moe_w_up[layer // 2],
                               moe_w_down[layer // 2]).reshape(bsz, seq, d)
    return h


_drawn_inputs = setup_inputs


def setup_inputs(seed=0):
    import zlib

    import numpy as np

    out = dict(_drawn_inputs(seed))
    spreads = {}
    factors = {'ssm_lambda_re': 64.0,
     'nsa_q_norm': 3.421,
     'nsa_k_norm': 4.941,
     'norm_cross': 8.0,
     'norm_mem': 5.86,
     'x_q_norm': 6.037,
     'x_k_norm': 7.337,
     'norm_ffn': 3.149}
    for name, (base, spread) in spreads.items():
        noise = np.random.default_rng([zlib.crc32(name.encode()), seed]).standard_normal(out[name].shape)
        drawn = base * np.exp(spread * noise) if base else spread * noise
        out[name] = __import__('jax').numpy.asarray(drawn.astype(out[name].dtype))
    for name, factor in factors.items():
        out[name] = (out[name] * factor).astype(out[name].dtype)
    return out
```

```python
from contextlib import ExitStack
import math

import numpy as np

import concourse.bass as bass
from concourse import mybir

F32 = mybir.dt.float32
BF16 = mybir.dt.bfloat16
I32 = mybir.dt.int32
ALU = mybir.AluOpType
ACT = mybir.ActivationFunctionType
AX = mybir.AxisListType.X

P = 128
D, SEQ, L = 1024, 256, 2
KT, NT = D // P, SEQ // P
HD, NH, KVH = 64, 8, 2
XH = 4
G, GP, GH = 16, 64, 16
SJ = G * GP // P
CK, CW = 31, 256
NCMP, STRIDE, LCMP = 15, 16, 32
BUCKETS, MAXD = 32, 128
PROJ = 2072
FF, E, TOPK = 2816, 8, 2
HT = FF // P
CH = HT // 2
CAP = 96
PASSES = -(-SEQ // CAP)
EPS = 1e-6
NEG = -1e30
SCALE = HD ** -0.5
SLOTS = 4
UPW, DNW = KT * 2 * 256, 2 * D
FF_SLOTS = [2, 3, 1, 0, 2, 3, 1, 0, 2, 3, 1]
GELU_C, GELU_S = 0.044715, math.sqrt(2 / math.pi)
TWO_PI_HI = 6.28125
TWO_PI_LO = 2 * math.pi - TWO_PI_HI
ROUND = 1.5 * 2 ** 23
FX = 384

C_ID, C_M16, C_M64, C_NH, C_TRI, C_ONE, C_IOTA, C_LT, C_PASS = 0, 128, 130, 132, 148, 276, 404, 500, 564
C_MOE, C_END = C_TRI, 588


def shape_constants():
    c = np.zeros((P, C_END), np.float32)
    p = np.arange(P)
    c[:, C_ID:C_ID + P] = np.eye(P)
    c[:, C_TRI:C_TRI + P] = p[:, None] < p[None, :]
    c[:, C_ONE:C_ONE + P] = 1.0
    c[:, C_M16:C_M16 + 2] = (p[:, None] // GH) % 2 == np.arange(2)
    c[:, C_M64:C_M64 + 2] = p[:, None] // GP == np.arange(2)
    c[:, C_IOTA:C_IOTA + CAP] = np.arange(CAP)
    c[:, C_LT:C_LT + 64] = (np.arange(8)[None, :] < np.arange(8)[:, None]).reshape(64)
    c[:, C_PASS:C_PASS + 24] = np.repeat(np.arange(PASSES) * CAP, E)
    c[:, C_NH:C_NH + 16] = -0.5
    j = np.arange(512)
    n = np.maximum(j - 255, 0)
    nf = np.maximum(n, 1).astype(np.float32)
    large = 16 + (np.log(nf / np.float32(16)) / np.float32(math.log(MAXD / 16)) * np.float32(16)).astype(np.int32)
    b = np.where(n < 16, n, np.minimum(large, BUCKETS - 1))
    hot = np.zeros((BUCKETS + 1, 512), np.float32)
    hot[b, j] = 1.0
    hot[:, j < 255] = 0.0
    hot[BUCKETS, j < 255] = 1.0
    return c, hot


class Sems:

    def __init__(self, nc, ctx):
        self.nc, self.ctx, self.made = nc, ctx, {}

    def __getitem__(self, name):
        if name not in self.made:
            self.made[name] = self.ctx.enter_context(self.nc.semaphore(name))
        return self.made[name]


class Banks:

    def __init__(self, sems):
        self.filled = [sems[f"bank{b}_filled"] for b in range(8)]
        self.drained = [sems[f"bank{b}_drained"] for b in range(8)]
        self.at, self.fills, self.drains = {}, [0] * 8, [0] * 8
        self.opened = [0] * 8
        self.loop = None

    def add(self, name, bank, readers=1):
        assert name not in self.at, name
        self.at[name] = (bank, self.fills[bank], self.drains[bank], self.loop)
        self.fills[bank] += 1
        self.drains[bank] += readers

    def begin_loop(self):
        self.loop = {"fills": list(self.fills), "drains": list(self.drains)}

    def end_loop(self):
        a = self.loop
        a["per_f"] = [x - y for x, y in zip(self.fills, a["fills"])]
        a["per_d"] = [x - y for x, y in zip(self.drains, a["drains"])]
        self.loop = None

    def bank(self, name):
        return self.at[name][0]

    def count(self, name, turn, filled):
        bank, f, d, loop = self.at[name]
        n = f + 1 if filled else d
        if loop is None or turn is None:
            return n
        per = (loop["per_f"] if filled else loop["per_d"])[bank]
        return n + turn * per if per else n

    def open(self, pe, name, turn=None):
        bank, f, _, loop = self.at[name]
        if turn is None or loop is None:
            assert self.opened[bank] == f, name
            self.opened[bank] += 1
        n = self.count(name, turn, False)
        if not (isinstance(n, int) and n == 0):
            pe.wait_ge(self.drained[self.bank(name)], n)

    def wait(self, eng, name, turn=None):
        eng.wait_ge(self.filled[self.bank(name)], self.count(name, turn, True))

    def fill(self, name):
        return self.filled[self.bank(name)]

    def drain(self, name):
        return self.drained[self.bank(name)]


def plan_banks(banks):
    add = banks.add
    add("par", 0, 2)
    add("t5", 1)
    for l in range(L):
        def a(name, bank, readers=1):
            add(f"{name}{l}", bank, readers)
        for g in range(4):
            a(f"mix_T{g}_", g % 2)
        if l == 0:
            for g in range(4):
                a(f"mem_T{g}_", 6 + g % 2)
        a("u", 2); a("bu0_", 3); a("ca", 6); a("bu1_", 4); a("cg", 7)
        a("q0_", 5, 2); a("q1_", 0, 2)
        a("bu2_", 3); a("kvc", 1); a("bu3_", 4)
        a("kv0_", 6, 3); a("kv1_", 7, 3); a("gates", 2); a("ys", 2)
        a("bu4_", 3); a("bu5_", 4); a("bu6_", 3); a("bu7_", 4)
        a("qT00_", 5); a("qT01_", 0); a("qT10_", 5); a("qT11_", 0)
        a("kT0_", 1); a("kT1_", 5)
        a("cmp1_", 6); a("cmp2_", 7, 2); a("cmpT", 6)
        a("glu0_", 3, 2); a("glu1_", 4, 2)
        a("cvT", 1, 1); a("cvB", 2); a("cvW", 1)
        a("mkv0_", 6, 3); a("mkv1_", 7, 3)
        a("mkT0_", 6); a("mkT1_", 7)
        for i in range(NT):
            a(f"sc_c{i}_", 3); a(f"pcT{i}0_", 4); a(f"pcT{i}1_", 5)
            for h in range(NH):
                a(f"sc{i}{h}_", h % 2)
            for h in range(NH):
                a(f"pT{i}{h}_", 6 + h % 2)
            a(f"oc{i}_", 3); a(f"os{i}_", 4); a(f"ow{i}_", 5)
        for g in range(4):
            a(f"y_T{g}_", g % 2)
        for g in range(4):
            a(f"out{g}_", 2 + g, 0)
        for g in range(4):
            a(f"cross_T{g}_", g % 2)
        a("xq", 2, 2); a("xqT0_", 3); a("xqT1_", 4)
        for u in range(4):
            a(f"xs{u}_", 6 + u % 2, 0)
            a(f"xpT{u}_", u % 2)
        a("xo0_", 2); a("xo1_", 5); a("xoT", 3)
        for g in range(4):
            a(f"xout{g}_", 4 + g, 0)
        for g in range(4):
            a(f"ffn_T{g}_", g % 2)
        if l == 0:
            for t in range(HT):
                add(f"up{t}", t % 4, 0)
            for g in range(4):
                add(f"down{g}", 4 + g, 0)
        else:
            add("router", 2)
            add("count", 3)
            add("gather0", 6); add("gather1", 7); add("gateT", 2)
            banks.begin_loop()
            for t in range(HT):
                add(f"mup{t}", t % 4, 0)
            for g in range(2):
                add(f"mdown{g}", 4 + g)
            add("ngather0", 6); add("ngather1", 7); add("ngateT", 2)
            add("sc0", 6); add("sc1", 7); add("sc2", 6); add("sc3", 7)
            
            banks.end_loop()


def trunk(nc, x, mem, w_in, w_glu, w_pw, cmp_w1, cmp_w2, w_out, t5_table, x_w_q, x_w_kv, x_w_o,
          ffn_up, ffn_down, router, moe_up, moe_down, rows128, rows64, lam_re, lam_im, log_dt, conv_w,
          b_re, b_im, c_re, c_im, cmp_pe, consts, t5_hot, bias_rows, out):
    with ExitStack() as ctx:
        sem = Sems(nc, ctx)
        banks = Banks(sem)
        plan_banks(banks)
        slot_full = [sem[f"slot{s}_full"] for s in range(SLOTS)]
        slot_free = [sem[f"slot{s}_free"] for s in range(SLOTS)]

        def sb(name, shape, dt=F32):
            return ctx.enter_context(nc.sbuf_tensor(name, shape, dt))

        pb = [ctx.enter_context(nc.psum_tensor(f"bank{b}", [P, 512], F32)) for b in range(8)]

        def ps(name):
            return pb[banks.bank(name)]

        h = sb("h", [P, NT, D])
        xn = sb("xn", [P, NT, D])
        xT = sb("xT", [P, KT, SEQ])
        memT = sb("memT", [P, KT, SEQ])
        ring = sb("ring", [P, SLOTS, UPW + DNW])
        cst = sb("cst", [P, C_MOE])
        tab = sb("tab", [BUCKETS + 1, NH])
        M = sb("M", [P, NH, FX])
        par = sb("par", [P, 264])
        gk = sb("gk", [HD, L, 4])
        qT = sb("qT", [P, NT, NH, P])
        kT = sb("kT", [P, 4, SEQ])
        kn = sb("kn", [P, NT, 2, P])
        vv = sb("vv", [P, NT, 2, P])
        gates = sb("gates", [P, NT, 24])
        kcT = sb("kcT", [HD, KVH, NCMP])
        kcn = sb("kcn", [NCMP, KVH, HD])
        vc = sb("vc", [NCMP, KVH, HD])
        cmpx = sb("cmpx", [HD, 4, 2, KVH, NCMP])
        cb = sb("cb", [HD, 2])
        uT = sb("uT", [P, 2, SEQ])
        cv = sb("cv", [P, 2, CK - 1 + SEQ])
        ca = sb("ca", [P, 2, SEQ])
        R = sb("R", [P, 2, SJ, SEQ])
        zz = sb("zz", [P, 2, 2, SEQ])
        X = sb("X", [P, 2, 2, SEQ])
        BL = sb("BL", [P, 2, 2, 2, GP])
        CL = sb("CL", [P, 2, SJ, 32])
        mag = sb("mag", [P, SJ])
        wn = sb("wn", [P, 2, 2, SJ])
        wt = sb("wt", [P, 2, SJ])
        ldt = sb("ldt", [P, 36])
        scr = sb("scr", [P, 4, 512])
        pc = sb("pc", [P, NH, NCMP])
        sq = sb("sq", [P, 512])
        st = sb("st", [P, 160])
        rs = sb("rs", [P, 160])
        nmx = sb("nmx", [P, 2, 2])
        sums = sb("sums", [P, NT, 2, NH])
        sumc = sb("sumc", [P, NT, 3, NH])
        mxc = sb("mxc", [P, NH])
        rt = sb("rt", [P, KT, E])
        hT = zz[:].rearrange("p a b t -> p (a b) t")
        th = X[:, 1]
        junk = ca[:].rearrange("p a t -> p (a t)").bitcast(BF16)
        vx = X[:, 0]
        pcT = zz[0:NCMP].rearrange("p a b t -> p (a b t)").rearrange("p (h t) -> p h t", h=NH)
        lnb = scr[:, 1].rearrange("p (i c) -> p i c", i=NT)
        cste = memT[:].rearrange("p k t -> p (k t)")[:, 0:C_END - C_MOE]
        Rf = R[:].rearrange("p a j t -> p (a j t)")
        xg = Rf[:, 0:768].rearrange("p (k c) -> p k c", k=KT)
        ye = Rf[0:CAP, 768:1792]
        one = Rf[:, 1792:1984].rearrange("p (i c) -> p i c", i=NT)
        og = Rf[:, 1984:2176].rearrange("p (i c) -> p i c", i=NT)
        ogT = Rf[0:CAP, 2176:2432]
        table = Rf[:, 2432:2532].rearrange("p (e k) -> p e k", k=4)
        cur = Rf[:, 2532:2536]
        lg = Rf[:, 2560:2576].rearrange("p (i e) -> p i e", i=NT)
        cmpj = Rf[:, 2576:2704].rearrange("p (i e j) -> p i e j", i=NT, e=E)
        cmpe = Rf[:, 2704:2832].rearrange("p (i e j) -> p i e j", i=NT, e=E)
        rk = Rf[:, 2832:2848].rearrange("p (i e) -> p i e", i=NT)
        sel = Rf[:, 2848:2864].rearrange("p (i e) -> p i e", i=NT)
        ex = Rf[:, 2864:2880].rearrange("p (i e) -> p i e", i=NT)
        mx2 = Rf[:, 2880:2884]
        pos = Rf[:, 2896:2912].rearrange("p (i e) -> p i e", i=NT)
        gsum = Rf[:, 2912:2916]
        flag = sb("flag", [1, 4], I32)

        ident = cst[:, C_ID:C_ID + P]
        raw = ring[:, 3, 0:P]
        hot = ring[0:BUCKETS + 1, 3, 512:1024]
        raw2 = ring[:, 3, P:2 * P]
        raw3 = ring[0:12, 3, 2 * P:2 * P + HD]
        memx = ring[:, 2, 0:NT * D].rearrange("p (i d) -> p i d", i=NT)
        q_of = [xn[:, i, 0:512] for i in range(NT)]
        CX = xn[:, :, 512:1024].rearrange("p kv (a t) -> p kv a t", a=KVH)

        def c_norm(n, i): return 2 * n + i
        def c_qk(l, i): return 16 + 24 * l + 12 * i
        def c_ln(l): return 64 + 2 * l
        def c_kc(l): return 68 + 2 * l
        def c_grp(l, i): return 72 + 6 * l + 3 * i
        def c_xk(l, i): return 84 + 8 * l + 4 * i
        def c_xq(l, i): return 100 + 8 * l + 4 * i
        NORM = {"mix0": 0, "mem": 1, "cross0": 2, "ffn0": 3, "mix1": 4, "cross1": 5, "ffn1": 6}
        G_MIX, G_CROSS, G_FFN, G_MEM, G_OUT, G_CB, G_LG, G_LB, G_D = 0, 16, 32, 48, 64, 80, 84, 88, 92

        def gain(base, l, k0, n):
            return par[:, base + KT * l + k0:base + KT * l + k0 + n]

        def small(l):
            s = ring[:, 0]
            return dict(w1=s[:, 0:2048].rearrange("p (v t o) -> p v t o", v=2, t=16),
                        glu=s[:, 2048:3072].rearrange("p (a n) -> p a n", a=2),
                        pw=s[:, 3072:3584].rearrange("p (a n) -> p a n", a=2),
                        xo=s[:, 3584:5632].rearrange("p (k n) -> p k n", k=2),
                        w2=s[0:HD, 5632:5760].rearrange("p (v o) -> p v o", v=2),
                        pe=s[:, 5760:5792].rearrange("p (v t) -> p v t", v=2))

        fill_of, counts = {}, [0] * SLOTS
        loads = {}
        for l in range(L):
            for n, c in enumerate(["in0", "in1", "in2", "in3", "small", "x", "out0", "out1"]):
                loads[c] = {"in3": 2, "small": 13, "x": 2}.get(c, 1)
                counts[n % 4] += 1
                fill_of[f"{c}_{l}"] = (n % 4, counts[n % 4])
            for c in range(CH if l == 0 else 0):
                s = FF_SLOTS[c]
                counts[s] += 1
                fill_of[f"ff{c}"] = (s, counts[s])
        full_before, k_full = {}, [0] * SLOTS
        for name, (s, n) in fill_of.items():
            k_full[s] += 16 * loads.get(name.rsplit("_", 1)[0], 3)
            full_before[name] = k_full[s]
        LOOP_FULL = list(k_full)
        LAST_USE = {"in0": "ca", "in1": "q1_", "in2": "kvc", "in3": "gates", "small": "xout3_", "x": "xq",
                    "out0": "out2_", "out1": "out3_"}
        USES = [FF_SLOTS.count(s) for s in range(SLOTS)]
        nth = [FF_SLOTS[:c].count(FF_SLOTS[c]) for c in range(CH)]

        def weights_in(eng, name):
            s, _ = fill_of[name]
            eng.wait_ge(slot_full[s], full_before[name])

        def expert_in(eng, turn, c):
            s = FF_SLOTS[c]
            eng.wait_ge(slot_full[s], turn * (48 * USES[s]) + (LOOP_FULL[s] + 48 * (nth[c] + 1)))

        dma_out = sem["out_written"]

        def transposed(u):
            l, k = divmod(u, 20)
            return f"pT{k // 8}{k % 8}_{l}" if k < 16 else f"xpT{k - 16}_{l}"
        block = ctx.enter_context(nc.Block())

        @block.sync
        def _(sp):
            for i in range(NT):
                sp.dma_start(h[:, i], x[i * P:(i + 1) * P]).then_inc(sem["x_loaded"], 16)

            def slot_is_free(name):
                s, n = fill_of[name]
                before = [k for k, v in fill_of.items() if v == (s, n - 1)]
                if not before:
                    return
                if before[0].startswith("ff"):
                    c = int(before[0][2:])
                    sp.wait_ge(slot_free[s], nth[c] + 1)
                else:
                    banks.wait(sp, LAST_USE[before[0][:-2]] + before[0][-1])

            def item(name, parts):
                s, n = fill_of[name]
                assert len(parts) == loads.get(name.rsplit("_", 1)[0], 3), name
                slot_is_free(name)
                for dst, src in parts:
                    sp.dma_start(dst, src).then_inc(slot_full[s], 16)

            def wide(w, c0, n):
                return w[:, c0:c0 + n].rearrange("(k p) n -> p k n", p=P)

            for l in range(L):
                for c in range(4):
                    if l == 0 and c == 2:
                        banks.wait(sp, "mem_T3_0")
                    if l == 0 and c == 3:
                        banks.wait(sp, "par")
                        sp.wait_ge(sem["m_stored"], 16)
                    parts = [(ring[:, c, 0:4096].rearrange("p (k n) -> p k n", k=KT), wide(w_in[l], 512 * c, 512))]
                    if c == 3:
                        parts.append((ring[:, 3, 4096:4288].rearrange("p (k n) -> p k n", k=KT), wide(w_in[l], 2048, 24)))
                    item(f"in{c}_{l}", parts)
                m = small(l)
                parts = []
                for v in range(2):
                    w1 = cmp_w1[l, v].rearrange("(a t d) o -> a d t o", a=2, t=16)
                    for a in range(2):
                        parts.append((m["w1"][64 * a:64 * a + 64, v], w1[a]))
                for a in range(2):
                    parts.append((m["glu"][:, a], w_glu[l, a * P:(a + 1) * P]))
                    parts.append((m["pw"][:, a], w_pw[l, a * P:(a + 1) * P]))
                    parts.append((m["xo"][:, a], x_w_o[l, a * P:(a + 1) * P]))
                parts.append((m["w2"], cmp_w2[l].rearrange("v d o -> d v o")))
                for v in range(2):
                    parts.append((m["pe"][:, v], cmp_pe[l, v]))
                item(f"small_{l}", parts)
                item(f"x_{l}", [(ring[:, 1, 0:4096].rearrange("p (k n) -> p k n", k=KT), wide(x_w_kv[l], 0, 512)),
                                (ring[:, 1, 4096:6144].rearrange("p (k n) -> p k n", k=KT), wide(x_w_q[l], 0, 256))])
                for c in range(2):
                    item(f"out{c}_{l}", [(ring[:, 2 + c, 0:4096].rearrange("p (k n) -> p k n", k=KT),
                                          wide(w_out[l], 512 * c, 512))])
                if l == 0:
                    for c in range(CH):
                        s = FF_SLOTS[c]
                        item(f"ff{c}", [
                            (ring[:, s, 0:UPW].rearrange("p (k g n) -> p k g n", k=KT, g=2)[:, :, g],
                             wide(ffn_up[0], g * FF + 256 * c, 256)) for g in range(2)] + [
                            (ring[:, s, UPW:].rearrange("p (m n) -> p m n", m=2),
                             ffn_down[0, 256 * c:256 * c + 256].rearrange("(m p) n -> p m n", p=P))])

            def expert(turn, e):
                for c in range(CH):
                    s = FF_SLOTS[c]
                    if nth[c] == 0:
                        banks.wait(sp, LAST_USE[{0: "small", 1: "x", 2: "out0", 3: "out1"}[s]] + "1")
                    sp.wait_ge(slot_free[s], turn * USES[s] + (USES[s] + nth[c]))
                    up = moe_up[bass.ds(e, 1)].rearrange("o (k p) (g n) -> p (o k) g n", p=P, g=2)
                    down = moe_down[bass.ds(e, 1), 256 * c:256 * c + 256].rearrange("o (m p) n -> p (o m) n", p=P)
                    for g in range(2):
                        sp.dma_start(ring[:, s, 0:UPW].rearrange("p (k g n) -> p k g n", k=KT, g=2)[:, :, g],
                                     up[:, :, g, 256 * c:256 * c + 256]).then_inc(slot_full[s], 16)
                    sp.dma_start(ring[:, s, UPW:].rearrange("p (m n) -> p m n", m=2), down).then_inc(slot_full[s], 16)

            with sp.Fori(0, E) as e:
                expert(e, e)
            sp.wait_ge(sem["flag_ready"], 1)
            over = sp.value_load(flag[0:1, 0:1], min_val=0, max_val=1)
            with sp.If(over > 0):
                for p in range(1, PASSES):
                    with sp.Fori(0, E) as e:
                        expert(e + p * E, e)
            sp.wait_ge(sem["h_final"], 1)
            for i in range(NT):
                sp.dma_start(out[i * P:(i + 1) * P], h[:, i]).then_inc(dma_out, 16)
            sp.wait_ge(dma_out, 16 * NT)

        @block.scalar
        def _(act):
            def load(dst, src, name):
                act.dma_start(dst, src, allow_slow_non_contiguous=True).then_inc(sem[name], 16)

            load(cst[:], consts[:, 0:C_MOE], "par_loaded")
            load(raw, rows128, "par_loaded")
            load(raw2[0:2 * CK * L], conv_w.rearrange("l k (a p) -> (l k a) p", p=P), "par_loaded")
            load(raw3, rows64, "par_loaded")
            load(memx, mem.rearrange("(i p) d -> p i d", p=P), "mem_loaded")
            load(hot[:], t5_hot, "t5_loaded")
            load(tab[0:BUCKETS], t5_table, "t5_loaded")
            load(ldt[:, 0:32], bass.AP(tensor=log_dt.tensor, offset=0, ap=[[0, P], [1, L * G]]), "ldt_loaded")
            for l in range(L):
                for a in range(2):
                    load(ldt[:, 32 + 2 * l + a:33 + 2 * l + a],
                         bass.AP(tensor=log_dt.tensor, offset=l * G + 8 * a, ap=[[1, 8], [0, GH], [1, 1]]), "ldt_loaded")

            def s5_params(l):
                for a in range(2):
                    for t, lam in ((0, lam_re), (1, lam_im)):
                        load(scr[:].rearrange("p a b -> p (a b)")[:, 136 * t + 8 + 64 * a:136 * t + 72 + 64 * a],
                             bass.AP(tensor=lam.tensor, offset=l * 1024 + 512 * a, ap=[[64, 8], [0, GH], [1, 64]]), "s5_loaded")
                Xf = X[:].rearrange("p a b t -> p (a b t)")
                for n, b in enumerate((b_re, b_im)):
                    load(Xf[:, n * P:(n + 1) * P].rearrange("p (a s) -> p a s", a=2),
                         b[l].rearrange("(a c) s -> c a s", a=2), "s5_loaded")
                for n, c in enumerate((c_re, c_im)):
                    load(Xf[:, (2 + n) * P:(3 + n) * P].rearrange("p (j c) -> p j c", j=SJ),
                         c[l].rearrange("(j s) c -> s j c", j=SJ), "s5_loaded")

            load(rt[:], router.rearrange("(k p) e -> p k e", p=P), "router_loaded")
            s5_params(0)
            squared = [0]

            def squares(src, n, i, wait):
                wait()
                if squared[0]:
                    act.wait_ge(sem["norm_sum"], squared[0])
                squared[0] += 1
                act.activation(junk, src, ACT.Square, accum_out=st[:, c_norm(n, i):c_norm(n, i) + 1])\
                   .then_inc(sem["norm_sum"], 1)

            def scaled(dst, src, n):
                act.wait_ge(sem["norm_rs"], n + 1)
                act.activation(dst, src, ACT.Copy, scale=rs[:, c_norm(n, 1):c_norm(n, 1) + 1])\
                   .then_inc(sem["xn1_ready"], 1)

            def gained(name, base, l, groups):
                for g in groups:
                    banks.wait(act, f"{name}{g}_{l}")
                    for k in range(2):
                        i = act.activation(xT[:, 2 * g + k], ps(f"{name}{g}_{l}")[:, 256 * k:256 * k + 256], ACT.Copy,
                                           scale=gain(base, l, 2 * g + k, 1))
                    i.then_inc(banks.drain(f"{name}{g}_{l}"), 1)

            act.wait_ge(banks.drain("t5"), 1)
            act.dma_start(bias_rows, hot[0:NH]).then_inc(sem["m_stored"], 16)
            banks.wait(act, "par")
            act.activation(par[:, 0:P], ps("par")[:, 0:P], ACT.Copy).then_inc(banks.drain("par"), 1)

            def s5_exps(l):
                S = scr[:].rearrange("p a b -> p (a b)")
                t = [S[:, 136 * n:136 * n + 136] for n in range(15)]
                act.wait_ge(sem["s5_dt"], l + 1)
                act.activation(t[3], t[2], ACT.Exp).then_inc(sem["s5_act"], 1)
                act.wait_ge(sem["s5_x1"], l + 1)
                act.activation(t[5], t[4], ACT.Exp).then_inc(sem["s5_act"], 1)
                act.wait_ge(sem["s5_ang"], 2 * l + 1)
                act.activation(t[8], t[7], ACT.Sin).then_inc(sem["s5_act"], 1)
                act.wait_ge(sem["s5_ang"], 2 * l + 2)
                act.activation(t[11], t[10], ACT.Sin).then_inc(sem["s5_act"], 1)

            def probs(u, b, src, scale, to):
                return act.activation(scr[:, u % 2, b * 256:b * 256 + src.shape[-1]] if src.shape[-1] == 256 else
                                      scr[:, u % 2, b * P:b * P + P], src, ACT.Exp, bias=nmx[:, u % 2, b:b + 1],
                                      scale=scale, accum_out=to)

            def pt_copy(u, name, n):
                banks.wait(act, name)
                if u >= 2:
                    act.wait_ge(sem["pv_done"], u - 1)
                act.activation(scr[:, 2 + u % 2, 0:n], ps(name)[:, 0:n], ACT.Copy).then_inc(banks.drain(name), 1)

            def q_copy(l, nm, dst):
                banks.wait(act, nm)
                act.activation(dst, ps(nm)[0:HD].rearrange("p (h t) -> p h t", h=4), ACT.Copy).then_inc(banks.drain(nm), 1)

            for l in range(L):
                n = NORM[f"mix{l}"]
                for i in range(NT):
                    squares(h[:, i], n, i, lambda: act.wait_ge(sem["x_loaded"], 16 * NT) if l == 0 else
                            act.wait_ge(sem["h_added"], 12 * l - 2 + 2 * i))
                scaled(xn[:, 1], h[:, 1], n)
                if l == 0:
                    for i in range(NT):
                        squares(memx[:, i], 1, i, lambda: act.wait_ge(sem["mem_loaded"], 16))
                    act.wait_ge(sem["par_ready"], 1)
                gained("mix_T", G_MIX, l, (1, 3))
                if l == 0:
                    act.wait_ge(sem["m_stored"], 16)
                    load(M[:], bass.AP(tensor=bias_rows.tensor, offset=0, ap=[[1, P], [512, NH], [1, FX]]), "m_loaded")
                    act.wait_ge(sem["norm_rs"], 2)
                    for i in range(NT):
                        act.activation(memx[:, i], memx[:, i], ACT.Copy, scale=rs[:, c_norm(1, i):c_norm(1, i) + 1])\
                           .then_inc(sem["memx_ready"], 1)
                    for g in range(4):
                        banks.wait(act, f"mem_T{g}_0")
                        act.activation(memT[:, 2 * g:2 * g + 2], ps(f"mem_T{g}_0")[:].rearrange("p (k t) -> p k t", k=2),
                                       ACT.Copy).then_inc(banks.drain(f"mem_T{g}_0"), 1)
                    s5_exps(0)
                banks.wait(act, f"cg{l}")
                act.activation(ca[:], ps(f"cg{l}")[:].rearrange("p (a t) -> p a t", a=2), ACT.Tanh, scale=0.5)\
                   .then_inc(banks.drain(f"cg{l}"), 1)
                for i in range(NT):
                    banks.wait(act, f"q{i}_{l}")
                    if 4 * l + i:
                        act.wait_ge(sem["head_sum"], 7 * l + i)
                    act.activation(sq[:], ps(f"q{i}_{l}")[:], ACT.Square).then_inc(banks.drain(f"q{i}_{l}"), 1)
                banks.wait(act, f"kvc{l}")
                kvc = ps(f"kvc{l}")[:].rearrange("p (v t) -> p v t", v=2)
                act.activation(CX[0:64, :, 0], kvc[0:64], ACT.Copy)
                act.activation(CX[0:64, :, 1], kvc[64:128], ACT.Copy)
                act.activation(CX[64:128, :, 0, 0:240], kvc[0:64, :, 16:256], ACT.Copy)
                act.activation(CX[64:128, :, 1, 0:240], kvc[64:128, :, 16:256], ACT.Copy).then_inc(banks.drain(f"kvc{l}"), 1)
                for i in range(NT):
                    nm = f"kv{i}_{l}"
                    banks.wait(act, nm)
                    kv = ps(nm)[:].rearrange("p (b c d) -> p b c d", b=2, c=2)
                    if l:
                        banks.wait(act, f"ow1_{l - 1}")
                    act.activation(vv[:, i], kv[:, :, 1], ACT.Copy).then_inc(banks.drain(nm), 1)
                    act.wait_ge(sem["head_sum"], 7 * l + 2 + i)
                    act.activation(sq[:, 0:256].rearrange("p (b d) -> p b d", b=2), kv[:, :, 0], ACT.Square)\
                       .then_inc(banks.drain(nm), 1)
                banks.wait(act, f"gates{l}")
                act.activation(gates[:], ps(f"gates{l}")[:, 0:48].rearrange("p (i c) -> p i c", i=NT), ACT.Tanh, scale=0.5)\
                   .then_inc(banks.drain(f"gates{l}"), 1)
                for i in range(NT):
                    for g in range(2):
                        q_copy(l, f"qT{i}{g}_{l}", qT[0:HD, i, 4 * g:4 * g + 4])
                act.wait_ge(sem["cmp_w"], l + 1)
                act.activation(cmpx[:, 2], cmpx[:, 1], ACT.Tanh, scale=GELU_S).then_inc(sem["cmp_t"], 1)
                banks.wait(act, f"cmp2_{l}")
                act.wait_ge(sem["head_sum"], 7 * l + 4)
                act.activation(sq[0:NCMP, 0:128], ps(f"cmp2_{l}")[0:NCMP, 0:128], ACT.Square, scale=0.5)\
                   .then_inc(banks.drain(f"cmp2_{l}"), 1)
                act.wait_ge(sem["ys_w"], l + 1)
                act.activation(scr[:, 2], scr[:, 1], ACT.Tanh, scale=GELU_S).then_inc(sem["ys_t"], 1)
                for i in range(NT):
                    nm = f"glu{i}_{l}"
                    banks.wait(act, nm)
                    act.activation(scr[:, 3, 256 * i:256 * i + 256], ps(nm)[:, 256:512], ACT.Tanh, scale=0.25)\
                       .then_inc(banks.drain(nm), 1)
                act.wait_ge(sem["ln_centered"], l + 1)
                for i in range(NT):
                    if i:
                        act.wait_ge(sem["ln_sum"], 2 * l + i)
                    act.activation(scr[:, 3, 0:CW], lnb[:, i], ACT.Square, accum_out=st[:, c_ln(l) + i:c_ln(l) + i + 1])\
                       .then_inc(sem["ln_sum"], 1)
                act.wait_ge(sem["ln_gained"], l + 1)
                act.activation(lnb[:], ca[:], ACT.Tanh, scale=0.5).then_inc(sem["cv_t"], 1)
                banks.wait(act, f"cvW{l}")
                act.activation(xn[:, :, CW:2 * CW], ps(f"cvW{l}")[:].rearrange("p (i c) -> p i c", i=NT), ACT.Copy)\
                   .then_inc(banks.drain(f"cvW{l}"), 1)
                for i in range(NT):
                    nm = f"mkv{i}_{l}"
                    banks.wait(act, nm)
                    if l:
                        banks.wait(act, f"xo1_{l - 1}")
                    act.activation(vx[:, i], ps(nm)[:, 256:512], ACT.Copy).then_inc(banks.drain(nm), 1)
                    act.wait_ge(sem["kc_sum"], l + 1)
                    act.wait_ge(sem["head_sum"], 7 * l + 4 + i)
                    act.activation(sq[:, 0:256], ps(nm)[:, 0:256], ACT.Square).then_inc(banks.drain(nm), 1)
                for i in range(NT):
                    nk = P * (i + 1)
                    act.wait_ge(sem["c_centered"], 2 * l + i + 1)
                    act.activation(pc[:], pc[:], ACT.Exp).then_inc(sem["c_exp"], 1)
                    for g in range(2):
                        nm = f"pcT{i}{g}_{l}"
                        banks.wait(act, nm)
                        if l or i:
                            banks.wait(act, f"oc{1 - i}_{l + i - 1}")
                        act.activation(pcT[:, 4 * g:4 * g + 4], ps(nm)[0:NCMP].rearrange("p (h t) -> p h t", h=4), ACT.Copy)\
                           .then_inc(banks.drain(nm), 1)
                    for hh in range(NH + 1):
                        u = 20 * l + 8 * i + hh
                        if hh < NH:
                            act.wait_ge(sem["max_ready"], u + 1)
                            for b in range(2):
                                e = probs(u, b, scr[:, u % 2, b * nk:b * nk + nk], 1.0, sums[:, i, b, hh:hh + 1])
                            e.then_inc(sem["probs_ready"], 1)
                        if hh:
                            pt_copy(u - 1, f"pT{i}{hh - 1}_{l}", 2 * nk)
                for i in range(NT):
                    act.wait_ge(sem["y_ready"], 2 * l + i + 1)
                    if i:
                        act.wait_ge(sem["grp_sum"], 2 * l + i)
                    for n3, (c0, c1, f) in enumerate(((0, 256, 0.25), (256, 512, 0.5), (512, 1024, 1.0))):
                        k = act.activation(junk[:, c0:c1], xn[:, i, c0:c1], ACT.Square, scale=f,
                                           accum_out=st[:, c_grp(l, i) + n3:c_grp(l, i) + n3 + 1])
                    k.then_inc(sem["grp_sum"], 1)
                gained("y_T", G_OUT, l, (1, 3))
                n = NORM[f"cross{l}"]
                for i in range(NT):
                    squares(h[:, i], n, i, lambda: act.wait_ge(sem["h_added"], 12 * l + 2 + 2 * i))
                banks.wait(act, f"y_T3_{l}")
                scaled(xn[:, 1], h[:, 1], n)
                gained("cross_T", G_CROSS, l, (1, 3))
                banks.wait(act, f"xq{l}")
                act.wait_ge(sem["head_sum"], 7 * l + 6)
                act.activation(sq[:], ps(f"xq{l}")[:], ACT.Square).then_inc(banks.drain(f"xq{l}"), 1)
                for i in range(NT):
                    q_copy(l, f"xqT{i}_{l}", qT[64:128, i, 0:4])
                for k in range(5):
                    u = 20 * l + 16 + k
                    if k < 4:
                        i, hp = k // 2, k % 2
                        act.wait_ge(sem["max_ready"], u + 1)
                        banks.wait(act, f"xpT{k - 2}_{l}" if k >= 2 else f"pT1{NH - 2 + k}_{l}")
                        for b in range(2):
                            e = probs(u, b, ps(f"xs{k}_{l}")[:, 256 * b:256 * b + 256], SCALE,
                                      sums[:, i, 0, 2 * hp + b:2 * hp + b + 1])
                        e.then_inc(sem["probs_ready"], 1)
                    if k:
                        pt_copy(u - 1, f"xpT{k - 1}_{l}", 512)
                n = NORM[f"ffn{l}"]
                for i in range(NT):
                    squares(h[:, i], n, i, lambda: act.wait_ge(sem["h_added"], 12 * l + 6 + 2 * i))
                banks.wait(act, f"cross_T3_{l}")
                scaled(xn[:, 1], h[:, 1], n)
                gained("ffn_T", G_FFN, l, (1, 3))
                if l == 0:
                    for t in range(HT):
                        banks.wait(act, f"up{t}")
                        if t >= 2:
                            act.wait_ge(sem["gated"], t - 1)
                        act.activation(th[:, t % 2], ps(f"up{t}")[:, 0:256], ACT.Tanh, scale=0.5).then_inc(sem["tanh_up"], 1)
                    banks.wait(act, "xo1_0")
                    act.wait_ge(sem["gated"], HT)
                    s5_params(1)
                    s5_exps(1)
            act.wait_ge(sem["mem_gained"], L)
            load(cste, consts[:, C_MOE:C_END], "moe_consts_loaded")
            act.wait_ge(sem["r_centered"], 1)
            act.activation(ex, lg, ACT.Exp).then_inc(sem["r_exp"], 1)

            def expert(turn):
                for t in range(HT):
                    banks.wait(act, f"mup{t}", turn)
                    if t >= 2:
                        act.wait_ge(sem["e_gated"], turn * HT + (t - 1))
                    act.activation(th[:, t % 2, 0:CAP], ps(f"mup{t}")[:, 0:CAP], ACT.Tanh, scale=0.5)\
                       .then_inc(sem["e_tanh"], 1)
                for g in range(2):
                    banks.wait(act, f"mdown{g}", turn)
                    banks.wait(act, "sc3", turn - 1) if not isinstance(turn, int) and 0 else None
                    act.activation(ye[:, 512 * g:512 * g + 512], ps(f"mdown{g}")[0:CAP], ACT.Copy)\
                       .then_inc(banks.drain(f"mdown{g}"), 1)

            with act.Fori(0, E) as turn:
                expert(turn)
            act.wait_ge(sem["flag_ready"], 1)
            over = act.value_load(flag[0:1, 0:1], min_val=0, max_val=1)
            with act.If(over > 0):
                with act.Fori(E, PASSES * E) as turn:
                    expert(turn)

        @block.gpsimd
        def _(pool):
            n_own = [0]

            def own(i):
                n_own[0] += 1
                i.then_inc(sem["pool_step"], 1)
                pool.wait_ge(sem["pool_step"], n_own[0])

            def root(c, n, scale, name, parts=P):
                own(pool.tensor_scalar(rs[0:parts, c:c + n], st[0:parts, c:c + n], scale, EPS, ALU.mult, ALU.add))
                pool.tensor_tensor(rs[0:parts, c:c + n], rs[0:parts, c:c + n], cst[0:parts, C_NH:C_NH + 1].to_broadcast([parts, n]) if n > 16
                                   else cst[0:parts, C_NH:C_NH + n], ALU.pow).then_inc(sem[name], 1)

            own(pool.memset(tab[BUCKETS:BUCKETS + 1], NEG))
            pool.memset(cv[:], 0.0).then_inc(sem["pads_ready"], 1)
            pool.wait_ge(sem["par_loaded"], 16 * 4)
            sums_seen = [0]

            def norm(n):
                sums_seen[0] += 2
                pool.wait_ge(sem["norm_sum"], sums_seen[0])
                root(c_norm(n, 0), 2, 1.0 / D, "norm_rs")

            def turns(l):
                pool.wait_ge(sem["s5_unit"], l + 1)
                if l:
                    banks.wait(pool, "xo1_0")
                own(pool.memset(R[:, 0, :, 0:1], 1.0))
                own(pool.memset(R[:, 1, :, 0:1], 0.0))
                own(pool.tensor_copy(R[:, :, :, 1], wn[:, 0]))
                n, cur_w = 2, 0
                T = qT[:].rearrange("p a h t -> p (a h t)")
                while n < SEQ:
                    a, b = wn[:, cur_w], wn[:, 1 - cur_w]
                    own(pool.tensor_tensor(wt[:], a, a, ALU.mult))
                    own(pool.tensor_tensor(b[:, 0], wt[:, 0], wt[:, 1], ALU.subtract))
                    own(pool.tensor_tensor(wt[:, 0], a[:, 0], a[:, 1], ALU.mult))
                    own(pool.tensor_scalar(b[:, 1], wt[:, 0], 2.0, 0.0, ALU.mult, ALU.add))
                    cur_w = 1 - cur_w
                    for j in range(0, SJ, 4):
                        src = R[:, :, j:j + 4, 0:n]
                        T1 = T[:, 0:8 * n].rearrange("p (a j t) -> p a j t", a=2, j=4)
                        T2 = T[:, 1024:1024 + 8 * n].rearrange("p (a j t) -> p a j t", a=2, j=4)
                        for c in range(2):
                            w = [b[:, k, j:j + 4].rearrange("p (j o) -> p j o", o=1).to_broadcast([P, 4, n]) for k in range(2)]
                            pool.tensor_tensor(T1[:, c], src[:, c], w[0], ALU.mult)
                            own(pool.tensor_tensor(T2[:, c], src[:, c], w[1], ALU.mult))
                        own(pool.tensor_tensor(R[:, 0, j:j + 4, n:2 * n], T1[:, 0], T2[:, 1], ALU.subtract))
                        k = pool.tensor_tensor(R[:, 1, j:j + 4, n:2 * n], T1[:, 1], T2[:, 0], ALU.add)
                        own(k)
                    n *= 2
                pool.sem_inc(sem["angles_ready"], 1) if 0 else None
                pool.tensor_copy(wt[:], wt[:]).then_inc(sem["angles_ready"], 1)

            for l in range(L):
                norm(NORM[f"mix{l}"])
                if l == 0:
                    norm(1)
                    turns(0)
                for j in range(SJ):
                    g = SJ * l + j
                    z, xo = zz[:, j % 2], X[:, j % 2]
                    pool.wait_ge(sem["scanned"], g + 1)
                    if g:
                        pool.wait_ge(sem["states_ready"], g)
                    if j >= 2:
                        pool.wait_ge(sem["states_used"], g - 1)
                    T1, T2 = scr[:, 2].rearrange("p (a t) -> p a t", a=2), scr[:, 3].rearrange("p (a t) -> p a t", a=2)
                    for a in range(2):
                        pool.tensor_tensor(T1[:, a], z[:, a], R[:, 0, j], ALU.mult)
                        k = pool.tensor_tensor(T2[:, a], z[:, a], R[:, 1, j], ALU.mult)
                    own(k)
                    pool.tensor_tensor(xo[:, 0], T1[:, 0], T2[:, 1], ALU.subtract)
                    k = pool.tensor_tensor(xo[:, 1], T1[:, 1], T2[:, 0], ALU.add)
                    k.then_inc(sem["states_ready"], 1)
                    if j == 3:
                        for i in range(NT):
                            pool.wait_ge(sem["head_sum"], 7 * l + 1 + i)
                            pool.wait_ge(sem["head_sum"], 7 * l + 3 + i)
                            root(c_qk(l, i), 12, 1.0 / HD, "qk_rs")
                pool.wait_ge(sem["kc_sum"], l + 1)
                root(c_kc(l), 2, 1.0 / HD, "kc_rs", NCMP)
                pool.wait_ge(sem["ln_sum"], 2 * l + 2)
                root(c_ln(l), 2, 1.0 / CW, "ln_rs")
                for i in range(NT):
                    pool.wait_ge(sem["head_sum"], 7 * l + 5 + i)
                    root(c_xk(l, i), 4, 1.0 / HD, "xk_rs")
                for i in range(NT):
                    pool.wait_ge(sem["grp_sum"], 2 * l + i + 1)
                    c = c_grp(l, i)
                    own(pool.tensor_scalar(rs[:, c:c + 2], st[:, c:c + 2], 1.0 / CW, EPS, ALU.mult, ALU.add))
                    own(pool.tensor_scalar(rs[:, c + 2:c + 3], st[:, c + 2:c + 3], 1.0 / 512, EPS, ALU.mult, ALU.add))
                    pool.tensor_tensor(rs[:, c:c + 3], rs[:, c:c + 3], cst[:, C_NH:C_NH + 3], ALU.pow).then_inc(sem["grp_rs"], 1)
                norm(NORM[f"cross{l}"])
                pool.wait_ge(sem["head_sum"], 7 * l + 7)
                root(c_xq(l, 0), 8, 1.0 / HD, "xq_rs")
                norm(NORM[f"ffn{l}"])
                if l == 0:
                    turns(1)

        @block.vector
        def _(dve):
            n_own = [0]

            def own(i):
                n_own[0] += 1
                i.then_inc(sem["dve_step"], 1)
                dve.wait_ge(sem["dve_step"], n_own[0])

            def signal(s):
                dve.sem_inc(s, 1)

            def col(t, c):
                return t[:, c:c + 1]

            def spread(a, shape):
                return a.unsqueeze(len(a.shape)).to_broadcast(shape)

            def scaled(dst, src, n, wait):
                dve.wait_ge(sem["norm_rs"], n + 1)
                wait()
                dve.tensor_scalar(dst, src, col(rs, c_norm(n, 0)), None, ALU.mult).then_inc(sem["xn0_ready"], 1)

            def gained(name, base, l, groups):
                for g in groups:
                    nm = f"{name}{g}_{l}"
                    banks.wait(dve, nm)
                    dve.tensor_tensor(xT[:, 2 * g:2 * g + 2], ps(nm)[:].rearrange("p (k t) -> p k t", k=2),
                                      spread(gain(base, l, 2 * g, 2), [P, 2, SEQ]), ALU.mult).then_inc(banks.drain(nm), 1)

            def s5_weights(l):
                S = scr[:].rearrange("p a b -> p (a b)")
                t = [S[:, 136 * n:136 * n + 136] for n in range(15)]
                Xf = X[:].rearrange("p a b t -> p (a b t)")
                dve.wait_ge(sem["s5_loaded"], 16 * 8 * (l + 1))
                own(dve.tensor_copy(t[0][:, 0:8], par[:, 96 + 8 * l:104 + 8 * l]))
                own(dve.tensor_copy(t[1][:, 0:8], par[:, 112 + 8 * l:120 + 8 * l]))
                own(dve.tensor_copy(t[2][0:64, 0:8], ldt[0:64, 16 * l:16 * l + 16:2]))
                own(dve.tensor_copy(t[2][64:128, 0:8], ldt[64:128, 16 * l + 1:16 * l + 16:2]))
                dve.tensor_copy(t[2][:, 8:136].rearrange("p (a s) -> p a s", a=2),
                                spread(ldt[:, 32 + 2 * l:34 + 2 * l], [P, 2, 64])).then_inc(sem["s5_dt"], 1)
                lr, li, dt, mg = t[0], t[1], t[3], t[5]
                dve.wait_ge(sem["s5_act"], 4 * l + 1)
                dve.tensor_tensor(t[4], lr, dt, ALU.mult).then_inc(sem["s5_x1"], 1)
                own(dve.tensor_tensor(t[6], li, dt, ALU.mult))
                own(dve.tensor_scalar(t[7], t[6], 1 / (2 * math.pi), ROUND, ALU.mult, ALU.add))
                own(dve.tensor_scalar(t[8], t[7], -ROUND, None, ALU.add))
                own(dve.scalar_tensor_tensor(t[9], t[8], -TWO_PI_HI, t[6], ALU.mult, ALU.add))
                own(dve.scalar_tensor_tensor(t[10], t[8], -TWO_PI_LO, t[9], ALU.mult, ALU.add))
                dve.tensor_scalar(t[7], t[10], math.pi - 1e-6, -math.pi + 1e-6, ALU.min, ALU.max).then_inc(sem["s5_ang"], 1)
                dve.wait_ge(sem["s5_ang"], 2 * l + 1)
                own(dve.scalar_tensor_tensor(t[9], t[7], -1.0, t[7], ALU.mult, ALU.max))
                dve.tensor_scalar(t[10], t[9], -1.0, math.pi / 2, ALU.mult, ALU.add).then_inc(sem["s5_ang"], 1)
                sn, cs = t[8], t[11]
                own(dve.tensor_tensor(t[12], lr, lr, ALU.mult))
                own(dve.tensor_tensor(t[13], li, li, ALU.mult))
                own(dve.tensor_tensor(t[12], t[12], t[13], ALU.add))
                own(dve.reciprocal(t[12], t[12]))
                dve.wait_ge(sem["s5_act"], 4 * l + 4)
                if l:
                    dve.wait_ge(sem["angles_ready"], l)
                own(dve.tensor_copy(wn[:, 0, 0], cs[:, 0:8]))
                own(dve.tensor_copy(mag[:], mg[:, 0:8]))
                dve.tensor_copy(wn[:, 0, 1], sn[:, 0:8]).then_inc(sem["s5_unit"], 1)
                own(dve.tensor_tensor(t[9], mg, cs, ALU.mult))
                own(dve.tensor_tensor(t[6], mg, sn, ALU.mult))
                own(dve.tensor_scalar(t[9], t[9], -1.0, None, ALU.add))
                own(dve.tensor_tensor(t[4], t[9], lr, ALU.mult))
                own(dve.tensor_tensor(t[7], t[6], li, ALU.mult))
                own(dve.tensor_tensor(t[4], t[4], t[7], ALU.add))
                own(dve.tensor_tensor(t[4], t[4], t[12], ALU.mult))
                own(dve.tensor_tensor(t[7], t[6], lr, ALU.mult))
                own(dve.tensor_tensor(t[13], t[9], li, ALU.mult))
                own(dve.tensor_tensor(t[7], t[7], t[13], ALU.subtract))
                own(dve.tensor_tensor(t[7], t[7], t[12], ALU.mult))
                fr, fi = t[4][:, 8:136], t[7][:, 8:136]
                br, bi = Xf[:, 0:P], Xf[:, P:2 * P]
                o = [t[n][:, 8:136] for n in (0, 1, 2, 3)]
                own(dve.tensor_tensor(o[0], fr, br, ALU.mult))
                own(dve.tensor_tensor(o[1], fi, bi, ALU.mult))
                own(dve.tensor_tensor(o[2], fr, bi, ALU.mult))
                own(dve.tensor_tensor(o[3], fi, br, ALU.mult))
                own(dve.tensor_tensor(o[0], o[0], o[1], ALU.subtract))
                own(dve.tensor_tensor(o[2], o[2], o[3], ALU.add))
                m16 = cst[:, C_M16:C_M16 + 2]
                for c, b in enumerate((o[0], o[2])):
                    for a in range(2):
                        own(dve.tensor_tensor(BL[:, c, a], b[:, 64 * a:64 * a + 64].unsqueeze(1).to_broadcast([P, 2, 64]),
                                              spread(m16, [P, 2, 64]), ALU.mult))
                for c, s in ((0, 1.0), (1, -1.0)):
                    src = Xf[:, (2 + c) * P:(3 + c) * P].rearrange("p (j c) -> p j c", j=SJ)
                    for half in range(2):
                        k = dve.tensor_scalar(CL[:, c, :, 16 * half:16 * half + 16], src, col(cst, C_M64 + half), s, ALU.mult, ALU.mult)
                k.then_inc(sem["s5_weights"], 1)

            def s5(l, j):
                g = SJ * l + j
                nm = f"bu{j}_{l}"
                banks.wait(dve, nm)
                b = ps(nm)[:].rearrange("p (a t) -> p a t", a=2)
                T1, T2 = (scr[:, k].rearrange("p (a t) -> p a t", a=2) for k in range(2))
                if j == 0:
                    dve.wait_ge(sem["angles_ready"], l + 1)
                own(dve.tensor_tensor(T1, b, R[:, 0, j].unsqueeze(1).to_broadcast([P, 2, SEQ]), ALU.mult))
                dve.tensor_tensor(T2, b, R[:, 1, j].unsqueeze(1).to_broadcast([P, 2, SEQ]), ALU.mult).then_inc(banks.drain(nm), 1)
                dve.wait_ge(banks.drain(nm), banks.count(nm, None, False) + 1)
                if j >= 2:
                    dve.wait_ge(sem["states_ready"], g - 1)
                z = zz[:, j % 2]
                own(dve.tensor_tensor(z[:, 0], T1[:, 0], T2[:, 1], ALU.add))
                own(dve.tensor_tensor(z[:, 1], T1[:, 1], T2[:, 0], ALU.subtract))
                for a in range(2):
                    k = dve.tensor_tensor_scan(z[:, a], col(mag, j).to_broadcast([P, SEQ]), z[:, a], 0.0, ALU.mult, ALU.add)
                k.then_inc(sem["scanned"], 1)

            def head_sums(src, c, n, parts=P, name="head_sum"):
                dve.tensor_reduce(st[0:parts, c:c + n], src.rearrange("p (h d) -> p h d", h=n), AX, ALU.add).then_inc(sem[name], 1)

            def gelu_inner(dst, y):
                own(dve.tensor_tensor(dst, y, y, ALU.mult))
                own(dve.tensor_scalar(dst, dst, GELU_C, 1.0, ALU.mult, ALU.add))
                return dve.tensor_tensor(dst, dst, y, ALU.mult)

            for l in range(L):
                n = NORM[f"mix{l}"]
                if l:
                    scaled(xn[:, 0], h[:, 0], n, lambda: None)
                if l == 0:
                    banks.wait(dve, "t5")
                    dve.tensor_copy(hot[0:NH], ps("t5")[0:NH]).then_inc(banks.drain("t5"), 1)
                    dve.wait_ge(sem["x_loaded"], 16 * NT)
                    scaled(xn[:, 0], h[:, 0], n, lambda: None)
                    banks.wait(dve, "par")
                    own(dve.tensor_copy(par[:, P:252], ps("par")[:, P:252]))
                    own(dve.tensor_copy(par[0:HD, 252:264], ps("par")[0:HD, 252:264]))
                    dve.wait_ge(banks.drain("par"), 1)
                    for m in range(L):
                        for b in range(3):
                            own(dve.tensor_tensor(gk[:, m, b:b + 1], par[0:HD, 252 + m:253 + m],
                                                  par[0:HD, 254 + 3 * m + b:255 + 3 * m + b], ALU.mult))
                        own(dve.tensor_tensor(gk[:, m, 3:4], par[0:HD, 260 + m:261 + m], par[0:HD, 262 + m:263 + m], ALU.mult))
                    signal(sem["par_ready"])
                    signal(banks.drain("par"))
                gained("mix_T", G_MIX, l, (0, 2))
                if l == 0:
                    dve.wait_ge(sem["ldt_loaded"], 16 * 5)
                    s5_weights(0)
                banks.wait(dve, f"u{l}")
                dve.tensor_copy(uT[:], ps(f"u{l}")[:].rearrange("p (a t) -> p a t", a=2)).then_inc(banks.drain(f"u{l}"), 1)
                s5(l, 0)
                banks.wait(dve, f"ca{l}")
                dve.wait_ge(banks.drain(f"cg{l}"), banks.count(f"cg{l}", None, False) + 1)
                if l == 0:
                    dve.wait_ge(sem["pads_ready"], 1)
                dve.scalar_tensor_tensor(cv[:, :, CK - 1:], ca[:], 1.0, ps(f"ca{l}")[:].rearrange("p (a t) -> p a t", a=2),
                                         ALU.add, ALU.mult).then_inc(banks.drain(f"ca{l}"), 1)
                s5(l, 1)
                s5(l, 2)
                for i in range(NT):
                    dve.wait_ge(banks.drain(f"q{i}_{l}"), banks.count(f"q{i}_{l}", None, False) + 1)
                    head_sums(sq[:], c_qk(l, i), 8)
                s5(l, 3)
                for i in range(NT):
                    dve.wait_ge(banks.drain(f"kv{i}_{l}"), banks.count(f"kv{i}_{l}", None, False) + 2)
                    head_sums(sq[:, 0:256], c_qk(l, i) + 8, 4)
                s5(l, 4)
                s5(l, 5)
                for i in range(NT):
                    dve.wait_ge(sem["qk_rs"], 2 * l + i + 1)
                    c = c_qk(l, i)
                    dve.tensor_tensor(q_of[i].rearrange("p (h d) -> p h d", h=NH), ps(f"q{i}_{l}")[:].rearrange("p (h d) -> p h d", h=NH),
                                      spread(rs[:, c:c + 8], [P, NH, HD]), ALU.mult).then_inc(banks.drain(f"q{i}_{l}"), 1)
                    kv = ps(f"kv{i}_{l}")[:].rearrange("p (b c e d) -> p b c e d", b=2, c=2, e=2)
                    dve.tensor_tensor(kn[:, i].rearrange("p b (e d) -> p b e d", e=2), kv[:, :, 0],
                                      spread(rs[:, c + 8:c + 12].rearrange("p (b e) -> p b e", b=2), [P, 2, 2, HD]), ALU.mult)\
                       .then_inc(banks.drain(f"kv{i}_{l}"), 1)
                s5(l, 6)
                s5(l, 7)
                for k in range(KVH):
                    nm = f"kT{k}_{l}"
                    banks.wait(dve, nm)
                    for b in range(2):
                        e = dve.tensor_scalar(kT[0:HD, 2 * k + b], ps(nm)[0:HD, 256 * b:256 * b + 256], gk[:, l, 1 + b:2 + b], None, ALU.mult)
                    e.then_inc(banks.drain(nm), 1)
                nm = f"cmp1_{l}"
                banks.wait(dve, nm)
                own(dve.tensor_copy(cb[:], ps(nm)[0:HD, 64:66]))
                x1 = cmpx[:, 0].rearrange("p v h n -> p v (h n)")
                own(dve.tensor_tensor(x1, ps(nm)[0:HD, 0:60].rearrange("p (v n) -> p v n", v=2), spread(cb[:], [HD, 2, 30]), ALU.add))
                gelu_inner(cmpx[:, 1], cmpx[:, 0]).then_inc(sem["cmp_w"], 1)
                signal(banks.drain(nm))
                dve.wait_ge(sem["cmp_t"], l + 1)
                dve.scalar_tensor_tensor(cmpx[:, 3], cmpx[:, 2], 1.0, cmpx[:, 0], ALU.add, ALU.mult).then_inc(sem["cmp_g"], 1)
                nm = f"cmp2_{l}"
                banks.wait(dve, nm)
                dve.wait_ge(banks.drain(nm), banks.count(nm, None, False) + 1)
                head_sums(sq[0:NCMP, 0:128], c_kc(l), 2, NCMP, "kc_sum")
                own(dve.tensor_scalar(vc[:], ps(nm)[0:NCMP, 128:256].rearrange("p (h d) -> p h d", h=2), 0.5, None, ALU.mult))
                dve.wait_ge(sem["kc_rs"], l + 1)
                dve.scalar_tensor_tensor(kcn[:], ps(nm)[0:NCMP, 0:128].rearrange("p (h d) -> p h d", h=2), 0.5,
                                         spread(rs[0:NCMP, c_kc(l):c_kc(l) + 2], [NCMP, 2, HD]), ALU.mult, ALU.mult)\
                   .then_inc(banks.drain(nm), 1)
                nm = f"cmpT{l}"
                banks.wait(dve, nm)
                dve.tensor_scalar(kcT[:], ps(nm)[0:HD, 0:30].rearrange("p (h n) -> p h n", h=2), gk[:, l, 0:1], None, ALU.mult)\
                   .then_inc(banks.drain(nm), 1)
                nm = f"ys{l}"
                banks.wait(dve, nm)
                y = uT[:]
                for a in range(2):
                    e = dve.scalar_tensor_tensor(y[:, a], uT[:, a], col(par, G_D + 2 * l + a), ps(nm)[:, 256 * a:256 * a + 256],
                                                 ALU.mult, ALU.add)
                e.then_inc(banks.drain(nm), 1)
                dve.wait_ge(banks.drain(nm), banks.count(nm, None, False) + 1)
                w = scr[:, 1].rearrange("p (a t) -> p a t", a=2)
                gelu_inner(w, y).then_inc(sem["ys_w"], 1)
                dve.wait_ge(sem["ys_t"], l + 1)
                dve.scalar_tensor_tensor(scr[:, 0].rearrange("p (a t) -> p a t", a=2), scr[:, 2].rearrange("p (a t) -> p a t", a=2),
                                         1.0, y, ALU.add, ALU.mult).then_inc(sem["ys_g"], 1)
                for k in range(CK):
                    for a in range(2):
                        tap = par[:, P + (l * CK + k) * 2 + a:P + (l * CK + k) * 2 + a + 1]
                        if k == 0:
                            e = dve.tensor_scalar(ca[:, a], cv[:, a, 0:SEQ], tap, None, ALU.mult)
                        else:
                            e = dve.scalar_tensor_tensor(ca[:, a], cv[:, a, k:k + SEQ], tap, ca[:, a], ALU.mult, ALU.add)
                    own(e)
                for a in range(2):
                    e = dve.tensor_scalar(ca[:, a], ca[:, a], 0.5, col(par, G_CB + 2 * l + a), ALU.mult, ALU.add)
                e.then_inc(sem["conv_done"], 1)
                for i in range(NT):
                    nm = f"glu{i}_{l}"
                    dve.wait_ge(banks.drain(nm), banks.count(nm, None, False) + 1)
                    banks.wait(dve, f"qT11_{l}")
                    dve.scalar_tensor_tensor(xn[:, i, 0:CW], scr[:, 3, 256 * i:256 * i + 256], 1.0, ps(nm)[:, 0:256],
                                             ALU.add, ALU.mult).then_inc(banks.drain(nm), 1)
                nm = f"cvT{l}"
                banks.wait(dve, nm)
                pv = ps(nm)[:].rearrange("p (i c) -> p i c", i=NT)
                own(dve.tensor_reduce(rs[:, 140:142], pv, AX, ALU.add))
                own(dve.tensor_scalar(rs[:, 142:144], rs[:, 140:142], -1.0 / CW, None, ALU.mult))
                own(dve.tensor_tensor(lnb[:], pv, spread(rs[:, 142:144], [P, NT, CW]), ALU.add))
                signal(banks.drain(nm))
                signal(sem["ln_centered"])
                dve.wait_ge(sem["ln_rs"], l + 1)
                dve.tensor_tensor(lnb[:], lnb[:], spread(rs[:, c_ln(l):c_ln(l) + 2], [P, NT, CW]), ALU.mult).then_inc(sem["ln_scaled"], 1)
                nm = f"cvB{l}"
                banks.wait(dve, nm)
                for a in range(2):
                    own(dve.tensor_scalar(ca[:, a], ps(nm)[:, 256 * a:256 * a + 256], col(par, G_LG + 2 * l + a),
                                          col(par, G_LB + 2 * l + a), ALU.mult, ALU.add))
                signal(banks.drain(nm))
                signal(sem["ln_gained"])
                dve.wait_ge(sem["cv_t"], l + 1)
                dve.scalar_tensor_tensor(ca[:], lnb[:], 1.0, ca[:], ALU.add, ALU.mult).then_inc(sem["silu_ready"], 1)
                if l == 0:
                    dve.wait_ge(banks.drain("mem_T2_0"), banks.count("mem_T2_0", None, False) + 1)
                    dve.wait_ge(banks.drain("mem_T3_0"), banks.count("mem_T3_0", None, False) + 1)
                banks.wait(dve, f"gates{l}")
                dve.tensor_tensor(xT[:], memT[:], spread(gain(G_MEM, l, 0, KT), [P, KT, SEQ]), ALU.mult).then_inc(sem["mem_gained"], 1)
                for i in range(NT):
                    nm = f"mkv{i}_{l}"
                    dve.wait_ge(banks.drain(nm), banks.count(nm, None, False) + 2)
                    head_sums(sq[:, 0:256], c_xk(l, i), 4)
                for i in range(NT):
                    nm = f"mkv{i}_{l}"
                    dve.wait_ge(sem["xk_rs"], 2 * l + i + 1)
                    c = c_xk(l, i)
                    dve.tensor_tensor(kn[:, i].rearrange("p b (e d) -> p (b e) d", e=2), ps(nm)[:, 0:256].rearrange("p (h d) -> p h d", h=4),
                                      spread(rs[:, c:c + 4], [P, 4, HD]), ALU.mult).then_inc(banks.drain(nm), 1)
                for g in range(2):
                    nm = f"mkT{g}_{l}"
                    banks.wait(dve, nm)
                    dve.tensor_scalar(kT[64:128, 2 * g:2 * g + 2], ps(nm)[0:HD].rearrange("p (h t) -> p h t", h=2),
                                      gk[:, l, 3:4], None, ALU.mult).then_inc(banks.drain(nm), 1)
                for i in range(NT):
                    nk = P * (i + 1)
                    nm = f"sc_c{i}_{l}"
                    banks.wait(dve, nm)
                    if l or i:
                        banks.wait(dve, f"pcT{1 - i}1_{l + i - 1}")
                    if l == 0 and i == 0:
                        dve.wait_ge(sem["m_loaded"], 16)
                    lo = 128 * i + 224 - 16 * (NCMP - 1)
                    bias = M[:, :, lo:128 * i + 225:16][:, :, ::-1]
                    own(dve.scalar_tensor_tensor(pc[:], ps(nm)[:, 0:120].rearrange("p (h n) -> p h n", h=NH), SCALE, bias,
                                                 ALU.mult, ALU.add))
                    dve.tensor_reduce(mxc[:], pc[:], AX, ALU.max).then_inc(banks.drain(nm), 1)
                    dve.wait_ge(banks.drain(nm), banks.count(nm, None, False) + 1)
                    own(dve.tensor_scalar(mxc[:], mxc[:], -1e20, None, ALU.max))
                    dve.tensor_tensor(pc[:], pc[:], spread(mxc[:], [P, NH, NCMP]), ALU.subtract).then_inc(sem["c_centered"], 1)
                    dve.wait_ge(sem["c_exp"], 2 * l + i + 1)
                    own(dve.tensor_reduce(sumc[:, i, 0], pc[:], AX, ALU.add))
                    for hh in range(NH):
                        u = 20 * l + 8 * i + hh
                        nm = f"sc{i}{hh}_{l}"
                        banks.wait(dve, nm)
                        if u >= 2:
                            pv_name = transposed(u - 2)
                            banks.wait(dve, pv_name)
                        bias = M[:, hh, P:P * i + 256][:, ::-1].unsqueeze(1).to_broadcast([P, 2, nk])
                        S = scr[:, u % 2, 0:2 * nk].rearrange("p (b s) -> p b s", b=2)
                        dve.scalar_tensor_tensor(S, ps(nm)[:, 0:2 * nk].rearrange("p (b s) -> p b s", b=2), SCALE, bias,
                                                 ALU.mult, ALU.add).then_inc(banks.drain(nm), 1)
                        dve.wait_ge(banks.drain(nm), banks.count(nm, None, False) + 1)
                        dve.tensor_reduce(nmx[:, u % 2], S, AX, ALU.max, negate=True).then_inc(sem["max_ready"], 1)
                    own(dve.tensor_scalar(sumc[:, i, 0], sumc[:, i, 0], 1e-30, None, ALU.max))
                    dve.wait_ge(sem["probs_ready"], 20 * l + 8 * i + NH)
                    own(dve.tensor_copy(sumc[:, i, 1:3], sums[:, i]))
                    own(dve.reciprocal(sumc[:, i], sumc[:, i]))
                    own(dve.tensor_scalar(sq[:, 0:24], gates[:, i], 1.0, 0.5, ALU.add, ALU.mult))
                    own(dve.tensor_tensor(sumc[:, i], sumc[:, i], sq[:, 0:24].rearrange("p (h b) -> p b h", b=3), ALU.mult))
                    Y = xn[:, i, 512:1024].rearrange("p (h d) -> p h d", h=NH)
                    tmp = sq[:].rearrange("p (h d) -> p h d", h=NH)
                    for b, nm in enumerate((f"oc{i}_{l}", f"os{i}_{l}", f"ow{i}_{l}")):
                        banks.wait(dve, nm)
                        o = ps(nm)[:].rearrange("p (h d) -> p h d", h=NH)
                        dve.tensor_tensor(tmp if b else Y, o, spread(sumc[:, i, b], [P, NH, HD]), ALU.mult).then_inc(banks.drain(nm), 1)
                        dve.wait_ge(banks.drain(nm), banks.count(nm, None, False) + 1)
                        if b == 1:
                            own(dve.tensor_tensor(Y, Y, tmp, ALU.add))
                        if b == 2:
                            dve.tensor_tensor(Y, Y, tmp, ALU.add).then_inc(sem["y_ready"], 1)
                for i in range(NT):
                    dve.wait_ge(sem["grp_rs"], 2 * l + i + 1)
                    for n3, (c0, c1, f) in enumerate(((0, 256, 0.25), (256, 512, 0.5), (512, 1024, 1.0))):
                        e = dve.tensor_scalar(xn[:, i, c0:c1], xn[:, i, c0:c1], col(rs, c_grp(l, i) + n3), f, ALU.mult, ALU.mult)
                    e.then_inc(sem["y_scaled"], 1)
                gained("y_T", G_OUT, l, (0, 2))

                def add_in(name):
                    for i in range(NT):
                        for m in range(2):
                            nm = f"{name}{2 * i + m}_{l}" if name != "down" else f"down{2 * i + m}"
                            banks.wait(dve, nm)
                            dst = h[:, i, 512 * m:512 * m + 512]
                            dve.tensor_tensor(dst, dst, ps(nm)[:], ALU.add).then_inc(sem["h_added"], 1)

                add_in("out")
                n = NORM[f"cross{l}"]
                scaled(xn[:, 0], h[:, 0], n, lambda: banks.wait(dve, f"y_T3_{l}"))
                gained("cross_T", G_CROSS, l, (0, 2))
                dve.wait_ge(banks.drain(f"xq{l}"), banks.count(f"xq{l}", None, False) + 1)
                head_sums(sq[:], c_xq(l, 0), 8)
                dve.wait_ge(sem["xq_rs"], l + 1)
                dve.tensor_tensor(kn[:].rearrange("p i b (e d) -> p (i b e) d", e=2), ps(f"xq{l}")[:].rearrange("p (h d) -> p h d", h=8),
                                  spread(rs[:, c_xq(l, 0):c_xq(l, 0) + 8], [P, 8, HD]), ALU.mult).then_inc(banks.drain(f"xq{l}"), 1)
                for k in range(4):
                    u = 20 * l + 16 + k
                    banks.wait(dve, f"xs{k}_{l}")
                    dve.wait_ge(sem["probs_ready"], u - 1)
                    own(dve.tensor_reduce(nmx[:, u % 2], ps(f"xs{k}_{l}")[:].rearrange("p (b s) -> p b s", b=2), AX, ALU.max, negate=True))
                    dve.tensor_scalar(nmx[:, u % 2], nmx[:, u % 2], SCALE, None, ALU.mult).then_inc(sem["max_ready"], 1)
                for i in range(NT):
                    dve.wait_ge(sem["probs_ready"], 20 * l + 18 + 2 * i)
                    own(dve.reciprocal(sumc[:, i, 0, 0:4], sums[:, i, 0, 0:4]))
                    nm = f"xo{i}_{l}"
                    banks.wait(dve, nm)
                    dve.tensor_tensor(kn[:, i].rearrange("p b (e d) -> p (b e) d", e=2), ps(nm)[:, 0:256].rearrange("p (h d) -> p h d", h=4),
                                      spread(sumc[:, i, 0, 0:4], [P, 4, HD]), ALU.mult).then_inc(banks.drain(nm), 1)
                nm = f"xoT{l}"
                banks.wait(dve, nm)
                dve.tensor_copy(uT[:], ps(nm)[:].rearrange("p (a t) -> p a t", a=2)).then_inc(banks.drain(nm), 1)
                add_in("xout")
                n = NORM[f"ffn{l}"]
                scaled(xn[:, 0], h[:, 0], n, lambda: banks.wait(dve, f"cross_T3_{l}"))
                gained("ffn_T", G_FFN, l, (0, 2))
                if l == 0:
                    for t in range(HT):
                        up = ps(f"up{t}")
                        dve.wait_ge(sem["tanh_up"], t + 1)
                        if t >= 2:
                            dve.wait_ge(sem["gated"], t - 1)
                        own(dve.scalar_tensor_tensor(hT[:, 2 + t % 2], th[:, t % 2], 1.0, up[:, 0:256], ALU.add, ALU.mult))
                        dve.scalar_tensor_tensor(hT[:, t % 2], hT[:, 2 + t % 2], 0.5, up[:, 256:512], ALU.mult, ALU.mult).then_inc(sem["gated"], 1)
                    add_in("down")
                    s5_weights(1)
            banks.wait(dve, "router")
            dve.wait_ge(sem["moe_consts_loaded"], 16)
            own(dve.tensor_copy(lg, ps("router")[:, 0:16].rearrange("p (i e) -> p i e", i=NT)))
            of_j = lg.unsqueeze(2).to_broadcast([P, NT, E, E])
            of_e = lg.unsqueeze(3).to_broadcast([P, NT, E, E])
            own(dve.tensor_tensor(cmpj, of_j, of_e, ALU.is_gt))
            own(dve.tensor_tensor(cmpe, of_j, of_e, ALU.is_equal))
            lower = cste[:, C_LT - C_MOE:C_LT - C_MOE + 64].rearrange("p (e j) -> p e j", e=E).unsqueeze(1).to_broadcast([P, NT, E, E])
            own(dve.tensor_tensor(cmpe, cmpe, lower, ALU.mult))
            own(dve.tensor_tensor(cmpj, cmpj, cmpe, ALU.add))
            own(dve.tensor_reduce(rk, cmpj, AX, ALU.add))
            dve.tensor_scalar(sel, rk, TOPK - 0.5, None, ALU.is_lt).then_inc(sem["selected"], 1)
            own(dve.tensor_reduce(mx2[:, 0:2], lg, AX, ALU.max))
            dve.tensor_tensor(lg, lg, spread(mx2[:, 0:2], [P, NT, E]), ALU.subtract).then_inc(sem["r_centered"], 1)
            dve.wait_ge(sem["r_exp"], 1)
            dve.wait_ge(sem["selected"], 1)
            own(dve.tensor_tensor(ex, ex, sel, ALU.mult))
            own(dve.tensor_reduce(gsum[:, 0:2], ex, AX, ALU.add))
            own(dve.reciprocal(gsum[:, 0:2], gsum[:, 0:2]))
            own(dve.tensor_tensor(ex, ex, spread(gsum[:, 0:2], [P, NT, E]), ALU.mult))
            banks.wait(dve, "count")
            own(dve.tensor_scalar(pos, sel, -1e4, 1e4, ALU.mult, ALU.add))
            own(dve.tensor_tensor(pos, pos, ps("count")[:, 0:16].rearrange("p (i e) -> p i e", i=NT), ALU.add))
            own(dve.memset(table, 0.0))
            for i in range(NT):
                own(dve.tensor_tensor(table[:, 0:24, i].rearrange("p (q e) -> p q e", e=E), pos[:, i].unsqueeze(1).to_broadcast([P, PASSES, E]),
                                      cste[:, C_PASS - C_MOE:C_PASS - C_MOE + 24].rearrange("p (q e) -> p q e", e=E), ALU.subtract))
                own(dve.tensor_copy(table[:, 0:24, 2 + i].rearrange("p (q e) -> p q e", e=E), ex[:, i].unsqueeze(1).to_broadcast([P, PASSES, E])))
            own(dve.tensor_reduce(mx2[:, 2:3], ps("count")[:, 16:24], AX, ALU.max))
            own(dve.tensor_scalar(flag[:, 0:1], mx2[0:1, 2:3], CAP + 0.5, None, ALU.is_gt))
            signal(banks.drain("count"))
            signal(banks.drain("router"))
            signal(sem["flag_ready"])

            def pick(e, wait_to):
                dve.tensor_copy(cur, table[:, bass.ds(e, 1)].rearrange("p o k -> p (o k)")).then_inc(sem["e_step"], 1)
                wait_to(1)
                for i in range(NT):
                    dve.tensor_scalar(one[:, i], cste[:, C_IOTA - C_MOE:C_IOTA - C_MOE + CAP], cur[:, i:i + 1], None, ALU.is_equal)
                    k = dve.tensor_scalar(og[:, i], cste[:, C_IOTA - C_MOE:C_IOTA - C_MOE + CAP], cur[:, i:i + 1], cur[:, 2 + i:3 + i],
                                          ALU.is_equal, ALU.mult)
                k.then_inc(sem["picked"], 1)

            def gather_in(name, turn=None):
                for g in range(2):
                    nm = f"{name}gather{g}"
                    banks.wait(dve, nm, turn)
                    dve.tensor_tensor(xg[:, 4 * g:4 * g + 4], ps(nm)[:, 0:4 * CAP].rearrange("p (k c) -> p k c", k=4),
                                      spread(gain(G_FFN, 1, 4 * g, 4), [P, 4, CAP]), ALU.mult).then_inc(banks.drain(nm), 1)

            def gates_in(name, turn=None):
                nm = f"{name}gateT"
                banks.wait(dve, nm, turn)
                dve.tensor_copy(ogT, ps(nm)[0:CAP, 0:256]).then_inc(banks.drain(nm), 1)

            E_STEPS = 1 + HT

            pick(0, lambda k: dve.wait_ge(sem["e_step"], 1))
            gather_in("")
            gates_in("")

            def expert(turn):
                base = turn * E_STEPS + 1
                for t in range(HT):
                    up = ps(f"mup{t}")
                    dve.wait_ge(sem["e_tanh"], turn * HT + (t + 1))
                    if t >= 2:
                        dve.wait_ge(sem["e_gated"], turn * HT + (t - 1))
                    dve.scalar_tensor_tensor(hT[:, 2 + t % 2, 0:CAP], th[:, t % 2, 0:CAP], 1.0, up[:, 0:CAP], ALU.add, ALU.mult)\
                       .then_inc(sem["e_step"], 1)
                    dve.wait_ge(sem["e_step"], base + (t + 1))
                    dve.scalar_tensor_tensor(hT[:, t % 2, 0:CAP], hT[:, 2 + t % 2, 0:CAP], 0.5, up[:, CAP:2 * CAP], ALU.mult, ALU.mult)\
                       .then_inc(sem["e_gated"], 1)
                pick(turn + 1, lambda k: dve.wait_ge(sem["e_step"], base + E_STEPS))
                gather_in("n", turn)
                for g in range(4):
                    banks.wait(dve, f"sc{g}", turn)
                    dst = h[:, g // 2, 512 * (g % 2):512 * (g % 2) + 512]
                    dve.tensor_tensor(dst, dst, ps(f"sc{g}")[:], ALU.add).then_inc(banks.drain(f"sc{g}"), 1)
                gates_in("n", turn)

            with dve.Fori(0, E) as turn:
                expert(turn)
            over = dve.value_load(flag[0:1, 0:1], min_val=0, max_val=1)
            with dve.If(over > 0):
                with dve.Fori(E, PASSES * E) as turn:
                    expert(turn)
            dve.tensor_copy(flag[:, 1:2], flag[:, 0:1]).then_inc(sem["h_final"], 1)

        @block.tensor
        def _(pe):
            def done(name, i):
                i.then_inc(banks.fill(name), 1)

            def product(out_ap, pairs):
                n = len(pairs)
                for k, (a, b) in enumerate(pairs):
                    i = pe.matmul(out_ap, a, b, start=(k == 0), stop=(k == n - 1))
                return i

            def turn_tiles(name, l, src, wait):
                for g in range(4):
                    nm = f"{name}{g}_{l}"
                    banks.open(pe, nm)
                    for k in range(2):
                        for i in range(NT):
                            if g == 0 and k == 0:
                                wait(i)
                            e = pe.transpose(ps(nm)[:, 256 * k + P * i:256 * k + P * i + P],
                                             src[:, i, P * (2 * g + k):P * (2 * g + k) + P], ident)
                            if name == "mix_T" and l == 1 and g == k == i == 0:
                                e.then_inc(slot_free[FF_SLOTS[-1]], 1)
                    done(nm, e)

            def wait_norm(n):
                def w(i):
                    pe.wait_ge(sem[f"xn{i}_ready"], max(n, 1))
                return w

            def wait_xT(name, l):
                for g in (2, 3):
                    nm = f"{name}{g}_{l}"
                    pe.wait_ge(banks.drain(nm), banks.count(nm, None, False) + 1)

            def drained(nm, k=1):
                pe.wait_ge(banks.drain(nm), banks.count(nm, None, False) + k)

            pe.wait_ge(sem["par_loaded"], 16 * 4)
            banks.open(pe, "par")
            pe.transpose(pb[0][:, 0:P], raw, ident)
            pe.transpose(pb[0][:, P:P + 124], raw2[0:124], ident[0:124, 0:124])
            done("par", pe.transpose(pb[0][0:HD, 252:264], raw3, ident[0:12, 0:12]))
            pe.wait_ge(sem["t5_loaded"], 32)
            pe.wait_ge(sem["pads_ready"], 1)
            banks.open(pe, "t5")
            done("t5", pe.matmul(pb[1][0:NH, 0:512], tab[:], hot[:], start=True, stop=True))

            for l in range(L):
                win = [ring[:, c, 0:4096].rearrange("p (k n) -> p k n", k=KT) for c in range(4)]
                wgate = ring[:, 3, 4096:4288].rearrange("p (k n) -> p k n", k=KT)
                m = small(l)

                def feature_major(nm, w, cols):
                    banks.open(pe, nm)
                    for a, c in enumerate(cols):
                        e = product(ps(nm)[:, 256 * a:256 * a + 256], [(w[:, k, c:c + P], xT[:, k]) for k in range(KT)])
                    done(nm, e)

                def tokens(out_ap, i, w, c0, c1):
                    return product(out_ap, [(xT[:, k, P * i:P * i + P], w[:, k, c0:c1]) for k in range(KT)])

                def bu(j):
                    nm = f"bu{j}_{l}"
                    if j == 0:
                        drained(f"u{l}")
                        pe.wait_ge(sem["s5_weights"], l + 1)
                    banks.open(pe, nm)
                    r = slice(32 * (j % 4), 32 * (j % 4) + 32)
                    for c in range(2):
                        e = pe.matmul(ps(nm)[:, 256 * c:256 * c + 256], BL[r, c, j // 4].rearrange("p a s -> p (a s)"), uT[r, j // 4],
                                      start=True, stop=True)
                    done(nm, e)

                def ys(j):
                    nm = f"ys{l}"
                    if j == 0:
                        banks.open(pe, nm)
                    pe.wait_ge(sem["states_ready"], SJ * l + j + 1)
                    r = slice(32 * (j % 4), 32 * (j % 4) + 32)
                    o = ps(nm)[r, 256 * (j // 4):256 * (j // 4) + 256]
                    for c in range(2):
                        e = pe.matmul(o, CL[:, c, j], X[:, j % 2, c], start=(c == 0), stop=(c == 1),
                                      tile_position=(0, 32 * (j % 4)))
                    e.then_inc(sem["states_used"] if j < SJ - 1 else banks.fill(nm), 1)

                turn_tiles("mix_T", l, xn, wait_norm(NORM[f"mix{l}"]))
                if l == 0:
                    def wait_mem(i):
                        pe.wait_ge(sem["memx_ready"], i + 1)
                wait_xT("mix_T", l)
                weights_in(pe, f"in0_{l}")
                feature_major(f"u{l}", win[0], (0, 128))
                if l == 0:
                    turn_tiles("mem_T", 0, memx, wait_mem)
                feature_major(f"ca{l}", win[0], (256, 384))
                weights_in(pe, f"in1_{l}")
                feature_major(f"cg{l}", win[1], (0, 128))
                bu(0)
                bu(1)
                for i in range(NT):
                    nm = f"q{i}_{l}"
                    banks.open(pe, nm)
                    tokens(ps(nm)[:, 0:256], i, win[1], 256, 512)
                weights_in(pe, f"in2_{l}")
                for i in range(NT):
                    nm = f"q{i}_{l}"
                    done(nm, tokens(ps(nm)[:, 256:512], i, win[2], 0, 256))
                bu(2)
                feature_major(f"kvc{l}", win[2], (256, 384))
                bu(3)
                weights_in(pe, f"in3_{l}")
                for i in range(NT):
                    nm = f"kv{i}_{l}"
                    banks.open(pe, nm)
                    done(nm, tokens(ps(nm)[:], i, win[3], 0, 512))
                nm = f"gates{l}"
                banks.open(pe, nm)
                for i in range(NT):
                    e = tokens(ps(nm)[:, 24 * i:24 * i + 24], i, wgate, 0, 24)
                done(nm, e)
                for j in range(4, SJ):
                    ys(j - 4)
                    bu(j)
                for i in range(NT):
                    drained(f"q{i}_{l}", 2)
                    for g in range(2):
                        nm = f"qT{i}{g}_{l}"
                        banks.open(pe, nm)
                        for c in range(4):
                            e = pe.transpose(ps(nm)[0:HD, P * c:P * c + P], q_of[i][:, HD * (4 * g + c):HD * (4 * g + c) + HD], ident)
                        done(nm, e)
                for i in range(NT):
                    drained(f"kv{i}_{l}", 3)
                for k in range(KVH):
                    nm = f"kT{k}_{l}"
                    banks.open(pe, nm)
                    for b in range(2):
                        for i in range(NT):
                            e = pe.transpose(ps(nm)[0:HD, 256 * b + P * i:256 * b + P * i + P], kn[:, i, b, HD * k:HD * k + HD], ident)
                    done(nm, e)
                weights_in(pe, f"small_{l}")
                drained(f"kvc{l}")
                nm = f"cmp1_{l}"
                banks.open(pe, nm)
                for v in range(2):
                    product(ps(nm)[0:HD, 30 * v:30 * v + 30].rearrange("p (a n) -> p a n", a=2),
                            [(m["w1"][:, v, t], CX[:, v, :, t:t + 225:STRIDE]) for t in range(16)])
                for v in range(2):
                    e = product(ps(nm)[0:HD, 64 + v:65 + v], [(m["w1"][:, v, t], m["pe"][:, v, t:t + 1]) for t in range(16)])
                done(nm, e)
                for j in range(4, SJ):
                    ys(j)
                nm = f"cmp2_{l}"
                banks.open(pe, nm)
                pe.wait_ge(sem["cmp_g"], l + 1)
                for v in range(2):
                    for a in range(KVH):
                        e = pe.matmul(ps(nm)[0:NCMP, P * v + HD * a:P * v + HD * a + HD], cmpx[:, 3, v, a], m["w2"][:, v], start=True, stop=True)
                done(nm, e)
                nm = f"cmpT{l}"
                banks.open(pe, nm)
                drained(f"cmp2_{l}", 2)
                for a in range(KVH):
                    e = pe.transpose(ps(nm)[0:HD, NCMP * a:NCMP * a + NCMP], kcn[:, a], ident[0:NCMP, 0:NCMP])
                done(nm, e)
                pe.wait_ge(sem["ys_g"], l + 1)
                g2 = scr[:, 0].rearrange("p (a t) -> p a t", a=2)
                for i in range(NT):
                    nm = f"glu{i}_{l}"
                    banks.open(pe, nm)
                    done(nm, product(ps(nm)[:], [(g2[:, a, P * i:P * i + P], m["glu"][:, a]) for a in range(2)]))
                nm = f"cvT{l}"
                banks.open(pe, nm)
                pe.wait_ge(sem["conv_done"], l + 1)
                for i in range(NT):
                    for a in range(2):
                        e = pe.transpose(ps(nm)[:, 256 * i + P * a:256 * i + P * a + P], ca[:, a, P * i:P * i + P], ident)
                done(nm, e)
                nm = f"cvB{l}"
                banks.open(pe, nm)
                pe.wait_ge(sem["ln_scaled"], l + 1)
                for a in range(2):
                    for i in range(NT):
                        e = pe.transpose(ps(nm)[:, 256 * a + P * i:256 * a + P * i + P], lnb[:, i, P * a:P * a + P], ident)
                done(nm, e)
                nm = f"cvW{l}"
                banks.open(pe, nm)
                pe.wait_ge(sem["silu_ready"], l + 1)
                for i in range(NT):
                    e = product(ps(nm)[:, 256 * i:256 * i + 256], [(ca[:, a, P * i:P * i + P], m["pw"][:, a]) for a in range(2)])
                done(nm, e)
                weights_in(pe, f"x_{l}")
                wkv = ring[:, 1, 0:4096].rearrange("p (k n) -> p k n", k=KT)
                wq = ring[:, 1, 4096:6144].rearrange("p (k n) -> p k n", k=KT)
                pe.wait_ge(sem["mem_gained"], l + 1)
                for i in range(NT):
                    nm = f"mkv{i}_{l}"
                    banks.open(pe, nm)
                    done(nm, tokens(ps(nm)[:], i, wkv, 0, 512))
                for i in range(NT):
                    drained(f"mkv{i}_{l}", 3)
                for g in range(2):
                    nm = f"mkT{g}_{l}"
                    banks.open(pe, nm)
                    knx = kn[:].rearrange("p i b (e d) -> p i (b e) d", e=2)
                    for a in range(2):
                        for i in range(NT):
                            e = pe.transpose(ps(nm)[0:HD, 256 * a + P * i:256 * a + P * i + P], knx[:, i, 2 * g + a], ident)
                    done(nm, e)
                for i in range(NT):
                    nk = P * (i + 1)
                    nm = f"sc_c{i}_{l}"
                    banks.open(pe, nm)
                    drained(f"cmpT{l}")
                    drained(f"qT11_{l}")
                    drained(f"kT1_{l}")
                    for hh in range(NH):
                        e = pe.matmul(ps(nm)[:, NCMP * hh:NCMP * hh + NCMP], qT[0:HD, i, hh], kcT[:, hh // 4], start=True, stop=True)
                    done(nm, e)

                    def scores(hh):
                        nm = f"sc{i}{hh}_{l}"
                        banks.open(pe, nm)
                        kv = hh // 4
                        done(nm, pe.matmul(ps(nm)[:, 0:2 * nk].rearrange("p (b s) -> p b s", b=2), qT[0:HD, i, hh],
                                           kT[0:HD, 2 * kv:2 * kv + 2, 0:nk], start=True, stop=True))

                    def values(hh):
                        u = 20 * l + 8 * i + hh
                        drained(f"pT{i}{hh}_{l}")
                        for b, nm in enumerate((f"os{i}_{l}", f"ow{i}_{l}")):
                            if hh == 0:
                                banks.open(pe, nm)
                            kv = hh // 4
                            pt = scr[:, 2 + u % 2, 0:2 * nk].rearrange("p (b s t) -> p b s t", b=2, s=i + 1)
                            e = product(ps(nm)[:, HD * hh:HD * hh + HD],
                                        [(pt[:, b, s], vv[:, s, b, HD * kv:HD * kv + HD]) for s in range(i + 1)])
                            if hh == NH - 1 and b == 0:
                                done(nm, e)
                        if hh < NH - 1:
                            e.then_inc(sem["pv_done"], 1)
                        else:
                            done(nm, e)
                            pe.transpose(ps(f"pT{i}{hh}_{l}")[0:1, 0:1], ident[0:1, 0:1], ident[0:1, 0:1]).then_inc(sem["pv_done"], 1)

                    scores(0)
                    scores(1)
                    pe.wait_ge(sem["c_exp"], 2 * l + i + 1)
                    for g in range(2):
                        nm = f"pcT{i}{g}_{l}"
                        banks.open(pe, nm)
                        for c in range(4):
                            e = pe.transpose(ps(nm)[0:NCMP, P * c:P * c + P], pc[:, 4 * g + c], ident)
                        done(nm, e)
                    nm = f"oc{i}_{l}"
                    banks.open(pe, nm)
                    drained(f"pcT{i}0_{l}")
                    drained(f"pcT{i}1_{l}")
                    for hh in range(NH):
                        e = pe.matmul(ps(nm)[:, HD * hh:HD * hh + HD], pcT[:, hh], vc[:, hh // 4], start=True, stop=True)
                    done(nm, e)
                    for hh in range(NH):
                        u = 20 * l + 8 * i + hh
                        nm = f"pT{i}{hh}_{l}"
                        pe.wait_ge(sem["probs_ready"], u + 1)
                        banks.open(pe, nm)
                        for c in range(2 * (i + 1)):
                            e = pe.transpose(ps(nm)[:, P * c:P * c + P], scr[:, u % 2, P * c:P * c + P], ident)
                        done(nm, e)
                        if hh + 2 < NH:
                            scores(hh + 2)
                        if hh:
                            values(hh - 1)
                    values(NH - 1)
                def wait_y(i):
                    pe.wait_ge(sem["y_scaled"], 2 * l + i + 1)
                turn_tiles("y_T", l, xn, wait_y)
                wait_xT("y_T", l)
                for i in range(NT):
                    for n in range(2):
                        nm = f"out{2 * i + n}_{l}"
                        if i == 0:
                            weights_in(pe, f"out{n}_{l}")
                        banks.open(pe, nm)
                        done(nm, tokens(ps(nm)[:], i, ring[:, 2 + n, 0:4096].rearrange("p (k n) -> p k n", k=KT), 0, 512))
                turn_tiles("cross_T", l, xn, wait_norm(NORM[f"cross{l}"]))
                wait_xT("cross_T", l)
                nm = f"xq{l}"
                banks.open(pe, nm)
                for i in range(NT):
                    e = tokens(ps(nm)[:, 256 * i:256 * i + 256], i, wq, 0, 256)
                done(nm, e)
                drained(nm, 2)
                for i in range(NT):
                    nm = f"xqT{i}_{l}"
                    banks.open(pe, nm)
                    for c in range(XH):
                        e = pe.transpose(ps(nm)[0:HD, P * c:P * c + P], kn[:, i].rearrange("p b t -> p (b t)")[:, HD * c:HD * c + HD], ident)
                    done(nm, e)

                def xscores(k):
                    i, hp = k // 2, k % 2
                    nm = f"xs{k}_{l}"
                    banks.open(pe, nm)
                    drained(f"xqT{i}_{l}")
                    for a in range(2):
                        e = pe.matmul(ps(nm)[:, 256 * a:256 * a + 256], qT[64:128, i, 2 * hp + a], kT[64:128, 2 * hp + a],
                                      start=True, stop=True)
                    done(nm, e)

                def xvalues(k):
                    i, hp = k // 2, k % 2
                    u = 20 * l + 16 + k
                    drained(f"xpT{k}_{l}")
                    nm = f"xo{i}_{l}"
                    if hp == 0:
                        banks.open(pe, nm)
                    pt = scr[:, 2 + u % 2].rearrange("p (a s t) -> p a s t", a=2, s=2)
                    for a in range(2):
                        c = 2 * hp + a
                        e = product(ps(nm)[:, HD * c:HD * c + HD], [(pt[:, a, s], vx[:, s, HD * c:HD * c + HD]) for s in range(NT)])
                    if hp:
                        done(nm, e)
                        pe.transpose(ps(f"xpT{k}_{l}")[0:1, 0:1], ident[0:1, 0:1], ident[0:1, 0:1]).then_inc(sem["pv_done"], 1)
                    else:
                        e.then_inc(sem["pv_done"], 1)

                drained(f"mkT1_{l}")
                xscores(0)
                xscores(1)
                for k in range(4):
                    u = 20 * l + 16 + k
                    nm = f"xpT{k}_{l}"
                    pe.wait_ge(sem["probs_ready"], u + 1)
                    banks.open(pe, nm)
                    for c in range(4):
                        e = pe.transpose(ps(nm)[:, P * c:P * c + P], scr[:, u % 2, P * c:P * c + P], ident)
                    done(nm, e)
                    if k + 2 < 4:
                        xscores(k + 2)
                    if k:
                        xvalues(k - 1)
                xvalues(3)
                nm = f"xoT{l}"
                banks.open(pe, nm)
                for i in range(NT):
                    drained(f"xo{i}_{l}")
                for a in range(2):
                    for i in range(NT):
                        e = pe.transpose(ps(nm)[:, 256 * a + P * i:256 * a + P * i + P],
                                         kn[:, i].rearrange("p b t -> p (b t)")[:, P * a:P * a + P], ident)
                done(nm, e)
                drained(nm)
                for i in range(NT):
                    for n in range(2):
                        nm = f"xout{2 * i + n}_{l}"
                        banks.open(pe, nm)
                        done(nm, product(ps(nm)[:], [(uT[:, a, P * i:P * i + P], m["xo"][:, a, 512 * n:512 * n + 512]) for a in range(2)]))
                turn_tiles("ffn_T", l, xn, wait_norm(NORM[f"ffn{l}"]))
                wait_xT("ffn_T", l)

                def up_products(name, c, mt, rhs, width, turn=None):
                    w = ring[:, FF_SLOTS[c], 0:UPW].rearrange("p (k g n) -> p k g n", k=KT, g=2)
                    t = 2 * c + mt
                    banks.open(pe, f"{name}{t}", turn)
                    for g in range(2):
                        e = product(ps(f"{name}{t}")[:, width * g:width * g + width],
                                    [(w[:, k, g, P * mt:P * mt + P], rhs[:, k]) for k in range(KT)])
                    done(f"{name}{t}", e)

                if l == 0:
                    def down_products(t):
                        c, mt = t // 2, t % 2
                        w = ring[:, FF_SLOTS[c], UPW:].rearrange("p (m n) -> p m n", m=2)
                        pe.wait_ge(sem["gated"], t + 1)
                        for g in range(4):
                            if t == 0:
                                banks.open(pe, f"down{g}")
                            e = pe.matmul(pb[4 + g][:], hT[:, t % 2, P * (g // 2):P * (g // 2) + P],
                                          w[:, mt, 512 * (g % 2):512 * (g % 2) + 512], start=(t == 0), stop=(t == HT - 1))
                            if t == HT - 1:
                                done(f"down{g}", e)
                        if mt and t < HT - 1:
                            e.then_inc(slot_free[FF_SLOTS[c]], 1)

                    for t in range(HT):
                        if t % 2 == 0:
                            weights_in(pe, f"ff{t // 2}")
                        up_products("up", t // 2, t % 2, xT, SEQ)
                        if t:
                            down_products(t - 1)
                    down_products(HT - 1)
            nm = "router"
            banks.open(pe, nm)
            pe.wait_ge(sem["router_loaded"], 16)
            for i in range(NT):
                e = tokens(ps(nm)[:, 8 * i:8 * i + 8], i, rt, 0, 8)
            done(nm, e)
            nm = "count"
            banks.open(pe, nm)
            pe.wait_ge(sem["selected"], 1)
            before, ones = cste[:, C_TRI - C_MOE:C_TRI - C_MOE + P], cste[:, C_ONE - C_MOE:C_ONE - C_MOE + P]
            product(ps(nm)[:, 0:8], [(before, sel[:, 0])])
            product(ps(nm)[:, 8:16], [(before, sel[:, 1]), (ones, sel[:, 0])])
            done(nm, product(ps(nm)[:, 16:24], [(ones, sel[:, 0]), (ones, sel[:, 1])]))

            def gather(name, turn=None):
                for g in range(2):
                    nm = f"{name}gather{g}"
                    banks.open(pe, nm, turn)
                    for k in range(4):
                        e = product(ps(nm)[:, CAP * k:CAP * k + CAP],
                                    [(xn[:, i, P * (4 * g + k):P * (4 * g + k) + P], one[:, i]) for i in range(NT)])
                    done(nm, e)

            def gate_tiles(name, turn=None, free=None):
                nm = f"{name}gateT"
                banks.open(pe, nm, turn)
                for i in range(NT):
                    e = pe.transpose(ps(nm)[0:CAP, P * i:P * i + P], og[:, i], ident)
                    if i == 0 and free is not None:
                        e.then_inc(free, 1)
                done(nm, e)

            pe.wait_ge(sem["picked"], 1)
            gather("")
            gate_tiles("")

            def expert(turn):
                def down(t):
                    c, mt = t // 2, t % 2
                    w = ring[:, FF_SLOTS[c], UPW:].rearrange("p (m n) -> p m n", m=2)
                    pe.wait_ge(sem["e_gated"], turn * HT + (t + 1))
                    for g in range(2):
                        if t == 0:
                            banks.open(pe, f"mdown{g}", turn)
                        e = pe.matmul(pb[4 + g][0:CAP], hT[:, t % 2, 0:CAP], w[:, mt, 512 * g:512 * g + 512],
                                      start=(t == 0), stop=(t == HT - 1))
                        if t == HT - 1:
                            done(f"mdown{g}", e)
                    if mt and t < HT - 1:
                        e.then_inc(slot_free[FF_SLOTS[c]], 1)

                pe.wait_ge(banks.drain("gather1"), turn * 3 + (gathered + 1))
                for t in range(HT):
                    if t % 2 == 0:
                        expert_in(pe, turn, t // 2)
                    up_products("mup", t // 2, t % 2, xg, CAP, turn)
                    if t:
                        down(t - 1)
                pe.wait_ge(sem["picked"], turn + 2)
                gather("n", turn)
                down(HT - 1)
                gate_tiles("n", turn, slot_free[FF_SLOTS[-1]])
                for g in range(4):
                    nm = f"sc{g}"
                    banks.open(pe, nm, turn)
                    if g < 2:
                        pe.wait_ge(banks.drain(f"mdown{g}"), banks.count(f"mdown{g}", turn, False) + 1)
                    done(nm, pe.matmul(ps(nm)[:], ogT[:, P * (g // 2):P * (g // 2) + P], ye[:, 512 * (g % 2):512 * (g % 2) + 512],
                                       start=True, stop=True))

            gathered = banks.count("gather1", None, False)
            with pe.Fori(0, E) as turn:
                expert(turn)
            pe.wait_ge(sem["flag_ready"], 1)
            over = pe.value_load(flag[0:1, 0:1], min_val=0, max_val=1)
            with pe.If(over > 0):
                with pe.Fori(E, PASSES * E) as turn:
                    expert(turn)


def kernel(x, mem, norm_mix, w_in, ssm_lambda_re, ssm_lambda_im, ssm_log_dt, ssm_b_re, ssm_b_im, ssm_c_re, ssm_c_im,
           ssm_d, ssm_w_glu, conv_w_dw, conv_b_dw, conv_ln_g, conv_ln_b, conv_w_pw, nsa_q_norm, nsa_k_norm,
           nsa_cmp_pe, nsa_cmp_w1, nsa_cmp_w2, mix_out_norm, w_out, t5_table, norm_cross, norm_mem, x_w_q, x_w_kv,
           x_q_norm, x_k_norm, x_w_o, norm_ffn, ffn_w_up, ffn_w_down, moe_router, moe_w_up, moe_w_down):
    import concourse.bacc as bacc
    from concourse.bass_utils import run_bass_kernel_spmd

    consts, hot = shape_constants()
    rows = (L, G * GH, GP)
    arrays = dict(
        x=x[0], mem=mem[0], w_in=w_in, w_glu=ssm_w_glu, w_pw=conv_w_pw, cmp_w1=nsa_cmp_w1, cmp_w2=nsa_cmp_w2,
        w_out=w_out, t5_table=t5_table, x_w_q=x_w_q, x_w_kv=x_w_kv, x_w_o=x_w_o, ffn_up=ffn_w_up, ffn_down=ffn_w_down,
        router=moe_router[0], moe_up=moe_w_up[0], moe_down=moe_w_down[0],
        rows128=np.concatenate([a.reshape(-1, P) for a in (
            norm_mix, norm_cross, norm_ffn, norm_mem, mix_out_norm, conv_b_dw, conv_ln_g, conv_ln_b, ssm_d,
            ssm_lambda_re, ssm_lambda_im)]),
        rows64=np.concatenate([a.reshape(-1, HD) for a in (nsa_q_norm, nsa_k_norm, x_q_norm, x_k_norm)]),
        lam_re=ssm_lambda_re.reshape(L, G * GP), lam_im=ssm_lambda_im.reshape(L, G * GP), log_dt=ssm_log_dt, conv_w=conv_w_dw,
        b_re=ssm_b_re.transpose(0, 1, 3, 2).reshape(rows), b_im=ssm_b_im.transpose(0, 1, 3, 2).reshape(rows),
        c_re=ssm_c_re.transpose(0, 1, 3, 2).reshape(L, G * GP, GH), c_im=ssm_c_im.transpose(0, 1, 3, 2).reshape(L, G * GP, GH),
        cmp_pe=nsa_cmp_pe.reshape(L, 2, 2, 16, HD).transpose(0, 1, 2, 4, 3).reshape(L, 2, P, 16),
        consts=consts, t5_hot=hot)
    arrays = {k: np.ascontiguousarray(v) for k, v in arrays.items()}
    nc = bacc.Bacc("TRN2", target_bir_lowering=False, num_devices=1)
    args = {k: nc.dram_tensor(f"{k}_dram", list(v.shape), F32, kind="ExternalInput").ap() for k, v in arrays.items()}
    bias_rows = nc.dram_tensor("bias_rows_dram", [NH, 512], F32, kind="Internal").ap()
    out = nc.dram_tensor("out_dram", [SEQ, D], F32, kind="ExternalOutput").ap()
    trunk(nc, **args, bias_rows=bias_rows, out=out)
    r = run_bass_kernel_spmd(nc, [{f"{k}_dram": v for k, v in arrays.items()}], core_ids=[0])
    return np.asarray(r.results[0]["out_dram"]).reshape(1, SEQ, D)
```

```python
from contextlib import ExitStack
import math

import numpy as np

import concourse.bass as bass
from concourse import mybir

F32 = mybir.dt.float32
BF16 = mybir.dt.bfloat16
I32 = mybir.dt.int32
ALU = mybir.AluOpType
ACT = mybir.ActivationFunctionType
AX = mybir.AxisListType.X

P = 128
D, SEQ, L = 1024, 256, 2
KT, NT = D // P, SEQ // P
HD, NH, KVH = 64, 8, 2
XH = 4
G, GP, GH = 16, 64, 16
SJ = G * GP // P
CK, CW = 31, 256
NCMP, STRIDE, LCMP = 15, 16, 32
BUCKETS, MAXD = 32, 128
PROJ = 2072
FF, E, TOPK = 2816, 8, 2
HT = FF // P
CH = HT // 2
CAP = 96
PASSES = -(-SEQ // CAP)
EPS = 1e-6
NEG = -1e30
SCALE = HD ** -0.5
SLOTS = 4
S5_FIRST = [3, 1]
UPW, DNW = KT * 2 * 256, 2 * D
FF_SLOTS = [2, 3, 1, 0, 2, 3, 1, 0, 2, 3, 1]
C_SCORES, C_EXPS, C_TURN, C_VALUES = (1, 10), (2, 11), (3, 12), (5, 14)
CONV_TURN, CONV_GAIN, CONV_TANH, CONV_SILU, CONV_OUT, CONV_COPY = 6, 7, 7, 8, 9, 10
COMBINE, Y_SQUARES, Y_SCALE = 9, 11, 14
GELU_C, GELU_S = 0.044715, math.sqrt(2 / math.pi)
TWO_PI_HI = 6.28125
TWO_PI_LO = 2 * math.pi - TWO_PI_HI
ROUND, ROUND_12 = 1.5 * 2 ** 23, 1.5 * 2 ** 11
FX = 384

C_ID, C_M16, C_M64, C_NH, C_T, C_Q = 0, 128, 130, 132, 148, 148 + SEQ
C_TRI = C_Q + 1
C_ONE, C_IOTA = C_TRI + P, C_TRI + 2 * P
C_LT = C_IOTA + CAP
C_PASS = C_LT + E * E
C_MOE, C_END = C_TRI, C_PASS + PASSES * E


def shape_constants():
    c = np.zeros((P, C_END), np.float32)
    p = np.arange(P)
    c[:, C_ID:C_ID + P] = np.eye(P)
    c[:, C_TRI:C_TRI + P] = p[:, None] < p[None, :]
    c[:, C_ONE:C_ONE + P] = 1.0
    c[:, C_M16:C_M16 + 2] = (p[:, None] // GH) % 2 == np.arange(2)
    c[:, C_M64:C_M64 + 2] = p[:, None] // GP == np.arange(2)
    c[:, C_IOTA:C_IOTA + CAP] = np.arange(CAP)
    c[:, C_LT:C_LT + 64] = (np.arange(8)[None, :] < np.arange(8)[:, None]).reshape(64)
    c[:, C_PASS:C_END] = np.repeat(np.arange(PASSES) * CAP, E)
    c[:, C_NH:C_NH + 16] = -0.5
    c[:, C_T:C_T + SEQ] = np.arange(SEQ)
    c[:, C_Q] = math.pi / 2
    j = np.arange(512)
    n = np.maximum(j - 255, 0)
    nf = np.maximum(n, 1).astype(np.float32)
    large = 16 + (np.log(nf / np.float32(16)) / np.float32(math.log(MAXD / 16)) * np.float32(16)).astype(np.int32)
    b = np.where(n < 16, n, np.minimum(large, BUCKETS - 1))
    hot = np.zeros((BUCKETS + 1, 512), np.float32)
    hot[b, j] = 1.0
    hot[:, j < 255] = 0.0
    hot[BUCKETS, j < 255] = 1.0
    return c, hot


class Sems:

    def __init__(self, nc, ctx):
        self.nc, self.ctx, self.made = nc, ctx, {}

    def __getitem__(self, name):
        if name not in self.made:
            self.made[name] = self.ctx.enter_context(self.nc.semaphore(name))
        return self.made[name]


class Banks:

    def __init__(self, sems):
        self.filled = [sems[f"bank{b}_filled"] for b in range(8)]
        self.drained = [sems[f"bank{b}_drained"] for b in range(8)]
        self.at, self.fills, self.drains = {}, [0] * 8, [0] * 8
        self.opened = [0] * 8
        self.loop = None

    def add(self, name, bank, readers=1):
        assert name not in self.at, name
        self.at[name] = (bank, self.fills[bank], self.drains[bank], self.loop)
        self.fills[bank] += 1
        self.drains[bank] += readers

    def begin_loop(self):
        self.loop = {"fills": list(self.fills), "drains": list(self.drains)}

    def end_loop(self):
        a = self.loop
        a["per_f"] = [x - y for x, y in zip(self.fills, a["fills"])]
        a["per_d"] = [x - y for x, y in zip(self.drains, a["drains"])]
        self.loop = None

    def bank(self, name):
        return self.at[name][0]

    def count(self, name, turn, filled):
        bank, f, d, loop = self.at[name]
        n = f + 1 if filled else d
        if loop is None or turn is None:
            return n
        per = (loop["per_f"] if filled else loop["per_d"])[bank]
        return n + turn * per if per else n

    def open(self, pe, name, turn=None):
        bank, f, _, loop = self.at[name]
        if turn is None or loop is None:
            assert self.opened[bank] == f, name
            self.opened[bank] += 1
        n = self.count(name, turn, False)
        if not (isinstance(n, int) and n == 0):
            pe.wait_ge(self.drained[self.bank(name)], n)

    def wait(self, eng, name, turn=None):
        eng.wait_ge(self.filled[self.bank(name)], self.count(name, turn, True))

    def fill(self, name):
        return self.filled[self.bank(name)]

    def drain(self, name):
        return self.drained[self.bank(name)]


def plan_banks(banks):
    add = banks.add
    add("par", 0, 2)
    add("t5", 1)
    for l in range(L):
        def a(name, bank, readers=1):
            add(f"{name}{l}", bank, readers)
        for g in range(4):
            a(f"mix_T{g}_", g % 2)
        if l == 0:
            for g in range(4):
                a(f"mem_T{g}_", 6 + g % 2)
        a("u", 2); a("ca", 6); a("cg", 7)
        for j in range(SJ):
            a(f"bu{j}_", 3 + j % 2)
        a("ys", 2)
        a("q0_", 5, 2); a("q1_", 0, 2); a("kvc", 1); a("kv0_", 6, 3); a("kv1_", 7, 3); a("gates", 1)
        a("cmp1_", 1)
        a("qT00_", 5); a("qT01_", 0); a("qT10_", 5); a("qT11_", 0)
        a("kT0_", 6); a("kT1_", 7)
        a("glu0_", 3, 2); a("glu1_", 4, 2)
        a("cmp2_", 0, 2)
        a("mkv0_", 6, 3)
        a("cmpT", 1)
        a("cvT", 2)
        for i in range(NT):
            for hh in range(NH):
                a(f"sc{i}{hh}_", hh % 2)
                a(f"pT{i}{hh}_", 6 + hh % 2)
        a("sc_c0_", 3); a("pcT00_", 2); a("pcT01_", 3); a("oc0_", 3)
        a("cvB", 2); a("cvW", 2)
        a("sc_c1_", 3); a("pcT10_", 2); a("pcT11_", 3); a("oc1_", 3)
        for i in range(NT):
            a(f"os{i}_", 4); a(f"ow{i}_", 5)
        a("mkv1_", 7, 3)
        for g in range(4):
            a(f"y_T{g}_", g % 2)
        for g in range(4):
            a(f"out{g}_", 2 + g, 0)
        a("mkT0_", 6); a("mkT1_", 7)
        for g in range(4):
            a(f"cross_T{g}_", g % 2)
        a("xq", 2, 2); a("xqT0_", 3); a("xqT1_", 4)
        for u in range(4):
            a(f"xs{u}_", 6 + u % 2, 0)
            a(f"xpT{u}_", u % 2)
        a("xo0_", 2); a("xo1_", 5); a("xoT", 3)
        for g in range(4):
            a(f"xout{g}_", 4 + g, 0)
        for g in range(4):
            a(f"ffn_T{g}_", g % 2)
        if l == 0:
            for t in range(HT):
                add(f"up{t}", t % 4, 0)
            for g in range(4):
                add(f"down{g}", 4 + g, 0)
        else:
            add("router", 2)
            add("count", 3)
            add("gather0", 6); add("gather1", 7); add("gateT", 2)
            banks.begin_loop()
            for t in range(HT):
                add(f"mup{t}", t % 4, 0)
            for g in range(2):
                add(f"mdown{g}", 4 + g)
            add("ngather0", 6); add("ngather1", 7); add("ngateT", 2)
            add("sc0", 6); add("sc1", 7); add("sc2", 6); add("sc3", 7)

            banks.end_loop()


def trunk(nc, x, mem, w_in, w_glu, w_pw, cmp_w1, cmp_w2, w_out, t5_table, x_w_q, x_w_kv, x_w_o,
          ffn_up, ffn_down, router, moe_up, moe_down, rows128, rows64, lam_re, lam_im, log_dt, conv_w,
          b_re, b_im, c_re, c_im, cmp_pe, consts, t5_hot, bias_rows, out):
    with ExitStack() as ctx:
        sem = Sems(nc, ctx)
        banks = Banks(sem)
        plan_banks(banks)
        slot_full = [sem[f"slot{s}_full"] for s in range(SLOTS)]
        slot_free = [sem[f"slot{s}_free"] for s in range(SLOTS)]

        def sb(name, shape, dt=F32):
            return ctx.enter_context(nc.sbuf_tensor(name, shape, dt))

        pb = [ctx.enter_context(nc.psum_tensor(f"bank{b}", [P, 512], F32)) for b in range(8)]

        def ps(name):
            return pb[banks.bank(name)]

        h = sb("h", [P, NT, D])
        xn = sb("xn", [P, NT, D])
        xT = sb("xT", [P, KT, SEQ])
        memT = sb("memT", [P, KT, SEQ])
        ring = sb("ring", [P, SLOTS, UPW + DNW])
        cst = sb("cst", [P, C_MOE])
        tab = sb("tab", [BUCKETS + 1, NH])
        M = sb("M", [P, NH, FX])
        par = sb("par", [P, 264])
        gk = sb("gk", [HD, L, 4])
        qT = sb("qT", [P, NT, NH, P])
        kT = sb("kT", [P, 4, SEQ])
        kn = sb("kn", [P, NT, 2, P])
        vv = sb("vv", [P, NT, 2, P])
        gates = sb("gates", [P, NT, 24])
        kcT = sb("kcT", [HD, KVH, NCMP])
        kcn = sb("kcn", [NCMP, KVH, HD])
        vc = sb("vc", [NCMP, KVH, HD])
        cmpx = sb("cmpx", [HD, 4, 2, KVH, NCMP])
        cb = sb("cb", [HD, 2])
        uT = sb("uT", [P, 2, SEQ])
        cv = sb("cv", [P, 2, CK - 1 + SEQ])
        ca = sb("ca", [P, 2, SEQ])
        R = sb("R", [P, 2, SJ, SEQ])
        zz = sb("zz", [P, 2, 2, SEQ])
        X = sb("X", [P, 2, 2, SEQ])
        BL = sb("BL", [P, 2, 2, 2, GP])
        CL = sb("CL", [P, 2, SJ, 32])
        mag = sb("mag", [P, SJ])
        turn_step = sb("turn_step", [P, 2, SJ])
        ldt = sb("ldt", [P, 36])
        scr = sb("scr", [P, 4, 512])
        pc = sb("pc", [P, NH, NCMP])
        sq = sb("sq", [P, 512])
        st = sb("st", [P, 160])
        rs = sb("rs", [P, 160])
        nmx = sb("nmx", [P, 2, 2])
        sums = sb("sums", [P, NT, 2, NH])
        sumc = sb("sumc", [P, NT, 3, NH])
        mxc = sb("mxc", [P, NH])
        rt = sb("rt", [P, KT, E])
        hT = zz[:].rearrange("p a b t -> p (a b) t")
        th = X[:, 1]
        junk = ca[:].rearrange("p a t -> p (a t)").bitcast(BF16)
        vx = X[:, 0]
        pcT = zz[0:NCMP].rearrange("p a b t -> p (a b t)").rearrange("p (h t) -> p h t", h=NH)
        lnb = R[:, 0, 0:2]
        memg = R[:, 1]
        cste = memT[:].rearrange("p k t -> p (k t)")[:, 0:C_END - C_MOE]
        Rf = R[:].rearrange("p a j t -> p (a j t)")
        xg = Rf[:, 0:KT * CAP].rearrange("p (k c) -> p k c", k=KT)
        ye = Rf[0:CAP, 768:1792]
        one = Rf[:, 1792:1792 + NT * CAP].rearrange("p (i c) -> p i c", i=NT)
        og = Rf[:, 1984:1984 + NT * CAP].rearrange("p (i c) -> p i c", i=NT)
        ogT = Rf[0:CAP, 2176:2432]
        table = Rf[:, 3072:3072 + 4 * (PASSES * E + 1)].rearrange("p (e k) -> p e k", k=4)
        cur = Rf[:, 2532:2536]
        lg = Rf[:, 2560:2576].rearrange("p (i e) -> p i e", i=NT)
        cmpj = Rf[:, 2576:2704].rearrange("p (i e j) -> p i e j", i=NT, e=E)
        cmpe = Rf[:, 2704:2832].rearrange("p (i e j) -> p i e j", i=NT, e=E)
        rk = Rf[:, 2832:2848].rearrange("p (i e) -> p i e", i=NT)
        sel = Rf[:, 2848:2864].rearrange("p (i e) -> p i e", i=NT)
        ex = Rf[:, 2864:2880].rearrange("p (i e) -> p i e", i=NT)
        mx2 = Rf[:, 2880:2884]
        pos = Rf[:, 2896:2912].rearrange("p (i e) -> p i e", i=NT)
        gsum = Rf[:, 2912:2916]
        flag = sb("flag", [1, 4], I32)

        ident = cst[:, C_ID:C_ID + P]
        raw = ring[:, 3, 0:P]
        hot = ring[0:BUCKETS + 1, 3, 512:1024]
        raw2 = ring[:, 3, P:2 * P]
        raw3 = ring[0:12, 3, 2 * P:2 * P + HD]
        memx = ring[:, 2, 0:NT * D].rearrange("p (i d) -> p i d", i=NT)
        q_of = [xn[:, i, 0:512] for i in range(NT)]
        CX = xn[:, :, 512:1024].rearrange("p kv (a t) -> p kv a t", a=KVH)

        def c_norm(n, i): return 2 * n + i
        def c_qk(l, i): return 16 + 24 * l + 12 * i
        def c_ln(l): return 64 + 2 * l
        def c_kc(l): return 68 + 2 * l
        def c_grp(l, i): return 72 + 6 * l + 3 * i
        def c_xk(l, i): return 84 + 8 * l + 4 * i
        def c_xq(l, i): return 100 + 8 * l + 4 * i
        NORM = {"mix0": 0, "mem": 1, "cross0": 2, "ffn0": 3, "mix1": 4, "cross1": 5, "ffn1": 6}
        G_MIX, G_CROSS, G_FFN, G_MEM, G_OUT, G_CB, G_LG, G_LB, G_D = 0, 16, 32, 48, 64, 80, 84, 88, 92

        def gain(base, l, k0, n):
            return par[:, base + KT * l + k0:base + KT * l + k0 + n]

        def small(l):
            s = ring[:, 0]
            return dict(w1=s[:, 0:2048].rearrange("p (v t o) -> p v t o", v=2, t=16),
                        glu=s[:, 2048:3072].rearrange("p (a n) -> p a n", a=2),
                        pw=s[:, 3072:3584].rearrange("p (a n) -> p a n", a=2),
                        xo=s[:, 3584:5632].rearrange("p (k n) -> p k n", k=2),
                        w2=s[0:HD, 5632:5760].rearrange("p (v o) -> p v o", v=2),
                        pe=s[:, 5760:5792].rearrange("p (v t) -> p v t", v=2))

        fill_of, counts = {}, [0] * SLOTS
        loads = {}
        for l in range(L):
            for n, c in enumerate(["in0", "in1", "in2", "in3", "small", "x", "out0", "out1"]):
                loads[c] = {"in3": 2, "small": 13, "x": 2}.get(c, 1)
                counts[n % 4] += 1
                fill_of[f"{c}_{l}"] = (n % 4, counts[n % 4])
            for c in range(CH if l == 0 else 0):
                s = FF_SLOTS[c]
                counts[s] += 1
                fill_of[f"ff{c}"] = (s, counts[s])
        full_before, k_full = {}, [0] * SLOTS
        for name, (s, n) in fill_of.items():
            k_full[s] += 16 * loads.get(name.rsplit("_", 1)[0], 3)
            full_before[name] = k_full[s]
        LOOP_FULL = list(k_full)
        LAST_USE = {"in0": "ca", "in1": "q1_", "in2": "kvc", "in3": "gates", "small": "xout3_", "x": "xq",
                    "out0": "out2_", "out1": "out3_"}
        USES = [FF_SLOTS.count(s) for s in range(SLOTS)]
        nth = [FF_SLOTS[:c].count(FF_SLOTS[c]) for c in range(CH)]

        def weights_in(eng, name):
            s, _ = fill_of[name]
            eng.wait_ge(slot_full[s], full_before[name])

        def expert_in(eng, turn, c):
            s = FF_SLOTS[c]
            eng.wait_ge(slot_full[s], turn * (48 * USES[s]) + (LOOP_FULL[s] + 48 * (nth[c] + 1)))

        dma_out = sem["out_written"]

        def transposed(u):
            l, k = divmod(u, 20)
            return f"pT{k // 8}{k % 8}_{l}" if k < 16 else f"xpT{k - 16}_{l}"
        block = ctx.enter_context(nc.Block())

        def load_by(eng):
            def load(dst, src, name):
                eng.dma_start(dst, src, allow_slow_non_contiguous=True).then_inc(sem[name], 16)
            return load

        def s5_params(load, l):
            for a in range(2):
                for t, lam in ((0, lam_re), (1, lam_im)):
                    load(scr[:].rearrange("p a b -> p (a b)")[:, 136 * t + 8 + 64 * a:136 * t + 72 + 64 * a],
                         bass.AP(tensor=lam.tensor, offset=l * 1024 + 512 * a, ap=[[64, 8], [0, GH], [1, 64]]), "s5_loaded")
            Xf = X[:].rearrange("p a b t -> p (a b t)")
            for n, b in enumerate((b_re, b_im)):
                load(Xf[:, n * P:(n + 1) * P].rearrange("p (a s) -> p a s", a=2),
                     b[l].rearrange("(a c) s -> c a s", a=2), "s5_loaded")
            for n, c in enumerate((c_re, c_im)):
                load(Xf[:, (2 + n) * P:(3 + n) * P].rearrange("p (j c) -> p j c", j=SJ),
                     c[l].rearrange("(j s) c -> s j c", j=SJ), "s5_loaded")

        @block.sync
        def _(sp):
            for i in range(NT):
                sp.dma_start(h[:, i], x[i * P:(i + 1) * P]).then_inc(sem["x_loaded"], 16)

            load = load_by(sp)
            s5_params(load, 0)
            load(ldt[:, 0:32], bass.AP(tensor=log_dt.tensor, offset=0, ap=[[0, P], [1, L * G]]), "ldt_loaded")
            for l in range(L):
                for a in range(2):
                    load(ldt[:, 32 + 2 * l + a:33 + 2 * l + a],
                         bass.AP(tensor=log_dt.tensor, offset=l * G + 8 * a, ap=[[1, 8], [0, GH], [1, 1]]), "ldt_loaded")

            def slot_is_free(name):
                s, n = fill_of[name]
                before = [k for k, v in fill_of.items() if v == (s, n - 1)]
                if not before:
                    return
                if before[0].startswith("ff"):
                    c = int(before[0][2:])
                    sp.wait_ge(slot_free[s], nth[c] + 1)
                else:
                    banks.wait(sp, LAST_USE[before[0][:-2]] + before[0][-1])

            def item(name, parts):
                s, n = fill_of[name]
                assert len(parts) == loads.get(name.rsplit("_", 1)[0], 3), name
                slot_is_free(name)
                for dst, src in parts:
                    sp.dma_start(dst, src).then_inc(slot_full[s], 16)

            def wide(w, c0, n):
                return w[:, c0:c0 + n].rearrange("(k p) n -> p k n", p=P)

            for l in range(L):
                for c in range(4):
                    if l == 0 and c == 2:
                        banks.wait(sp, "mem_T3_0")
                    if l == 0 and c == 3:
                        banks.wait(sp, "par")
                        sp.wait_ge(sem["m_stored"], 16)
                    parts = [(ring[:, c, 0:4096].rearrange("p (k n) -> p k n", k=KT), wide(w_in[l], 512 * c, 512))]
                    if c == 3:
                        parts.append((ring[:, 3, 4096:4288].rearrange("p (k n) -> p k n", k=KT), wide(w_in[l], 2048, 24)))
                    item(f"in{c}_{l}", parts)
                    if l == 0 and c == 0:
                        load(memx, mem.rearrange("(i p) d -> p i d", p=P), "mem_loaded")
                if l == 0:
                    load(rt[:], router.rearrange("(k p) e -> p k e", p=P), "router_loaded")
                m = small(l)
                parts = []
                for v in range(2):
                    w1 = cmp_w1[l, v].rearrange("(a t d) o -> a d t o", a=2, t=16)
                    for a in range(2):
                        parts.append((m["w1"][64 * a:64 * a + 64, v], w1[a]))
                for a in range(2):
                    parts.append((m["glu"][:, a], w_glu[l, a * P:(a + 1) * P]))
                    parts.append((m["pw"][:, a], w_pw[l, a * P:(a + 1) * P]))
                    parts.append((m["xo"][:, a], x_w_o[l, a * P:(a + 1) * P]))
                parts.append((m["w2"], cmp_w2[l].rearrange("v d o -> d v o")))
                for v in range(2):
                    parts.append((m["pe"][:, v], cmp_pe[l, v]))
                item(f"small_{l}", parts)
                item(f"x_{l}", [(ring[:, 1, 0:4096].rearrange("p (k n) -> p k n", k=KT), wide(x_w_kv[l], 0, 512)),
                                (ring[:, 1, 4096:6144].rearrange("p (k n) -> p k n", k=KT), wide(x_w_q[l], 0, 256))])
                for c in range(2):
                    item(f"out{c}_{l}", [(ring[:, 2 + c, 0:4096].rearrange("p (k n) -> p k n", k=KT),
                                          wide(w_out[l], 512 * c, 512))])
                if l == 0:
                    for c in range(CH):
                        s = FF_SLOTS[c]
                        item(f"ff{c}", [
                            (ring[:, s, 0:UPW].rearrange("p (k g n) -> p k g n", k=KT, g=2)[:, :, g],
                             wide(ffn_up[0], g * FF + 256 * c, 256)) for g in range(2)] + [
                            (ring[:, s, UPW:].rearrange("p (m n) -> p m n", m=2),
                             ffn_down[0, 256 * c:256 * c + 256].rearrange("(m p) n -> p m n", p=P))])

            def expert(turn, e):
                for c in range(CH):
                    s = FF_SLOTS[c]
                    if nth[c] == 0:
                        banks.wait(sp, LAST_USE[{0: "small", 1: "x", 2: "out0", 3: "out1"}[s]] + "1")
                    sp.wait_ge(slot_free[s], turn * USES[s] + (USES[s] + nth[c]))
                    up = moe_up[bass.ds(e, 1)].rearrange("o (k p) (g n) -> p (o k) g n", p=P, g=2)
                    down = moe_down[bass.ds(e, 1), 256 * c:256 * c + 256].rearrange("o (m p) n -> p (o m) n", p=P)
                    for g in range(2):
                        sp.dma_start(ring[:, s, 0:UPW].rearrange("p (k g n) -> p k g n", k=KT, g=2)[:, :, g],
                                     up[:, :, g, 256 * c:256 * c + 256]).then_inc(slot_full[s], 16)
                    sp.dma_start(ring[:, s, UPW:].rearrange("p (m n) -> p m n", m=2), down).then_inc(slot_full[s], 16)

            with sp.Fori(0, E) as e:
                expert(e, e)
            sp.wait_ge(sem["flag_ready"], 1)
            over = sp.value_load(flag[0:1, 0:1], min_val=0, max_val=1)
            with sp.If(over > 0):
                for p in range(1, PASSES):
                    with sp.Fori(0, E) as e:
                        expert(e + p * E, e)
            sp.wait_ge(sem["h_final"], 1)
            for i in range(NT):
                sp.dma_start(out[i * P:(i + 1) * P], h[:, i]).then_inc(dma_out, 16)
            sp.wait_ge(dma_out, 16 * NT)

        @block.scalar
        def _(act):
            load = load_by(act)
            load(cst[:], consts[:, 0:C_MOE], "par_loaded")
            load(raw, rows128, "par_loaded")
            load(raw2[0:2 * CK * L], conv_w.rearrange("l k (a p) -> (l k a) p", p=P), "par_loaded")
            load(raw3, rows64, "par_loaded")
            load(hot[:], t5_hot, "t5_loaded")
            load(tab[0:BUCKETS], t5_table, "t5_loaded")
            squared = [0]

            def squares(src, n, i, wait):
                wait()
                if squared[0]:
                    act.wait_ge(sem["norm_sum"], squared[0])
                squared[0] += 1
                act.activation(junk, src, ACT.Square, accum_out=st[:, c_norm(n, i):c_norm(n, i) + 1])\
                   .then_inc(sem["norm_sum"], 1)

            def scaled(dst, src, n):
                act.wait_ge(sem["norm_rs"], n + 1)
                act.activation(dst, src, ACT.Copy, scale=rs[:, c_norm(n, 1):c_norm(n, 1) + 1])\
                   .then_inc(sem["xn1_ready"], 1)

            def gained(name, base, l, groups):
                for g in groups:
                    banks.wait(act, f"{name}{g}_{l}")
                    for k in range(2):
                        i = act.activation(xT[:, 2 * g + k], ps(f"{name}{g}_{l}")[:, 256 * k:256 * k + 256], ACT.Copy,
                                           scale=gain(base, l, 2 * g + k, 1))
                    i.then_inc(banks.drain(f"{name}{g}_{l}"), 1)

            banks.wait(act, "par")
            act.activation(par[:, 0:P], ps("par")[:, 0:P], ACT.Copy).then_inc(banks.drain("par"), 1)

            def s5_exps(l):
                S = scr[:].rearrange("p a b -> p (a b)")
                t = [S[:, 136 * n:136 * n + 136] for n in range(15)]
                act.wait_ge(sem["s5_dt"], l + 1)
                act.activation(t[3], t[2], ACT.Exp).then_inc(sem["s5_act"], 1)
                yield
                act.wait_ge(sem["s5_x1"], l + 1)
                act.activation(t[5], t[4], ACT.Exp).then_inc(sem["s5_act"], 1)
                act.wait_ge(sem["s5_ang"], 2 * l + 1)
                act.activation(t[8], t[7], ACT.Sin).then_inc(sem["s5_act"], 1)
                act.wait_ge(sem["s5_ang"], 2 * l + 2)
                act.activation(t[11], t[10], ACT.Sin).then_inc(sem["s5_act"], 1)
                yield
                act.wait_ge(sem["turns_ready"], 2 * l + 1)
                act.activation(R[:, 1], R[:, 0], ACT.Sin, scale=2 * math.pi).then_inc(sem["angles_ready"], 1)
                act.wait_ge(sem["turns_ready"], 2 * l + 2)
                act.wait_ge(sem["angles_ready"], 2 * l + 1)
                act.activation(R[:, 0], qT[:].rearrange("p i h t -> p (i h t)").rearrange("p (j t) -> p j t", j=SJ), ACT.Sin,
                               scale=-2 * math.pi, bias=cst[:, C_Q:C_Q + 1]).then_inc(sem["angles_ready"], 1)

            def probs(u, b, src, scale, to):
                return act.activation(scr[:, u % 2, b * 256:b * 256 + src.shape[-1]] if src.shape[-1] == 256 else
                                      scr[:, u % 2, b * P:b * P + P], src, ACT.Exp, bias=nmx[:, u % 2, b:b + 1],
                                      scale=scale, accum_out=to)

            def pt_copy(u, name, n):
                banks.wait(act, name)
                if u >= 2:
                    act.wait_ge(sem["pv_done"], u - 1)
                act.activation(scr[:, 2 + u % 2, 0:n], ps(name)[:, 0:n], ACT.Copy).then_inc(banks.drain(name), 1)

            def q_copy(l, nm, dst):
                banks.wait(act, nm)
                act.activation(dst, ps(nm)[0:HD].rearrange("p (h t) -> p h t", h=4), ACT.Copy).then_inc(banks.drain(nm), 1)

            for l in range(L):
                n = NORM[f"mix{l}"]
                for i in range(NT):
                    squares(h[:, i], n, i, lambda: act.wait_ge(sem["x_loaded"], 16 * NT) if l == 0 else
                            act.wait_ge(sem["h_added"], 12 * l - 2 + 2 * i))
                if l == 0:
                    act.wait_ge(banks.drain("t5"), 1)
                    act.dma_start(bias_rows, hot[0:NH]).then_inc(sem["m_stored"], 16)
                    exps = s5_exps(0)
                    next(exps)
                if l == 0:
                    next(exps)
                scaled(xn[:, 1], h[:, 1], n)
                if l == 0:
                    act.wait_ge(sem["par_ready"], 1)
                gained("mix_T", G_MIX, l, (1, 3))
                if l == 0:
                    for i in range(NT):
                        squares(memx[:, i], 1, i, lambda: act.wait_ge(sem["mem_loaded"], 16))
                if l == 0:
                    act.wait_ge(sem["m_stored"], 16)
                    load(M[:], bass.AP(tensor=bias_rows.tensor, offset=0, ap=[[1, P], [512, NH], [1, FX]]), "m_loaded")
                    act.wait_ge(sem["norm_rs"], 2)
                    for i in range(NT):
                        act.activation(memx[:, i], memx[:, i], ACT.Copy, scale=rs[:, c_norm(1, i):c_norm(1, i) + 1])\
                           .then_inc(sem["memx_ready"], 1)
                    for g in range(4):
                        banks.wait(act, f"mem_T{g}_0")
                        act.activation(memT[:, 2 * g:2 * g + 2], ps(f"mem_T{g}_0")[:].rearrange("p (k t) -> p k t", k=2),
                                       ACT.Copy).then_inc(banks.drain(f"mem_T{g}_0"), 1)
                banks.wait(act, f"u{l}")
                act.activation(uT[:], ps(f"u{l}")[:].rearrange("p (a t) -> p a t", a=2), ACT.Copy).then_inc(banks.drain(f"u{l}"), 1)
                if l == 0:
                    next(exps, None)
                banks.wait(act, f"cg{l}")
                act.activation(ca[:], ps(f"cg{l}")[:].rearrange("p (a t) -> p a t", a=2), ACT.Tanh, scale=0.5)\
                   .then_inc(banks.drain(f"cg{l}"), 1)
                for i in range(NT):
                    banks.wait(act, f"q{i}_{l}")
                    if 4 * l + i:
                        act.wait_ge(sem["head_sum"], 7 * l + i)
                    act.activation(sq[:], ps(f"q{i}_{l}")[:], ACT.Square).then_inc(banks.drain(f"q{i}_{l}"), 1)
                banks.wait(act, f"kvc{l}")
                kvc = ps(f"kvc{l}")[:].rearrange("p (v t) -> p v t", v=2)
                act.activation(CX[0:64, :, 0], kvc[0:64], ACT.Copy)
                act.activation(CX[0:64, :, 1], kvc[64:128], ACT.Copy)
                act.activation(CX[64:128, :, 0, 0:240], kvc[0:64, :, 16:256], ACT.Copy)
                act.activation(CX[64:128, :, 1, 0:240], kvc[64:128, :, 16:256], ACT.Copy).then_inc(banks.drain(f"kvc{l}"), 1)
                for i in range(NT):
                    nm = f"kv{i}_{l}"
                    banks.wait(act, nm)
                    kv = ps(nm)[:].rearrange("p (b c d) -> p b c d", b=2, c=2)
                    if l:
                        banks.wait(act, f"ow1_{l - 1}")
                    act.activation(vv[:, i], kv[:, :, 1], ACT.Copy).then_inc(banks.drain(nm), 1)
                    act.wait_ge(sem["head_sum"], 7 * l + 2 + i)
                    act.activation(sq[:, 0:256].rearrange("p (b d) -> p b d", b=2), kv[:, :, 0], ACT.Square)\
                       .then_inc(banks.drain(nm), 1)
                banks.wait(act, f"gates{l}")
                act.activation(gates[:], ps(f"gates{l}")[:, 0:48].rearrange("p (i c) -> p i c", i=NT), ACT.Tanh, scale=0.5)\
                   .then_inc(banks.drain(f"gates{l}"), 1)
                act.wait_ge(sem["ys_w"], l + 1)
                act.activation(scr[:, 2], scr[:, 1], ACT.Tanh, scale=GELU_S).then_inc(sem["ys_t"], 1)
                act.wait_ge(sem["cmp_w"], l + 1)
                act.activation(cmpx[:, 2], cmpx[:, 1], ACT.Tanh, scale=GELU_S).then_inc(sem["cmp_t"], 1)
                for i in range(NT):
                    for g in range(2):
                        q_copy(l, f"qT{i}{g}_{l}", qT[0:HD, i, 4 * g:4 * g + 4])
                for i in range(NT):
                    nm = f"glu{i}_{l}"
                    banks.wait(act, nm)
                    act.activation(scr[:, 3, 256 * i:256 * i + 256], ps(nm)[:, 256:512], ACT.Tanh, scale=0.25)\
                       .then_inc(banks.drain(nm), 1)
                banks.wait(act, f"cmp2_{l}")
                act.wait_ge(sem["head_sum"], 7 * l + 4)
                act.activation(sq[0:NCMP, 0:128], ps(f"cmp2_{l}")[0:NCMP, 0:128], ACT.Square, scale=0.5)\
                   .then_inc(banks.drain(f"cmp2_{l}"), 1)

                def mem_kv(i):
                    nm = f"mkv{i}_{l}"
                    banks.wait(act, nm)
                    if l:
                        banks.wait(act, f"xo1_{l - 1}")
                    act.activation(vx[:, i], ps(nm)[:, 256:512], ACT.Copy).then_inc(banks.drain(nm), 1)
                    act.wait_ge(sem["kc_sum"], l + 1)
                    act.wait_ge(sem["head_sum"], 7 * l + 4 + i)
                    act.activation(sq[:, 0:256], ps(nm)[:, 0:256], ACT.Square).then_inc(banks.drain(nm), 1)

                mem_kv(0)
                act.wait_ge(sem["ln_centered"], l + 1)
                for i in range(NT):
                    if i:
                        act.wait_ge(sem["ln_sum"], 2 * l + i)
                    act.activation(R[:, 0, 2], lnb[:, i], ACT.Square, accum_out=st[:, c_ln(l) + i:c_ln(l) + i + 1])\
                       .then_inc(sem["ln_sum"], 1)
                def group_squares(i):
                    act.wait_ge(sem["y_ready"], 2 * l + i + 1)
                    act.wait_ge(banks.drain(f"cvW{l}"), banks.count(f"cvW{l}", None, False) + 1)
                    if i:
                        act.wait_ge(sem["grp_sum"], 2 * l + i)
                    for n3, (c0, c1, f) in enumerate(((0, 256, 0.25), (256, 512, 0.5), (512, 1024, 1.0))):
                        k = act.activation(junk[:, c0:c1], xn[:, i, c0:c1], ACT.Square, scale=f,
                                           accum_out=st[:, c_grp(l, i) + n3:c_grp(l, i) + n3 + 1])
                    k.then_inc(sem["grp_sum"], 1)

                for v in range(2 * NH + 1):
                    i, hh = divmod(v, NH)
                    nk = P * (i + 1)
                    u = 20 * l + v
                    if v < 2 * NH:
                        act.wait_ge(sem["max_ready"], u + 1)
                        for b in range(2):
                            e = probs(u, b, scr[:, u % 2, b * nk:b * nk + nk], 1.0, sums[:, i, b, hh:hh + 1])
                        e.then_inc(sem["probs_ready"], 1)
                    if v:
                        pi, ph = divmod(v - 1, NH)
                        pt_copy(u - 1, f"pT{pi}{ph}_{l}", 2 * P * (pi + 1))
                    if v in C_EXPS:
                        act.wait_ge(sem["c_centered"], 2 * l + C_EXPS.index(v) + 1)
                        act.activation(pc[:], pc[:], ACT.Exp).then_inc(sem["c_exp"], 1)
                    if v - 1 in C_TURN:
                        ci = C_TURN.index(v - 1)
                        for g in range(2):
                            nm = f"pcT{ci}{g}_{l}"
                            banks.wait(act, nm)
                            if l or ci:
                                banks.wait(act, f"oc{1 - ci}_{l + ci - 1}")
                            act.activation(pcT[:, 4 * g:4 * g + 4], ps(nm)[0:NCMP].rearrange("p (h t) -> p h t", h=4), ACT.Copy)\
                               .then_inc(banks.drain(nm), 1)
                    if v == CONV_TANH:
                        act.wait_ge(sem["ln_gained"], l + 1)
                        act.activation(lnb[:], ca[:], ACT.Tanh, scale=0.5).then_inc(sem["cv_t"], 1)
                    if v == CONV_COPY:
                        banks.wait(act, f"cvW{l}")
                        act.activation(xn[:, :, CW:2 * CW], ps(f"cvW{l}")[:].rearrange("p (i c) -> p i c", i=NT), ACT.Copy)\
                           .then_inc(banks.drain(f"cvW{l}"), 1)
                    if v == Y_SQUARES:
                        group_squares(0)
                group_squares(1)
                gained("y_T", G_OUT, l, (1, 3))
                mem_kv(1)
                n = NORM[f"cross{l}"]
                for i in range(NT):
                    squares(h[:, i], n, i, lambda: act.wait_ge(sem["h_added"], 12 * l + 2 + 2 * i))
                banks.wait(act, f"y_T3_{l}")
                scaled(xn[:, 1], h[:, 1], n)
                gained("cross_T", G_CROSS, l, (1, 3))
                banks.wait(act, f"xq{l}")
                act.wait_ge(sem["head_sum"], 7 * l + 6)
                act.activation(sq[:], ps(f"xq{l}")[:], ACT.Square).then_inc(banks.drain(f"xq{l}"), 1)
                for i in range(NT):
                    q_copy(l, f"xqT{i}_{l}", qT[64:128, i, 0:4])
                for k in range(5):
                    u = 20 * l + 16 + k
                    if k < 4:
                        i, hp = k // 2, k % 2
                        act.wait_ge(sem["max_ready"], u + 1)
                        banks.wait(act, f"xpT{k - 2}_{l}" if k >= 2 else f"pT1{NH - 2 + k}_{l}")
                        for b in range(2):
                            e = probs(u, b, ps(f"xs{k}_{l}")[:, 256 * b:256 * b + 256], SCALE,
                                      sums[:, i, 0, 2 * hp + b:2 * hp + b + 1])
                        e.then_inc(sem["probs_ready"], 1)
                    if k:
                        pt_copy(u - 1, f"xpT{k - 1}_{l}", 512)
                n = NORM[f"ffn{l}"]
                for i in range(NT):
                    squares(h[:, i], n, i, lambda: act.wait_ge(sem["h_added"], 12 * l + 6 + 2 * i))
                banks.wait(act, f"cross_T3_{l}")
                scaled(xn[:, 1], h[:, 1], n)
                gained("ffn_T", G_FFN, l, (1, 3))
                if l == 0:
                    banks.wait(act, "xo1_0")
                    s5_params(load, 1)
                    exps = s5_exps(1)
                    for t in range(HT):
                        if t in (5, 9, 18):
                            next(exps, None)
                        banks.wait(act, f"up{t}")
                        if t >= 2:
                            act.wait_ge(sem["gated"], t - 1)
                        act.activation(th[:, t % 2], ps(f"up{t}")[:, 0:256], ACT.Tanh, scale=0.5).then_inc(sem["tanh_up"], 1)
            act.wait_ge(sem["mem_gained"], L)
            load(cste, consts[:, C_MOE:C_END], "moe_consts_loaded")
            act.wait_ge(sem["r_centered"], 1)
            act.activation(ex, lg, ACT.Exp).then_inc(sem["r_exp"], 1)

            def expert(turn):
                for t in range(HT):
                    banks.wait(act, f"mup{t}", turn)
                    if t >= 2:
                        act.wait_ge(sem["e_gated"], turn * HT + (t - 1))
                    act.activation(th[:, t % 2, 0:CAP], ps(f"mup{t}")[:, 0:CAP], ACT.Tanh, scale=0.5)\
                       .then_inc(sem["e_tanh"], 1)
                for g in range(2):
                    banks.wait(act, f"mdown{g}", turn)
                    act.activation(ye[:, 512 * g:512 * g + 512], ps(f"mdown{g}")[0:CAP], ACT.Copy)\
                       .then_inc(banks.drain(f"mdown{g}"), 1)

            with act.Fori(0, E) as turn:
                expert(turn)
            act.wait_ge(sem["flag_ready"], 1)
            over = act.value_load(flag[0:1, 0:1], min_val=0, max_val=1)
            with act.If(over > 0):
                with act.Fori(E, PASSES * E) as turn:
                    expert(turn)

        @block.gpsimd
        def _(pool):
            n_own = [0]

            def own(i):
                n_own[0] += 1
                i.then_inc(sem["pool_step"], 1)
                pool.wait_ge(sem["pool_step"], n_own[0])

            def root(c, n, scale, name, parts=P):
                own(pool.tensor_scalar(rs[0:parts, c:c + n], st[0:parts, c:c + n], scale, EPS, ALU.mult, ALU.add))
                pool.tensor_tensor(rs[0:parts, c:c + n], rs[0:parts, c:c + n], cst[0:parts, C_NH:C_NH + 1].to_broadcast([parts, n]) if n > 16
                                   else cst[0:parts, C_NH:C_NH + n], ALU.pow).then_inc(sem[name], 1)

            own(pool.memset(tab[BUCKETS:BUCKETS + 1], NEG))
            pool.memset(cv[:], 0.0).then_inc(sem["pads_ready"], 1)
            pool.wait_ge(sem["par_loaded"], 16 * 4)
            sums_seen = [0]

            def norm(n):
                sums_seen[0] += 2
                pool.wait_ge(sem["norm_sum"], sums_seen[0])
                root(c_norm(n, 0), 2, 1.0 / D, "norm_rs")

            for l in range(L):
                norm(NORM[f"mix{l}"])
                if l == 0:
                    norm(1)
                for j in range(SJ):
                    g = SJ * l + j
                    z, xo = zz[:, j % 2], X[:, j % 2]
                    pool.wait_ge(sem["scanned"], g + 1)
                    if g:
                        pool.wait_ge(sem["states_ready"], g)
                    if j >= 2:
                        pool.wait_ge(sem["states_used"], g - 1)
                    T1, T2 = scr[:, 2].rearrange("p (a t) -> p a t", a=2), scr[:, 3].rearrange("p (a t) -> p a t", a=2)
                    for a in range(2):
                        pool.tensor_tensor(T1[:, a], z[:, a], R[:, 0, j], ALU.mult)
                        k = pool.tensor_tensor(T2[:, a], z[:, a], R[:, 1, j], ALU.mult)
                    own(k)
                    pool.tensor_tensor(xo[:, 0], T1[:, 0], T2[:, 1], ALU.subtract)
                    k = pool.tensor_tensor(xo[:, 1], T1[:, 1], T2[:, 0], ALU.add)
                    k.then_inc(sem["states_ready"], 1)
                    if j == 5 - l:
                        for i in range(NT):
                            pool.wait_ge(sem["head_sum"], 7 * l + 1 + i)
                            root(c_qk(l, i), 8, 1.0 / HD, "q_rs")
                for i in range(NT):
                    pool.wait_ge(sem["head_sum"], 7 * l + 3 + i)
                    root(c_qk(l, i) + 8, 4, 1.0 / HD, "k_rs")
                pool.wait_ge(sem["kc_sum"], l + 1)
                root(c_kc(l), 2, 1.0 / HD, "kc_rs", NCMP)
                pool.wait_ge(sem["ln_sum"], 2 * l + 2)
                root(c_ln(l), 2, 1.0 / CW, "ln_rs")
                pool.wait_ge(sem["head_sum"], 7 * l + 5)
                root(c_xk(l, 0), 4, 1.0 / HD, "xk_rs")
                for i in range(NT):
                    pool.wait_ge(sem["grp_sum"], 2 * l + i + 1)
                    c = c_grp(l, i)
                    own(pool.tensor_scalar(rs[:, c:c + 2], st[:, c:c + 2], 1.0 / CW, EPS, ALU.mult, ALU.add))
                    own(pool.tensor_scalar(rs[:, c + 2:c + 3], st[:, c + 2:c + 3], 1.0 / 512, EPS, ALU.mult, ALU.add))
                    pool.tensor_tensor(rs[:, c:c + 3], rs[:, c:c + 3], cst[:, C_NH:C_NH + 3], ALU.pow).then_inc(sem["grp_rs"], 1)
                pool.wait_ge(sem["head_sum"], 7 * l + 6)
                root(c_xk(l, 1), 4, 1.0 / HD, "xk_rs")
                norm(NORM[f"cross{l}"])
                pool.wait_ge(sem["head_sum"], 7 * l + 7)
                root(c_xq(l, 0), 8, 1.0 / HD, "xq_rs")
                norm(NORM[f"ffn{l}"])

        @block.vector
        def _(dve):
            n_own = [0]

            def own(i):
                n_own[0] += 1
                i.then_inc(sem["dve_step"], 1)
                dve.wait_ge(sem["dve_step"], n_own[0])

            def signal(s):
                dve.sem_inc(s, 1)

            def col(t, c):
                return t[:, c:c + 1]

            def spread(a, shape):
                return a.unsqueeze(len(a.shape)).to_broadcast(shape)

            def scaled(dst, src, n, wait):
                dve.wait_ge(sem["norm_rs"], n + 1)
                wait()
                dve.tensor_scalar(dst, src, col(rs, c_norm(n, 0)), None, ALU.mult).then_inc(sem["xn0_ready"], 1)

            def gained(name, base, l, groups):
                for g in groups:
                    nm = f"{name}{g}_{l}"
                    banks.wait(dve, nm)
                    dve.tensor_tensor(xT[:, 2 * g:2 * g + 2], ps(nm)[:].rearrange("p (k t) -> p k t", k=2),
                                      spread(gain(base, l, 2 * g, 2), [P, 2, SEQ]), ALU.mult).then_inc(banks.drain(nm), 1)

            def s5_weights(l):
                S = scr[:].rearrange("p a b -> p (a b)")
                t = [S[:, 136 * n:136 * n + 136] for n in range(15)]
                Xf = X[:].rearrange("p a b t -> p (a b t)")
                dve.wait_ge(sem["s5_loaded"], 16 * 8 * (l + 1))
                own(dve.tensor_copy(t[0][:, 0:8], par[:, 96 + 8 * l:104 + 8 * l]))
                own(dve.tensor_copy(t[1][:, 0:8], par[:, 112 + 8 * l:120 + 8 * l]))
                own(dve.tensor_copy(t[2][0:64, 0:8], ldt[0:64, 16 * l:16 * l + 16:2]))
                own(dve.tensor_copy(t[2][64:128, 0:8], ldt[64:128, 16 * l + 1:16 * l + 16:2]))
                dve.tensor_copy(t[2][:, 8:136].rearrange("p (a s) -> p a s", a=2),
                                spread(ldt[:, 32 + 2 * l:34 + 2 * l], [P, 2, 64])).then_inc(sem["s5_dt"], 1)
                yield
                lr, li, dt, mg = t[0], t[1], t[3], t[5]
                dve.wait_ge(sem["s5_act"], 4 * l + 1)
                dve.tensor_tensor(t[4], lr, dt, ALU.mult).then_inc(sem["s5_x1"], 1)
                own(dve.tensor_tensor(t[6], li, dt, ALU.mult))
                own(dve.tensor_scalar(t[7], t[6], 1 / (2 * math.pi), ROUND, ALU.mult, ALU.add))
                own(dve.tensor_scalar(t[8], t[7], -ROUND, None, ALU.add))
                own(dve.scalar_tensor_tensor(t[9], t[8], -TWO_PI_HI, t[6], ALU.mult, ALU.add))
                own(dve.scalar_tensor_tensor(t[10], t[8], -TWO_PI_LO, t[9], ALU.mult, ALU.add))
                dve.tensor_scalar(t[7], t[10], math.pi - 1e-6, -math.pi + 1e-6, ALU.min, ALU.max).then_inc(sem["s5_ang"], 1)
                dve.wait_ge(sem["s5_ang"], 2 * l + 1)
                own(dve.scalar_tensor_tensor(t[9], t[7], -1.0, t[7], ALU.mult, ALU.max))
                t_red = t[14][:, 0:8]
                own(dve.tensor_copy(t_red, t[10][:, 0:8]))
                dve.tensor_scalar(t[10], t[9], -1.0, math.pi / 2, ALU.mult, ALU.add).then_inc(sem["s5_ang"], 1)
                rad = t[13][:, 0:8]
                own(dve.tensor_scalar(turn_step[:, 0], t_red, 1 / (2 * math.pi), ROUND_12, ALU.mult, ALU.add))
                own(dve.tensor_scalar(turn_step[:, 0], turn_step[:, 0], -ROUND_12, None, ALU.add))
                own(dve.scalar_tensor_tensor(rad, turn_step[:, 0], -TWO_PI_HI, t_red, ALU.mult, ALU.add))
                own(dve.scalar_tensor_tensor(rad, turn_step[:, 0], -TWO_PI_LO, rad, ALU.mult, ALU.add))
                own(dve.tensor_scalar(turn_step[:, 1], rad, 1 / (2 * math.pi), None, ALU.mult))
                yield
                sn, cs = t[8], t[11]
                own(dve.tensor_tensor(t[12], lr, lr, ALU.mult))
                own(dve.tensor_tensor(t[13], li, li, ALU.mult))
                own(dve.tensor_tensor(t[12], t[12], t[13], ALU.add))
                own(dve.reciprocal(t[12], t[12]))
                dve.wait_ge(sem["s5_act"], 4 * l + 4)
                own(dve.tensor_copy(mag[:], mg[:, 0:8]))
                own(dve.tensor_tensor(t[9], mg, cs, ALU.mult))
                own(dve.tensor_tensor(t[6], mg, sn, ALU.mult))
                own(dve.tensor_scalar(t[9], t[9], -1.0, None, ALU.add))
                own(dve.tensor_tensor(t[4], t[9], lr, ALU.mult))
                own(dve.tensor_tensor(t[7], t[6], li, ALU.mult))
                own(dve.tensor_tensor(t[4], t[4], t[7], ALU.add))
                own(dve.tensor_tensor(t[4], t[4], t[12], ALU.mult))
                own(dve.tensor_tensor(t[7], t[6], lr, ALU.mult))
                own(dve.tensor_tensor(t[13], t[9], li, ALU.mult))
                own(dve.tensor_tensor(t[7], t[7], t[13], ALU.subtract))
                own(dve.tensor_tensor(t[7], t[7], t[12], ALU.mult))
                yield
                fr, fi = t[4][:, 8:136], t[7][:, 8:136]
                br, bi = Xf[:, 0:P], Xf[:, P:2 * P]
                o = [t[n][:, 8:136] for n in (0, 1, 2, 3)]
                own(dve.tensor_tensor(o[0], fr, br, ALU.mult))
                own(dve.tensor_tensor(o[1], fi, bi, ALU.mult))
                own(dve.tensor_tensor(o[2], fr, bi, ALU.mult))
                own(dve.tensor_tensor(o[3], fi, br, ALU.mult))
                own(dve.tensor_tensor(o[0], o[0], o[1], ALU.subtract))
                own(dve.tensor_tensor(o[2], o[2], o[3], ALU.add))
                m16 = cst[:, C_M16:C_M16 + 2]
                for c, b in enumerate((o[0], o[2])):
                    for a in range(2):
                        own(dve.tensor_tensor(BL[:, c, a], b[:, 64 * a:64 * a + 64].unsqueeze(1).to_broadcast([P, 2, 64]),
                                              spread(m16, [P, 2, 64]), ALU.mult))
                for c, s in ((0, 1.0), (1, -1.0)):
                    src = Xf[:, (2 + c) * P:(3 + c) * P].rearrange("p (j c) -> p j c", j=SJ)
                    for half in range(2):
                        k = dve.tensor_scalar(CL[:, c, :, 16 * half:16 * half + 16], src, col(cst, C_M64 + half), s, ALU.mult, ALU.mult)
                k.then_inc(sem["s5_weights"], 1)

            def s5_turns(l):
                A, B, C = qT[:].rearrange("p i h t -> p (i h t)").rearrange("p (j t) -> p j t", j=SJ), R[:, 0], R[:, 1]
                time = cst[:, C_T:C_T + SEQ].unsqueeze(1).to_broadcast([P, SJ, SEQ])
                own(dve.tensor_tensor(A, time, spread(turn_step[:, 0], [P, SJ, SEQ]), ALU.mult))
                own(dve.tensor_tensor(B, time, spread(turn_step[:, 1], [P, SJ, SEQ]), ALU.mult))
                yield
                own(dve.tensor_tensor(C, A, B, ALU.add))
                own(dve.tensor_scalar(C, C, ROUND, None, ALU.add))
                yield
                own(dve.scalar_tensor_tensor(C, C, -ROUND, A, ALU.add, ALU.subtract))
                own(dve.tensor_tensor(B, B, C, ALU.subtract))
                yield
                dve.tensor_scalar(B, B, 0.5 - 1e-7, -0.5 + 1e-7, ALU.min, ALU.max).then_inc(sem["turns_ready"], 1)
                dve.wait_ge(sem["turns_ready"], 2 * l + 1)
                dve.scalar_tensor_tensor(A, B, -1.0, B, ALU.mult, ALU.max).then_inc(sem["turns_ready"], 1)

            def s5(l, j):
                g = SJ * l + j
                nm = f"bu{j}_{l}"
                banks.wait(dve, nm)
                b = ps(nm)[:].rearrange("p (a t) -> p a t", a=2)
                T1, T2 = (scr[:, k].rearrange("p (a t) -> p a t", a=2) for k in range(2))
                if j == 0:
                    dve.wait_ge(sem["angles_ready"], 2 * l + 2)
                own(dve.tensor_tensor(T1, b, R[:, 0, j].unsqueeze(1).to_broadcast([P, 2, SEQ]), ALU.mult))
                dve.tensor_tensor(T2, b, R[:, 1, j].unsqueeze(1).to_broadcast([P, 2, SEQ]), ALU.mult).then_inc(banks.drain(nm), 1)
                dve.wait_ge(banks.drain(nm), banks.count(nm, None, False) + 1)
                if j >= 2:
                    dve.wait_ge(sem["states_ready"], g - 1)
                z = zz[:, j % 2]
                own(dve.tensor_tensor(z[:, 0], T1[:, 0], T2[:, 1], ALU.add))
                own(dve.tensor_tensor(z[:, 1], T1[:, 1], T2[:, 0], ALU.subtract))
                for a in range(2):
                    k = dve.tensor_tensor_scan(z[:, a], col(mag, j).to_broadcast([P, SEQ]), z[:, a], 0.0, ALU.mult, ALU.add)
                k.then_inc(sem["scanned"], 1)

            def head_sums(src, c, n, parts=P, name="head_sum"):
                dve.tensor_reduce(st[0:parts, c:c + n], src.rearrange("p (h d) -> p h d", h=n), AX, ALU.add).then_inc(sem[name], 1)

            def gelu_inner(dst, y):
                own(dve.tensor_tensor(dst, y, y, ALU.mult))
                own(dve.tensor_scalar(dst, dst, GELU_C, 1.0, ALU.mult, ALU.add))
                return dve.tensor_tensor(dst, dst, y, ALU.mult)

            for l in range(L):
                n = NORM[f"mix{l}"]
                if l:
                    scaled(xn[:, 0], h[:, 0], n, lambda: None)
                if l == 0:
                    banks.wait(dve, "par")
                    dve.wait_ge(banks.drain("par"), 1)
                    own(dve.tensor_copy(par[:, P:252], ps("par")[:, P:252]))
                    own(dve.tensor_copy(par[0:HD, 252:264], ps("par")[0:HD, 252:264]))
                    for m in range(L):
                        for b in range(3):
                            own(dve.tensor_tensor(gk[:, m, b:b + 1], par[0:HD, 252 + m:253 + m],
                                                  par[0:HD, 254 + 3 * m + b:255 + 3 * m + b], ALU.mult))
                        own(dve.tensor_tensor(gk[:, m, 3:4], par[0:HD, 260 + m:261 + m], par[0:HD, 262 + m:263 + m], ALU.mult))
                    signal(sem["par_ready"])
                    signal(banks.drain("par"))
                    dve.wait_ge(sem["ldt_loaded"], 16 * 5)
                    weights = s5_weights(0)
                    next(weights)
                    banks.wait(dve, "t5")
                    dve.tensor_copy(hot[0:NH], ps("t5")[0:NH]).then_inc(banks.drain("t5"), 1)
                    next(weights)
                    dve.wait_ge(sem["x_loaded"], 16 * NT)
                    scaled(xn[:, 0], h[:, 0], n, lambda: None)
                gained("mix_T", G_MIX, l, (0, 2))
                if l == 0:
                    for make in (weights, s5_turns(0)):
                        for _ in make:
                            pass
                taps_done = [0]

                def taps(n):
                    for k in range(taps_done[0], min(taps_done[0] + n, CK)):
                        for a in range(2):
                            tap = par[:, P + (l * CK + k) * 2 + a:P + (l * CK + k) * 2 + a + 1]
                            if k == 0:
                                e = dve.tensor_scalar(ca[:, a], cv[:, a, 0:SEQ], tap, None, ALU.mult)
                            else:
                                e = dve.scalar_tensor_tensor(ca[:, a], cv[:, a, k:k + SEQ], tap, ca[:, a], ALU.mult, ALU.add)
                        own(e)
                    taps_done[0] += n
                    if taps_done[0] >= CK:
                        for a in range(2):
                            e = dve.tensor_scalar(ca[:, a], ca[:, a], 0.5, col(par, G_CB + 2 * l + a), ALU.mult, ALU.add)
                        e.then_inc(sem["conv_done"], 1)

                def conv_input():
                    banks.wait(dve, f"ca{l}")
                    dve.wait_ge(banks.drain(f"cg{l}"), banks.count(f"cg{l}", None, False) + 1)
                    if l == 0:
                        dve.wait_ge(sem["pads_ready"], 1)
                    own(dve.scalar_tensor_tensor(cv[:, :, CK - 1:], ca[:], 1.0, ps(f"ca{l}")[:].rearrange("p (a t) -> p a t", a=2),
                                                 ALU.add, ALU.mult))
                    signal(banks.drain(f"ca{l}"))

                def q_sums(i):
                    dve.wait_ge(banks.drain(f"q{i}_{l}"), banks.count(f"q{i}_{l}", None, False) + 1)
                    head_sums(sq[:], c_qk(l, i), 8)

                def q_norm(i):
                    dve.wait_ge(sem["q_rs"], 2 * l + i + 1)
                    c = c_qk(l, i)
                    dve.tensor_tensor(q_of[i].rearrange("p (h d) -> p h d", h=NH), ps(f"q{i}_{l}")[:].rearrange("p (h d) -> p h d", h=NH),
                                      spread(rs[:, c:c + 8], [P, NH, HD]), ALU.mult).then_inc(banks.drain(f"q{i}_{l}"), 1)

                if l == 0:
                    conv_input()
                s5(l, 0)
                if l:
                    s5(l, 1)
                    conv_input()
                    s5(l, 2)
                    taps(1)
                    s5(l, 3)
                    taps(1)
                    s5(l, 4)
                    q_sums(0)
                    s5(l, 5)
                    q_sums(1)
                    taps(1)
                    s5(l, 6)
                    s5(l, 7)
                else:
                    for j in range(1, 5):
                        taps(2)
                        s5(l, j)
                    q_sums(0)
                    s5(l, 5)
                    q_sums(1)
                    s5(l, 6)
                    taps(1)
                    s5(l, 7)
                for i in range(NT):
                    q_norm(i)
                taps(4)
                for i in range(NT):
                    dve.wait_ge(banks.drain(f"kv{i}_{l}"), banks.count(f"kv{i}_{l}", None, False) + 2)
                    head_sums(sq[:, 0:256], c_qk(l, i) + 8, 4)
                    if i == 0:
                        taps(3)
                nm = f"ys{l}"
                banks.wait(dve, nm)
                y = uT[:]
                for a in range(2):
                    e = dve.scalar_tensor_tensor(y[:, a], uT[:, a], col(par, G_D + 2 * l + a), ps(nm)[:, 256 * a:256 * a + 256],
                                                 ALU.mult, ALU.add)
                e.then_inc(banks.drain(nm), 1)
                dve.wait_ge(banks.drain(nm), banks.count(nm, None, False) + 1)
                w = scr[:, 1].rearrange("p (a t) -> p a t", a=2)
                gelu_inner(w, y).then_inc(sem["ys_w"], 1)
                for i in range(NT):
                    dve.wait_ge(sem["k_rs"], 2 * l + i + 1)
                    c = c_qk(l, i)
                    kv = ps(f"kv{i}_{l}")[:].rearrange("p (b c e d) -> p b c e d", b=2, c=2, e=2)
                    dve.tensor_tensor(kn[:, i].rearrange("p b (e d) -> p b e d", e=2), kv[:, :, 0],
                                      spread(rs[:, c + 8:c + 12].rearrange("p (b e) -> p b e", b=2), [P, 2, 2, HD]), ALU.mult)\
                       .then_inc(banks.drain(f"kv{i}_{l}"), 1)
                if l == 0:
                    dve.wait_ge(banks.drain("mem_T2_0"), banks.count("mem_T2_0", None, False) + 1)
                    dve.wait_ge(banks.drain("mem_T3_0"), banks.count("mem_T3_0", None, False) + 1)
                dve.tensor_tensor(memg, memT[:], spread(gain(G_MEM, l, 0, KT), [P, KT, SEQ]), ALU.mult).then_inc(sem["mem_gained"], 1)
                dve.wait_ge(sem["ys_t"], l + 1)
                dve.scalar_tensor_tensor(scr[:, 0].rearrange("p (a t) -> p a t", a=2), scr[:, 2].rearrange("p (a t) -> p a t", a=2),
                                         1.0, y, ALU.add, ALU.mult).then_inc(sem["ys_g"], 1)
                taps(8)
                nm = f"cmp1_{l}"
                banks.wait(dve, nm)
                own(dve.tensor_copy(cb[:], ps(nm)[0:HD, 64:66]))
                x1 = cmpx[:, 0].rearrange("p v h n -> p v (h n)")
                own(dve.tensor_tensor(x1, ps(nm)[0:HD, 0:60].rearrange("p (v n) -> p v n", v=2), spread(cb[:], [HD, 2, 30]), ALU.add))
                gelu_inner(cmpx[:, 1], cmpx[:, 0]).then_inc(sem["cmp_w"], 1)
                signal(banks.drain(nm))
                taps(1)
                dve.wait_ge(sem["cmp_t"], l + 1)
                dve.scalar_tensor_tensor(cmpx[:, 3], cmpx[:, 2], 1.0, cmpx[:, 0], ALU.add, ALU.mult).then_inc(sem["cmp_g"], 1)
                for k in range(KVH):
                    nm = f"kT{k}_{l}"
                    banks.wait(dve, nm)
                    for b in range(2):
                        e = dve.tensor_scalar(kT[0:HD, 2 * k + b], ps(nm)[0:HD, 256 * b:256 * b + 256], gk[:, l, 1 + b:2 + b], None, ALU.mult)
                    e.then_inc(banks.drain(nm), 1)
                for i in range(NT):
                    nm = f"glu{i}_{l}"
                    dve.wait_ge(banks.drain(nm), banks.count(nm, None, False) + 1)
                    banks.wait(dve, f"qT11_{l}")
                    dve.scalar_tensor_tensor(xn[:, i, 0:CW], scr[:, 3, 256 * i:256 * i + 256], 1.0, ps(nm)[:, 0:256],
                                             ALU.add, ALU.mult).then_inc(banks.drain(nm), 1)
                nm = f"cmp2_{l}"
                banks.wait(dve, nm)
                dve.wait_ge(banks.drain(nm), banks.count(nm, None, False) + 1)
                head_sums(sq[0:NCMP, 0:128], c_kc(l), 2, NCMP, "kc_sum")
                own(dve.tensor_scalar(vc[:], ps(nm)[0:NCMP, 128:256].rearrange("p (h d) -> p h d", h=2), 0.5, None, ALU.mult))
                dve.wait_ge(sem["kc_rs"], l + 1)
                dve.scalar_tensor_tensor(kcn[:], ps(nm)[0:NCMP, 0:128].rearrange("p (h d) -> p h d", h=2), 0.5,
                                         spread(rs[0:NCMP, c_kc(l):c_kc(l) + 2], [NCMP, 2, HD]), ALU.mult, ALU.mult)\
                   .then_inc(banks.drain(nm), 1)
                taps(CK)
                nm = f"cmpT{l}"
                banks.wait(dve, nm)
                dve.tensor_scalar(kcT[:], ps(nm)[0:HD, 0:30].rearrange("p (h n) -> p h n", h=2), gk[:, l, 0:1], None, ALU.mult)\
                   .then_inc(banks.drain(nm), 1)

                def mem_sums(i):
                    nm = f"mkv{i}_{l}"
                    dve.wait_ge(banks.drain(nm), banks.count(nm, None, False) + 2)
                    head_sums(sq[:, 0:256], c_xk(l, i), 4)

                mem_sums(0)
                nm = f"cvT{l}"
                banks.wait(dve, nm)
                pv = ps(nm)[:].rearrange("p (i c) -> p i c", i=NT)
                own(dve.tensor_reduce(rs[:, 140:142], pv, AX, ALU.add))
                own(dve.tensor_scalar(rs[:, 142:144], rs[:, 140:142], -1.0 / CW, None, ALU.mult))
                own(dve.tensor_tensor(lnb[:], pv, spread(rs[:, 142:144], [P, NT, CW]), ALU.add))
                signal(banks.drain(nm))
                signal(sem["ln_centered"])

                def mem_keys(i):
                    nm = f"mkv{i}_{l}"
                    dve.wait_ge(sem["xk_rs"], 2 * l + i + 1)
                    c = c_xk(l, i)
                    dve.tensor_tensor(kn[:, i].rearrange("p b (e d) -> p (b e) d", e=2), ps(nm)[:, 0:256].rearrange("p (h d) -> p h d", h=4),
                                      spread(rs[:, c:c + 4], [P, 4, HD]), ALU.mult).then_inc(banks.drain(nm), 1)

                mem_keys(0)
                dve.wait_ge(sem["ln_rs"], l + 1)
                dve.tensor_tensor(lnb[:], lnb[:], spread(rs[:, c_ln(l):c_ln(l) + 2], [P, NT, CW]), ALU.mult).then_inc(sem["ln_scaled"], 1)

                def conv_gained():
                    nm = f"cvB{l}"
                    banks.wait(dve, nm)
                    for a in range(2):
                        own(dve.tensor_scalar(ca[:, a], ps(nm)[:, 256 * a:256 * a + 256], col(par, G_LG + 2 * l + a),
                                              col(par, G_LB + 2 * l + a), ALU.mult, ALU.add))
                    signal(banks.drain(nm))
                    signal(sem["ln_gained"])

                def conv_silu():
                    dve.wait_ge(sem["cv_t"], l + 1)
                    dve.scalar_tensor_tensor(ca[:], lnb[:], 1.0, ca[:], ALU.add, ALU.mult).then_inc(sem["silu_ready"], 1)

                def c_scores(i):
                    nm = f"sc_c{i}_{l}"
                    banks.wait(dve, nm)
                    if l or i:
                        banks.wait(dve, f"pcT{1 - i}1_{l + i - 1}")
                    lo = 128 * i + 224 - 16 * (NCMP - 1)
                    bias = M[:, :, lo:128 * i + 225:16][:, :, ::-1]
                    own(dve.scalar_tensor_tensor(pc[:], ps(nm)[:, 0:120].rearrange("p (h n) -> p h n", h=NH), SCALE, bias,
                                                 ALU.mult, ALU.add))
                    dve.tensor_reduce(mxc[:], pc[:], AX, ALU.max).then_inc(banks.drain(nm), 1)
                    dve.wait_ge(banks.drain(nm), banks.count(nm, None, False) + 1)
                    own(dve.tensor_scalar(mxc[:], mxc[:], -1e20, None, ALU.max))
                    dve.tensor_tensor(pc[:], pc[:], spread(mxc[:], [P, NH, NCMP]), ALU.subtract).then_inc(sem["c_centered"], 1)

                def c_sums(i):
                    dve.wait_ge(sem["c_exp"], 2 * l + i + 1)
                    own(dve.tensor_reduce(sumc[:, i, 0], pc[:], AX, ALU.add))
                    own(dve.tensor_scalar(sumc[:, i, 0], sumc[:, i, 0], 1e-30, None, ALU.max))

                def combine(i):
                    dve.wait_ge(sem["probs_ready"], 20 * l + 8 * i + NH)
                    own(dve.tensor_copy(sumc[:, i, 1:3], sums[:, i]))
                    own(dve.reciprocal(sumc[:, i], sumc[:, i]))
                    own(dve.tensor_scalar(sq[:, 0:24], gates[:, i], 1.0, 0.5, ALU.add, ALU.mult))
                    own(dve.tensor_tensor(sumc[:, i], sumc[:, i], sq[:, 0:24].rearrange("p (h b) -> p b h", b=3), ALU.mult))
                    Y = xn[:, i, 512:1024].rearrange("p (h d) -> p h d", h=NH)
                    tmp = sq[:].rearrange("p (h d) -> p h d", h=NH)
                    for n, (b, nm) in enumerate(((0, f"oc{i}_{l}"), (1, f"os{i}_{l}"), (2, f"ow{i}_{l}"))):
                        banks.wait(dve, nm)
                        o = ps(nm)[:].rearrange("p (h d) -> p h d", h=NH)
                        dve.tensor_tensor(tmp if n else Y, o, spread(sumc[:, i, b], [P, NH, HD]), ALU.mult).then_inc(banks.drain(nm), 1)
                        dve.wait_ge(banks.drain(nm), banks.count(nm, None, False) + 1)
                        if n == 1:
                            own(dve.tensor_tensor(Y, Y, tmp, ALU.add))
                        if n == 2:
                            dve.tensor_tensor(Y, Y, tmp, ALU.add).then_inc(sem["y_ready"], 1)

                def y_scale(i):
                    dve.wait_ge(sem["grp_rs"], 2 * l + i + 1)
                    for n3, (c0, c1, f) in enumerate(((0, 256, 0.25), (256, 512, 0.5), (512, 1024, 1.0))):
                        e = dve.tensor_scalar(xn[:, i, c0:c1], xn[:, i, c0:c1], col(rs, c_grp(l, i) + n3), f, ALU.mult, ALU.mult)
                    e.then_inc(sem["y_scaled"], 1)

                if l == 0:
                    dve.wait_ge(sem["m_loaded"], 16)
                for v in range(2 * NH):
                    i, hh = divmod(v, NH)
                    nk = P * (i + 1)
                    u = 20 * l + v
                    nm = f"sc{i}{hh}_{l}"
                    banks.wait(dve, nm)
                    if u >= 2:
                        banks.wait(dve, transposed(u - 2))
                    bias = M[:, hh, P:P * i + 256][:, ::-1].unsqueeze(1).to_broadcast([P, 2, nk])
                    S = scr[:, u % 2, 0:2 * nk].rearrange("p (b s) -> p b s", b=2)
                    dve.scalar_tensor_tensor(S, ps(nm)[:, 0:2 * nk].rearrange("p (b s) -> p b s", b=2), SCALE, bias,
                                             ALU.mult, ALU.add).then_inc(banks.drain(nm), 1)
                    dve.wait_ge(banks.drain(nm), banks.count(nm, None, False) + 1)
                    dve.tensor_reduce(nmx[:, u % 2], S, AX, ALU.max, negate=True).then_inc(sem["max_ready"], 1)
                    if v in C_EXPS:
                        c_scores(C_EXPS.index(v))
                    if v in C_TURN:
                        c_sums(C_TURN.index(v))
                    if v == CONV_GAIN:
                        conv_gained()
                    if v == CONV_SILU:
                        conv_silu()
                    if v == COMBINE:
                        combine(0)
                    if v == Y_SCALE:
                        y_scale(0)
                combine(1)
                y_scale(1)
                gained("y_T", G_OUT, l, (0, 2))
                mem_sums(1)
                mem_keys(1)

                def add_in(name):
                    for i in range(NT):
                        for m in range(2):
                            nm = f"{name}{2 * i + m}_{l}" if name != "down" else f"down{2 * i + m}"
                            banks.wait(dve, nm)
                            dst = h[:, i, 512 * m:512 * m + 512]
                            dve.tensor_tensor(dst, dst, ps(nm)[:], ALU.add).then_inc(sem["h_added"], 1)

                add_in("out")
                for g in range(2):
                    nm = f"mkT{g}_{l}"
                    banks.wait(dve, nm)
                    dve.tensor_scalar(kT[64:128, 2 * g:2 * g + 2], ps(nm)[0:HD].rearrange("p (h t) -> p h t", h=2),
                                      gk[:, l, 3:4], None, ALU.mult).then_inc(banks.drain(nm), 1)
                n = NORM[f"cross{l}"]
                scaled(xn[:, 0], h[:, 0], n, lambda: banks.wait(dve, f"y_T3_{l}"))
                gained("cross_T", G_CROSS, l, (0, 2))
                dve.wait_ge(banks.drain(f"xq{l}"), banks.count(f"xq{l}", None, False) + 1)
                head_sums(sq[:], c_xq(l, 0), 8)
                dve.wait_ge(sem["xq_rs"], l + 1)
                dve.tensor_tensor(kn[:].rearrange("p i b (e d) -> p (i b e) d", e=2), ps(f"xq{l}")[:].rearrange("p (h d) -> p h d", h=8),
                                  spread(rs[:, c_xq(l, 0):c_xq(l, 0) + 8], [P, 8, HD]), ALU.mult).then_inc(banks.drain(f"xq{l}"), 1)
                for k in range(4):
                    u = 20 * l + 16 + k
                    banks.wait(dve, f"xs{k}_{l}")
                    dve.wait_ge(sem["probs_ready"], u - 1)
                    own(dve.tensor_reduce(nmx[:, u % 2], ps(f"xs{k}_{l}")[:].rearrange("p (b s) -> p b s", b=2), AX, ALU.max, negate=True))
                    dve.tensor_scalar(nmx[:, u % 2], nmx[:, u % 2], SCALE, None, ALU.mult).then_inc(sem["max_ready"], 1)
                for i in range(NT):
                    dve.wait_ge(sem["probs_ready"], 20 * l + 18 + 2 * i)
                    own(dve.reciprocal(sumc[:, i, 0, 0:4], sums[:, i, 0, 0:4]))
                    nm = f"xo{i}_{l}"
                    banks.wait(dve, nm)
                    dve.tensor_tensor(kn[:, i].rearrange("p b (e d) -> p (b e) d", e=2), ps(nm)[:, 0:256].rearrange("p (h d) -> p h d", h=4),
                                      spread(sumc[:, i, 0, 0:4], [P, 4, HD]), ALU.mult).then_inc(banks.drain(nm), 1)
                nm = f"xoT{l}"
                banks.wait(dve, nm)
                dve.tensor_copy(uT[:], ps(nm)[:].rearrange("p (a t) -> p a t", a=2)).then_inc(banks.drain(nm), 1)
                add_in("xout")
                n = NORM[f"ffn{l}"]
                scaled(xn[:, 0], h[:, 0], n, lambda: banks.wait(dve, f"cross_T3_{l}"))
                gained("ffn_T", G_FFN, l, (0, 2))
                if l == 0:
                    weights, turns = s5_weights(1), s5_turns(1)
                    banks.wait(dve, "xo1_0")
                    for t in range(HT):
                        if t in (3, 7, 15, 17):
                            next(weights, None)
                        if 9 <= t < 13:
                            next(turns, None)
                        up = ps(f"up{t}")
                        dve.wait_ge(sem["tanh_up"], t + 1)
                        if t >= 2:
                            dve.wait_ge(sem["gated"], t - 1)
                        own(dve.scalar_tensor_tensor(hT[:, 2 + t % 2], th[:, t % 2], 1.0, up[:, 0:256], ALU.add, ALU.mult))
                        dve.scalar_tensor_tensor(hT[:, t % 2], hT[:, 2 + t % 2], 0.5, up[:, 256:512], ALU.mult, ALU.mult).then_inc(sem["gated"], 1)
                    add_in("down")
            banks.wait(dve, "router")
            dve.wait_ge(sem["moe_consts_loaded"], 16)
            own(dve.tensor_copy(lg, ps("router")[:, 0:16].rearrange("p (i e) -> p i e", i=NT)))
            of_j = lg.unsqueeze(2).to_broadcast([P, NT, E, E])
            of_e = lg.unsqueeze(3).to_broadcast([P, NT, E, E])
            own(dve.tensor_tensor(cmpj, of_j, of_e, ALU.is_gt))
            own(dve.tensor_tensor(cmpe, of_j, of_e, ALU.is_equal))
            lower = cste[:, C_LT - C_MOE:C_LT - C_MOE + E * E].rearrange("p (e j) -> p e j", e=E).unsqueeze(1).to_broadcast([P, NT, E, E])
            own(dve.tensor_tensor(cmpe, cmpe, lower, ALU.mult))
            own(dve.tensor_tensor(cmpj, cmpj, cmpe, ALU.add))
            own(dve.tensor_reduce(rk, cmpj, AX, ALU.add))
            dve.tensor_scalar(sel, rk, TOPK - 0.5, None, ALU.is_lt).then_inc(sem["selected"], 1)
            own(dve.tensor_reduce(mx2[:, 0:2], lg, AX, ALU.max))
            dve.tensor_tensor(lg, lg, spread(mx2[:, 0:2], [P, NT, E]), ALU.subtract).then_inc(sem["r_centered"], 1)
            dve.wait_ge(sem["r_exp"], 1)
            dve.wait_ge(sem["selected"], 1)
            own(dve.tensor_tensor(ex, ex, sel, ALU.mult))
            own(dve.tensor_reduce(gsum[:, 0:2], ex, AX, ALU.add))
            own(dve.reciprocal(gsum[:, 0:2], gsum[:, 0:2]))
            own(dve.tensor_tensor(ex, ex, spread(gsum[:, 0:2], [P, NT, E]), ALU.mult))
            banks.wait(dve, "count")
            own(dve.tensor_scalar(pos, sel, -1e4, 1e4, ALU.mult, ALU.add))
            own(dve.tensor_tensor(pos, pos, ps("count")[:, 0:16].rearrange("p (i e) -> p i e", i=NT), ALU.add))
            own(dve.memset(table, 0.0))
            for i in range(NT):
                own(dve.tensor_tensor(table[:, 0:PASSES * E, i].rearrange("p (q e) -> p q e", e=E), pos[:, i].unsqueeze(1).to_broadcast([P, PASSES, E]),
                                      cste[:, C_PASS - C_MOE:C_PASS - C_MOE + PASSES * E].rearrange("p (q e) -> p q e", e=E), ALU.subtract))
                own(dve.tensor_copy(table[:, 0:PASSES * E, 2 + i].rearrange("p (q e) -> p q e", e=E), ex[:, i].unsqueeze(1).to_broadcast([P, PASSES, E])))
            own(dve.tensor_reduce(mx2[:, 2:3], ps("count")[:, 16:24], AX, ALU.max))
            own(dve.tensor_scalar(flag[:, 0:1], mx2[0:1, 2:3], CAP + 0.5, None, ALU.is_gt))
            signal(banks.drain("count"))
            signal(banks.drain("router"))
            signal(sem["flag_ready"])

            def pick(e, wait_to):
                dve.tensor_copy(cur, table[:, bass.ds(e, 1)].rearrange("p o k -> p (o k)")).then_inc(sem["e_step"], 1)
                wait_to(1)
                for i in range(NT):
                    dve.tensor_scalar(one[:, i], cste[:, C_IOTA - C_MOE:C_IOTA - C_MOE + CAP], cur[:, i:i + 1], None, ALU.is_equal)
                    k = dve.tensor_scalar(og[:, i], cste[:, C_IOTA - C_MOE:C_IOTA - C_MOE + CAP], cur[:, i:i + 1], cur[:, 2 + i:3 + i],
                                          ALU.is_equal, ALU.mult)
                k.then_inc(sem["picked"], 1)

            def gather_in(name, turn=None):
                for g in range(2):
                    nm = f"{name}gather{g}"
                    banks.wait(dve, nm, turn)
                    dve.tensor_tensor(xg[:, 4 * g:4 * g + 4], ps(nm)[:, 0:4 * CAP].rearrange("p (k c) -> p k c", k=4),
                                      spread(gain(G_FFN, 1, 4 * g, 4), [P, 4, CAP]), ALU.mult).then_inc(banks.drain(nm), 1)

            def gates_in(name, turn=None):
                nm = f"{name}gateT"
                banks.wait(dve, nm, turn)
                dve.tensor_copy(ogT, ps(nm)[0:CAP, 0:256]).then_inc(banks.drain(nm), 1)

            E_STEPS = 1 + HT

            pick(0, lambda k: dve.wait_ge(sem["e_step"], 1))
            gather_in("")
            gates_in("")

            def expert(turn):
                base = turn * E_STEPS + 1
                for t in range(HT):
                    up = ps(f"mup{t}")
                    dve.wait_ge(sem["e_tanh"], turn * HT + (t + 1))
                    if t >= 2:
                        dve.wait_ge(sem["e_gated"], turn * HT + (t - 1))
                    dve.scalar_tensor_tensor(hT[:, 2 + t % 2, 0:CAP], th[:, t % 2, 0:CAP], 1.0, up[:, 0:CAP], ALU.add, ALU.mult)\
                       .then_inc(sem["e_step"], 1)
                    dve.wait_ge(sem["e_step"], base + (t + 1))
                    dve.scalar_tensor_tensor(hT[:, t % 2, 0:CAP], hT[:, 2 + t % 2, 0:CAP], 0.5, up[:, CAP:2 * CAP], ALU.mult, ALU.mult)\
                       .then_inc(sem["e_gated"], 1)
                pick(turn + 1, lambda k: dve.wait_ge(sem["e_step"], base + E_STEPS))
                gather_in("n", turn)
                for g in range(4):
                    banks.wait(dve, f"sc{g}", turn)
                    dst = h[:, g // 2, 512 * (g % 2):512 * (g % 2) + 512]
                    dve.tensor_tensor(dst, dst, ps(f"sc{g}")[:], ALU.add).then_inc(banks.drain(f"sc{g}"), 1)
                gates_in("n", turn)

            with dve.Fori(0, E) as turn:
                expert(turn)
            over = dve.value_load(flag[0:1, 0:1], min_val=0, max_val=1)
            with dve.If(over > 0):
                with dve.Fori(E, PASSES * E) as turn:
                    expert(turn)
            dve.tensor_copy(flag[:, 1:2], flag[:, 0:1]).then_inc(sem["h_final"], 1)

        @block.tensor
        def _(pe):
            def done(name, i):
                i.then_inc(banks.fill(name), 1)

            def product(out_ap, pairs):
                n = len(pairs)
                for k, (a, b) in enumerate(pairs):
                    i = pe.matmul(out_ap, a, b, start=(k == 0), stop=(k == n - 1))
                return i

            def turn_tiles(name, l, src, wait):
                for g in range(4):
                    nm = f"{name}{g}_{l}"
                    banks.open(pe, nm)
                    for k in range(2):
                        for i in range(NT):
                            if g == 0 and k == 0:
                                wait(i)
                            e = pe.transpose(ps(nm)[:, 256 * k + P * i:256 * k + P * i + P],
                                             src[:, i, P * (2 * g + k):P * (2 * g + k) + P], ident)
                            if name == "mix_T" and l == 1 and g == k == i == 0:
                                e.then_inc(slot_free[FF_SLOTS[-1]], 1)
                    done(nm, e)

            def wait_norm(n):
                def w(i):
                    pe.wait_ge(sem[f"xn{i}_ready"], max(n, 1))
                return w

            def wait_xT(name, l):
                for g in (2, 3):
                    nm = f"{name}{g}_{l}"
                    pe.wait_ge(banks.drain(nm), banks.count(nm, None, False) + 1)

            def drained(nm, k=1):
                pe.wait_ge(banks.drain(nm), banks.count(nm, None, False) + k)

            pe.wait_ge(sem["par_loaded"], 16 * 4)
            banks.open(pe, "par")
            pe.transpose(pb[0][:, 0:P], raw, ident)
            pe.transpose(pb[0][:, P:P + 124], raw2[0:124], ident[0:124, 0:124])
            done("par", pe.transpose(pb[0][0:HD, 252:264], raw3, ident[0:12, 0:12]))
            pe.wait_ge(sem["t5_loaded"], 32)
            pe.wait_ge(sem["pads_ready"], 1)
            banks.open(pe, "t5")
            done("t5", pe.matmul(pb[1][0:NH, 0:512], tab[:], hot[:], start=True, stop=True))

            for l in range(L):
                win = [ring[:, c, 0:4096].rearrange("p (k n) -> p k n", k=KT) for c in range(4)]
                wgate = ring[:, 3, 4096:4288].rearrange("p (k n) -> p k n", k=KT)
                m = small(l)

                def feature_major(nm, w, cols):
                    banks.open(pe, nm)
                    for a, c in enumerate(cols):
                        e = product(ps(nm)[:, 256 * a:256 * a + 256], [(w[:, k, c:c + P], xT[:, k]) for k in range(KT)])
                    done(nm, e)

                def tokens(out_ap, i, w, c0, c1):
                    return product(out_ap, [(xT[:, k, P * i:P * i + P], w[:, k, c0:c1]) for k in range(KT)])

                def bu(j):
                    nm = f"bu{j}_{l}"
                    if j == 0:
                        drained(f"u{l}")
                        pe.wait_ge(sem["s5_weights"], l + 1)
                    banks.open(pe, nm)
                    r = slice(32 * (j % 4), 32 * (j % 4) + 32)
                    for c in range(2):
                        e = pe.matmul(ps(nm)[:, 256 * c:256 * c + 256], BL[r, c, j // 4].rearrange("p a s -> p (a s)"), uT[r, j // 4],
                                      start=True, stop=True)
                    done(nm, e)

                def ys(j):
                    nm = f"ys{l}"
                    if j == 0:
                        banks.open(pe, nm)
                    pe.wait_ge(sem["states_ready"], SJ * l + j + 1)
                    r = slice(32 * (j % 4), 32 * (j % 4) + 32)
                    o = ps(nm)[r, 256 * (j // 4):256 * (j // 4) + 256]
                    for c in range(2):
                        e = pe.matmul(o, CL[:, c, j], X[:, j % 2, c], start=(c == 0), stop=(c == 1),
                                      tile_position=(0, 32 * (j % 4)))
                    e.then_inc(sem["states_used"] if j < SJ - 1 else banks.fill(nm), 1)

                turn_tiles("mix_T", l, xn, wait_norm(NORM[f"mix{l}"]))
                if l == 0:
                    def wait_mem(i):
                        pe.wait_ge(sem["memx_ready"], i + 1)
                wait_xT("mix_T", l)
                weights_in(pe, f"in0_{l}")
                feature_major(f"u{l}", win[0], (0, 128))
                if l == 0:
                    turn_tiles("mem_T", 0, memx, wait_mem)

                def q_half(i, half):
                    nm = f"q{i}_{l}"
                    weights_in(pe, f"in{1 + half}_{l}")
                    if half == 0:
                        banks.open(pe, nm)
                        tokens(ps(nm)[:, 0:256], i, win[1], 256, 512)
                    else:
                        done(nm, tokens(ps(nm)[:, 256:512], i, win[2], 0, 256))

                def kvc_half(a):
                    nm = f"kvc{l}"
                    if a == 0:
                        banks.open(pe, nm)
                    e = product(ps(nm)[:, 256 * a:256 * a + 256], [(win[2][:, k, 256 + P * a:384 + P * a], xT[:, k]) for k in range(KT)])
                    if a:
                        done(nm, e)

                def kv_tile(i):
                    nm = f"kv{i}_{l}"
                    weights_in(pe, f"in3_{l}")
                    banks.open(pe, nm)
                    done(nm, tokens(ps(nm)[:], i, win[3], 0, 512))

                def gate_logits():
                    nm = f"gates{l}"
                    banks.open(pe, nm)
                    for i in range(NT):
                        e = tokens(ps(nm)[:, 24 * i:24 * i + 24], i, wgate, 0, 24)
                    done(nm, e)

                def conv_gate():
                    weights_in(pe, f"in1_{l}")
                    feature_major(f"cg{l}", win[1], (0, 128))

                projections = [lambda: feature_major(f"ca{l}", win[0], (256, 384)), conv_gate,
                               lambda: q_half(0, 0), lambda: q_half(1, 0), lambda: q_half(0, 1), lambda: q_half(1, 1),
                               lambda: kvc_half(0), lambda: kvc_half(1), lambda: kv_tile(0), lambda: kv_tile(1), gate_logits]
                first = S5_FIRST[l]
                for n in range(max(len(projections), first + SJ + 2)):
                    if n < len(projections):
                        projections[n]()
                    k = n - first
                    if k == 0:
                        bu(0)
                        bu(1)
                    if k >= 2 and k - 2 < SJ:
                        ys(k - 2)
                    if k >= 1 and k + 1 < SJ:
                        bu(k + 1)
                weights_in(pe, f"small_{l}")
                drained(f"kvc{l}")
                nm = f"cmp1_{l}"
                banks.open(pe, nm)
                for v in range(2):
                    product(ps(nm)[0:HD, 30 * v:30 * v + 30].rearrange("p (a n) -> p a n", a=2),
                            [(m["w1"][:, v, t], CX[:, v, :, t:t + 225:STRIDE]) for t in range(16)])
                for v in range(2):
                    e = product(ps(nm)[0:HD, 64 + v:65 + v], [(m["w1"][:, v, t], m["pe"][:, v, t:t + 1]) for t in range(16)])
                done(nm, e)
                for i in range(NT):
                    drained(f"q{i}_{l}", 2)
                    for g in range(2):
                        nm = f"qT{i}{g}_{l}"
                        banks.open(pe, nm)
                        for c in range(4):
                            e = pe.transpose(ps(nm)[0:HD, P * c:P * c + P], q_of[i][:, HD * (4 * g + c):HD * (4 * g + c) + HD], ident)
                        done(nm, e)
                for i in range(NT):
                    drained(f"kv{i}_{l}", 3)
                for k in range(KVH):
                    nm = f"kT{k}_{l}"
                    banks.open(pe, nm)
                    for b in range(2):
                        for i in range(NT):
                            e = pe.transpose(ps(nm)[0:HD, 256 * b + P * i:256 * b + P * i + P], kn[:, i, b, HD * k:HD * k + HD], ident)
                    done(nm, e)
                pe.wait_ge(sem["ys_g"], l + 1)
                g2 = scr[:, 0].rearrange("p (a t) -> p a t", a=2)
                for i in range(NT):
                    nm = f"glu{i}_{l}"
                    banks.open(pe, nm)
                    done(nm, product(ps(nm)[:], [(g2[:, a, P * i:P * i + P], m["glu"][:, a]) for a in range(2)]))
                nm = f"cmp2_{l}"
                banks.open(pe, nm)
                pe.wait_ge(sem["cmp_g"], l + 1)
                for v in range(2):
                    for a in range(KVH):
                        e = pe.matmul(ps(nm)[0:NCMP, P * v + HD * a:P * v + HD * a + HD], cmpx[:, 3, v, a], m["w2"][:, v], start=True, stop=True)
                done(nm, e)
                weights_in(pe, f"x_{l}")
                wkv = ring[:, 1, 0:4096].rearrange("p (k n) -> p k n", k=KT)
                wq = ring[:, 1, 4096:6144].rearrange("p (k n) -> p k n", k=KT)
                pe.wait_ge(sem["mem_gained"], l + 1)

                def mem_tile(i):
                    nm = f"mkv{i}_{l}"
                    banks.open(pe, nm)
                    done(nm, product(ps(nm)[:], [(memg[:, k, P * i:P * i + P], wkv[:, k]) for k in range(KT)]))

                mem_tile(0)
                nm = f"cmpT{l}"
                banks.open(pe, nm)
                drained(f"cmp2_{l}", 2)
                for a in range(KVH):
                    e = pe.transpose(ps(nm)[0:HD, NCMP * a:NCMP * a + NCMP], kcn[:, a], ident[0:NCMP, 0:NCMP])
                done(nm, e)
                nm = f"cvT{l}"
                banks.open(pe, nm)
                pe.wait_ge(sem["conv_done"], l + 1)
                for i in range(NT):
                    for a in range(2):
                        e = pe.transpose(ps(nm)[:, 256 * i + P * a:256 * i + P * a + P], ca[:, a, P * i:P * i + P], ident)
                done(nm, e)
                def conv_back():
                    nm = f"cvB{l}"
                    banks.open(pe, nm)
                    pe.wait_ge(sem["ln_scaled"], l + 1)
                    for a in range(2):
                        for i in range(NT):
                            e = pe.transpose(ps(nm)[:, 256 * a + P * i:256 * a + P * i + P], lnb[:, i, P * a:P * a + P], ident)
                    done(nm, e)

                def conv_out():
                    nm = f"cvW{l}"
                    banks.open(pe, nm)
                    pe.wait_ge(sem["silu_ready"], l + 1)
                    for i in range(NT):
                        e = product(ps(nm)[:, 256 * i:256 * i + 256], [(ca[:, a, P * i:P * i + P], m["pw"][:, a]) for a in range(2)])
                    done(nm, e)

                def scores(v):
                    i, hh = divmod(v, NH)
                    nk = P * (i + 1)
                    nm = f"sc{i}{hh}_{l}"
                    banks.open(pe, nm)
                    kv = hh // 4
                    done(nm, pe.matmul(ps(nm)[:, 0:2 * nk].rearrange("p (b s) -> p b s", b=2), qT[0:HD, i, hh],
                                       kT[0:HD, 2 * kv:2 * kv + 2, 0:nk], start=True, stop=True))

                def values(v):
                    i, hh = divmod(v, NH)
                    u = 20 * l + v
                    drained(f"pT{i}{hh}_{l}")
                    kv = hh // 4
                    pt = scr[:, 2 + u % 2, 0:2 * P * (i + 1)].rearrange("p (b s t) -> p b s t", b=2, s=i + 1)
                    for b, nm in enumerate((f"os{i}_{l}", f"ow{i}_{l}")):
                        if hh == 0:
                            banks.open(pe, nm)
                        e = product(ps(nm)[:, HD * hh:HD * hh + HD],
                                    [(pt[:, b, s], vv[:, s, b, HD * kv:HD * kv + HD]) for s in range(i + 1)])
                        if hh == NH - 1 and b == 0:
                            done(nm, e)
                    if hh < NH - 1:
                        e.then_inc(sem["pv_done"], 1)
                    else:
                        done(nm, e)
                        pe.transpose(ps(f"pT{i}{hh}_{l}")[0:1, 0:1], ident[0:1, 0:1], ident[0:1, 0:1]).then_inc(sem["pv_done"], 1)

                def c_scores(i):
                    nm = f"sc_c{i}_{l}"
                    banks.open(pe, nm)
                    drained(f"cmpT{l}")
                    for hh in range(NH):
                        e = pe.matmul(ps(nm)[:, NCMP * hh:NCMP * hh + NCMP], qT[0:HD, i, hh], kcT[:, hh // 4], start=True, stop=True)
                    done(nm, e)

                def c_turn(i):
                    pe.wait_ge(sem["c_exp"], 2 * l + i + 1)
                    for g in range(2):
                        nm = f"pcT{i}{g}_{l}"
                        banks.open(pe, nm)
                        for c in range(4):
                            e = pe.transpose(ps(nm)[0:NCMP, P * c:P * c + P], pc[:, 4 * g + c], ident)
                        done(nm, e)

                def c_values(i):
                    nm = f"oc{i}_{l}"
                    banks.open(pe, nm)
                    drained(f"pcT{i}0_{l}")
                    for hh in range(NH):
                        e = pe.matmul(ps(nm)[:, HD * hh:HD * hh + HD], pcT[:, hh], vc[:, hh // 4], start=True, stop=True)
                    done(nm, e)

                drained(f"qT11_{l}")
                drained(f"kT1_{l}")
                scores(0)
                scores(1)
                for v in range(2 * NH):
                    i, hh = divmod(v, NH)
                    u = 20 * l + v
                    nm = f"pT{i}{hh}_{l}"
                    pe.wait_ge(sem["probs_ready"], u + 1)
                    banks.open(pe, nm)
                    for c in range(2 * (i + 1)):
                        e = pe.transpose(ps(nm)[:, P * c:P * c + P], scr[:, u % 2, P * c:P * c + P], ident)
                    done(nm, e)
                    if v + 2 < 2 * NH:
                        scores(v + 2)
                    if v:
                        values(v - 1)
                    if v in C_SCORES:
                        c_scores(C_SCORES.index(v))
                    if v in C_TURN:
                        c_turn(C_TURN.index(v))
                    if v in C_VALUES:
                        c_values(C_VALUES.index(v))
                    if v == CONV_TURN:
                        conv_back()
                    if v == CONV_OUT:
                        conv_out()
                values(2 * NH - 1)
                mem_tile(1)
                def wait_y(i):
                    pe.wait_ge(sem["y_scaled"], 2 * l + i + 1)
                turn_tiles("y_T", l, xn, wait_y)
                wait_xT("y_T", l)
                for i in range(NT):
                    for n in range(2):
                        nm = f"out{2 * i + n}_{l}"
                        if i == 0:
                            weights_in(pe, f"out{n}_{l}")
                        banks.open(pe, nm)
                        done(nm, tokens(ps(nm)[:], i, ring[:, 2 + n, 0:4096].rearrange("p (k n) -> p k n", k=KT), 0, 512))
                for i in range(NT):
                    drained(f"mkv{i}_{l}", 3)
                for g in range(2):
                    nm = f"mkT{g}_{l}"
                    banks.open(pe, nm)
                    knx = kn[:].rearrange("p i b (e d) -> p i (b e) d", e=2)
                    for a in range(2):
                        for i in range(NT):
                            e = pe.transpose(ps(nm)[0:HD, 256 * a + P * i:256 * a + P * i + P], knx[:, i, 2 * g + a], ident)
                    done(nm, e)
                turn_tiles("cross_T", l, xn, wait_norm(NORM[f"cross{l}"]))
                wait_xT("cross_T", l)
                nm = f"xq{l}"
                banks.open(pe, nm)
                for i in range(NT):
                    e = tokens(ps(nm)[:, 256 * i:256 * i + 256], i, wq, 0, 256)
                done(nm, e)
                drained(nm, 2)
                for i in range(NT):
                    nm = f"xqT{i}_{l}"
                    banks.open(pe, nm)
                    for c in range(XH):
                        e = pe.transpose(ps(nm)[0:HD, P * c:P * c + P], kn[:, i].rearrange("p b t -> p (b t)")[:, HD * c:HD * c + HD], ident)
                    done(nm, e)

                def xscores(k):
                    i, hp = k // 2, k % 2
                    nm = f"xs{k}_{l}"
                    banks.open(pe, nm)
                    drained(f"xqT{i}_{l}")
                    for a in range(2):
                        e = pe.matmul(ps(nm)[:, 256 * a:256 * a + 256], qT[64:128, i, 2 * hp + a], kT[64:128, 2 * hp + a],
                                      start=True, stop=True)
                    done(nm, e)

                def xvalues(k):
                    i, hp = k // 2, k % 2
                    u = 20 * l + 16 + k
                    drained(f"xpT{k}_{l}")
                    nm = f"xo{i}_{l}"
                    if hp == 0:
                        banks.open(pe, nm)
                    pt = scr[:, 2 + u % 2].rearrange("p (a s t) -> p a s t", a=2, s=2)
                    for a in range(2):
                        c = 2 * hp + a
                        e = product(ps(nm)[:, HD * c:HD * c + HD], [(pt[:, a, s], vx[:, s, HD * c:HD * c + HD]) for s in range(NT)])
                    if hp:
                        done(nm, e)
                        pe.transpose(ps(f"xpT{k}_{l}")[0:1, 0:1], ident[0:1, 0:1], ident[0:1, 0:1]).then_inc(sem["pv_done"], 1)
                    else:
                        e.then_inc(sem["pv_done"], 1)

                drained(f"mkT1_{l}")
                xscores(0)
                xscores(1)
                for k in range(4):
                    u = 20 * l + 16 + k
                    nm = f"xpT{k}_{l}"
                    pe.wait_ge(sem["probs_ready"], u + 1)
                    banks.open(pe, nm)
                    for c in range(4):
                        e = pe.transpose(ps(nm)[:, P * c:P * c + P], scr[:, u % 2, P * c:P * c + P], ident)
                    done(nm, e)
                    if k + 2 < 4:
                        xscores(k + 2)
                    if k:
                        xvalues(k - 1)
                xvalues(3)
                nm = f"xoT{l}"
                banks.open(pe, nm)
                for i in range(NT):
                    drained(f"xo{i}_{l}")
                for a in range(2):
                    for i in range(NT):
                        e = pe.transpose(ps(nm)[:, 256 * a + P * i:256 * a + P * i + P],
                                         kn[:, i].rearrange("p b t -> p (b t)")[:, P * a:P * a + P], ident)
                done(nm, e)
                drained(nm)
                for i in range(NT):
                    for n in range(2):
                        nm = f"xout{2 * i + n}_{l}"
                        banks.open(pe, nm)
                        done(nm, product(ps(nm)[:], [(uT[:, a, P * i:P * i + P], m["xo"][:, a, 512 * n:512 * n + 512]) for a in range(2)]))
                turn_tiles("ffn_T", l, xn, wait_norm(NORM[f"ffn{l}"]))
                wait_xT("ffn_T", l)

                def up_products(name, c, mt, rhs, width, turn=None):
                    w = ring[:, FF_SLOTS[c], 0:UPW].rearrange("p (k g n) -> p k g n", k=KT, g=2)
                    t = 2 * c + mt
                    banks.open(pe, f"{name}{t}", turn)
                    for g in range(2):
                        e = product(ps(f"{name}{t}")[:, width * g:width * g + width],
                                    [(w[:, k, g, P * mt:P * mt + P], rhs[:, k]) for k in range(KT)])
                    done(f"{name}{t}", e)

                if l == 0:
                    def down_products(t):
                        c, mt = t // 2, t % 2
                        w = ring[:, FF_SLOTS[c], UPW:].rearrange("p (m n) -> p m n", m=2)
                        pe.wait_ge(sem["gated"], t + 1)
                        for g in range(4):
                            if t == 0:
                                banks.open(pe, f"down{g}")
                            e = pe.matmul(pb[4 + g][:], hT[:, t % 2, P * (g // 2):P * (g // 2) + P],
                                          w[:, mt, 512 * (g % 2):512 * (g % 2) + 512], start=(t == 0), stop=(t == HT - 1))
                            if t == HT - 1:
                                done(f"down{g}", e)
                        if mt and t < HT - 1:
                            e.then_inc(slot_free[FF_SLOTS[c]], 1)

                    for t in range(HT):
                        if t % 2 == 0:
                            weights_in(pe, f"ff{t // 2}")
                        up_products("up", t // 2, t % 2, xT, SEQ)
                        if t:
                            down_products(t - 1)
                    down_products(HT - 1)
            nm = "router"
            banks.open(pe, nm)
            pe.wait_ge(sem["router_loaded"], 16)
            for i in range(NT):
                e = tokens(ps(nm)[:, 8 * i:8 * i + 8], i, rt, 0, 8)
            done(nm, e)
            nm = "count"
            banks.open(pe, nm)
            pe.wait_ge(sem["selected"], 1)
            before, ones = cste[:, C_TRI - C_MOE:C_TRI - C_MOE + P], cste[:, C_ONE - C_MOE:C_ONE - C_MOE + P]
            product(ps(nm)[:, 0:8], [(before, sel[:, 0])])
            product(ps(nm)[:, 8:16], [(before, sel[:, 1]), (ones, sel[:, 0])])
            done(nm, product(ps(nm)[:, 16:24], [(ones, sel[:, 0]), (ones, sel[:, 1])]))

            def gather(name, turn=None):
                for g in range(2):
                    nm = f"{name}gather{g}"
                    banks.open(pe, nm, turn)
                    for k in range(4):
                        e = product(ps(nm)[:, CAP * k:CAP * k + CAP],
                                    [(xn[:, i, P * (4 * g + k):P * (4 * g + k) + P], one[:, i]) for i in range(NT)])
                    done(nm, e)

            def gate_tiles(name, turn=None, free=None):
                nm = f"{name}gateT"
                banks.open(pe, nm, turn)
                for i in range(NT):
                    e = pe.transpose(ps(nm)[0:CAP, P * i:P * i + P], og[:, i], ident)
                    if i == 0 and free is not None:
                        e.then_inc(free, 1)
                done(nm, e)

            pe.wait_ge(sem["picked"], 1)
            gather("")
            gate_tiles("")

            def expert(turn):
                def down(t):
                    c, mt = t // 2, t % 2
                    w = ring[:, FF_SLOTS[c], UPW:].rearrange("p (m n) -> p m n", m=2)
                    pe.wait_ge(sem["e_gated"], turn * HT + (t + 1))
                    for g in range(2):
                        if t == 0:
                            banks.open(pe, f"mdown{g}", turn)
                        e = pe.matmul(pb[4 + g][0:CAP], hT[:, t % 2, 0:CAP], w[:, mt, 512 * g:512 * g + 512],
                                      start=(t == 0), stop=(t == HT - 1))
                        if t == HT - 1:
                            done(f"mdown{g}", e)
                    if mt and t < HT - 1:
                        e.then_inc(slot_free[FF_SLOTS[c]], 1)

                pe.wait_ge(banks.drain("gather1"), turn * 3 + (gathered + 1))
                for t in range(HT):
                    if t % 2 == 0:
                        expert_in(pe, turn, t // 2)
                    up_products("mup", t // 2, t % 2, xg, CAP, turn)
                    if t:
                        down(t - 1)
                pe.wait_ge(sem["picked"], turn + 2)
                gather("n", turn)
                down(HT - 1)
                gate_tiles("n", turn, slot_free[FF_SLOTS[-1]])
                for g in range(4):
                    nm = f"sc{g}"
                    banks.open(pe, nm, turn)
                    if g < 2:
                        pe.wait_ge(banks.drain(f"mdown{g}"), banks.count(f"mdown{g}", turn, False) + 1)
                    done(nm, pe.matmul(ps(nm)[:], ogT[:, P * (g // 2):P * (g // 2) + P], ye[:, 512 * (g % 2):512 * (g % 2) + 512],
                                       start=True, stop=True))

            gathered = banks.count("gather1", None, False)
            with pe.Fori(0, E) as turn:
                expert(turn)
            pe.wait_ge(sem["flag_ready"], 1)
            over = pe.value_load(flag[0:1, 0:1], min_val=0, max_val=1)
            with pe.If(over > 0):
                with pe.Fori(E, PASSES * E) as turn:
                    expert(turn)


def kernel(x, mem, norm_mix, w_in, ssm_lambda_re, ssm_lambda_im, ssm_log_dt, ssm_b_re, ssm_b_im, ssm_c_re, ssm_c_im,
           ssm_d, ssm_w_glu, conv_w_dw, conv_b_dw, conv_ln_g, conv_ln_b, conv_w_pw, nsa_q_norm, nsa_k_norm,
           nsa_cmp_pe, nsa_cmp_w1, nsa_cmp_w2, mix_out_norm, w_out, t5_table, norm_cross, norm_mem, x_w_q, x_w_kv,
           x_q_norm, x_k_norm, x_w_o, norm_ffn, ffn_w_up, ffn_w_down, moe_router, moe_w_up, moe_w_down):
    import concourse.bacc as bacc
    from concourse.bass_utils import run_bass_kernel_spmd

    consts, hot = shape_constants()
    rows = (L, G * GH, GP)
    arrays = dict(
        x=x[0], mem=mem[0], w_in=w_in, w_glu=ssm_w_glu, w_pw=conv_w_pw, cmp_w1=nsa_cmp_w1, cmp_w2=nsa_cmp_w2,
        w_out=w_out, t5_table=t5_table, x_w_q=x_w_q, x_w_kv=x_w_kv, x_w_o=x_w_o, ffn_up=ffn_w_up, ffn_down=ffn_w_down,
        router=moe_router[0], moe_up=moe_w_up[0], moe_down=moe_w_down[0],
        rows128=np.concatenate([a.reshape(-1, P) for a in (
            norm_mix, norm_cross, norm_ffn, norm_mem, mix_out_norm, conv_b_dw, conv_ln_g, conv_ln_b, ssm_d,
            ssm_lambda_re, ssm_lambda_im)]),
        rows64=np.concatenate([a.reshape(-1, HD) for a in (nsa_q_norm, nsa_k_norm, x_q_norm, x_k_norm)]),
        lam_re=ssm_lambda_re.reshape(L, G * GP), lam_im=ssm_lambda_im.reshape(L, G * GP), log_dt=ssm_log_dt, conv_w=conv_w_dw,
        b_re=ssm_b_re.transpose(0, 1, 3, 2).reshape(rows), b_im=ssm_b_im.transpose(0, 1, 3, 2).reshape(rows),
        c_re=ssm_c_re.transpose(0, 1, 3, 2).reshape(L, G * GP, GH), c_im=ssm_c_im.transpose(0, 1, 3, 2).reshape(L, G * GP, GH),
        cmp_pe=nsa_cmp_pe.reshape(L, 2, 2, 16, HD).transpose(0, 1, 2, 4, 3).reshape(L, 2, P, 16),
        consts=consts, t5_hot=hot)
    arrays = {k: np.ascontiguousarray(v) for k, v in arrays.items()}
    nc = bacc.Bacc("TRN2", target_bir_lowering=False, num_devices=1)
    args = {k: nc.dram_tensor(f"{k}_dram", list(v.shape), F32, kind="ExternalInput").ap() for k, v in arrays.items()}
    bias_rows = nc.dram_tensor("bias_rows_dram", [NH, 512], F32, kind="Internal").ap()
    out = nc.dram_tensor("out_dram", [SEQ, D], F32, kind="ExternalOutput").ap()
    trunk(nc, **args, bias_rows=bias_rows, out=out)
    r = run_bass_kernel_spmd(nc, [{f"{k}_dram": v for k, v in arrays.items()}], core_ids=[0])
    return np.asarray(r.results[0]["out_dram"]).reshape(1, SEQ, D)
```
